# Optimizing a Trainium2 kernel written in Bass

```python
import jax, jax.numpy as jnp
from jax import lax
import numpy as np

D_MODEL = 1024
BATCH = 1
SEQ = 512
DEPTH = 1
DEC_BATCH = 1
DEC_SEQ = 32
PAST_LEN = 128

CHUNK = 64
CONV_WIDTH = 31
D_CONV = D_MODEL
D_GMLP = D_MODEL
GMLP_CHUNK = 128
GMLP_GROUPS = 8
GMLP_GROUP_DIM = D_GMLP // GMLP_GROUPS
N_GROUPS = 4
EXPERTS_PER_GROUP = 8
N_EXPERTS = N_GROUPS * EXPERTS_PER_GROUP
TOP_K = 2
D_EXPERT = D_MODEL // 4
D_IN = 2 * D_CONV + 2 * D_GMLP + 2 * D_MODEL
EPS = 1e-6

kernel_name = "hybrid_conv_gmlp_hmoe_stream_step"

def rms_norm(x, g):
    xf = x.astype(jnp.float32)
    y = xf * lax.rsqrt(jnp.mean(xf * xf, axis=-1, keepdims=True) + EPS)
    return (y * g.astype(jnp.float32)).astype(x.dtype)

def layer_norm(x, g, b):
    xf = x.astype(jnp.float32)
    mu = jnp.mean(xf, axis=-1, keepdims=True)
    var = jnp.mean(jnp.square(xf - mu), axis=-1, keepdims=True)
    y = (xf - mu) * lax.rsqrt(var + EPS) * g.astype(jnp.float32) + b.astype(jnp.float32)
    return y.astype(x.dtype)

def modulate(h, shift, scale):
    return h * (1 + scale) + shift

def depthwise_causal_conv(x_full, w, b):
    y = lax.conv_general_dilated(
        x_full, w[:, None, :], window_strides=(1,), padding='VALID',
        dimension_numbers=('NWC', 'WIO', 'NWC'), feature_group_count=x_full.shape[-1])
    return y + b

def spatial_gate(u, v, w_s, b_s):
    B, T, _ = v.shape
    L = min(T, GMLP_CHUNK)
    n = T // L
    mask = jnp.tril(jnp.ones((L, L), dtype=bool))
    w = jnp.where(mask, w_s[:, :L, :L], 0).astype(v.dtype)
    vc = v.reshape(B, n, L, GMLP_GROUPS, GMLP_GROUP_DIM)
    mixed = jnp.einsum('hts,bnshc->bnthc', w, vc) + b_s[:, :L].T[None, None, :, :, None]
    return u * mixed.reshape(B, T, D_GMLP)

def mixer_branch(h, conv_hist, w_in, b_in, conv_w, conv_b, ln_g, ln_b, w_a,
                 v_ln_g, v_ln_b, w_s, b_s, w_b, w_o):
    z = h @ w_in + b_in
    a = z[..., :2 * D_CONV]
    uv = z[..., 2 * D_CONV:2 * D_CONV + 2 * D_GMLP]
    gates = jax.nn.sigmoid(z[..., 2 * D_CONV + 2 * D_GMLP:])
    a = jax.nn.glu(a, axis=-1)
    a_full = jnp.concatenate([conv_hist.astype(a.dtype), a], axis=1)
    new_hist = a_full[:, -(CONV_WIDTH - 1):]
    a = jax.nn.silu(layer_norm(depthwise_causal_conv(a_full, conv_w, conv_b), ln_g, ln_b))
    y_a = a @ w_a
    uv = jax.nn.gelu(uv)
    u, v = uv[..., :D_GMLP], uv[..., D_GMLP:]
    v = layer_norm(v, v_ln_g, v_ln_b)
    y_b = spatial_gate(u, v, w_s, b_s) @ w_b
    merged = gates[..., :D_MODEL] * y_a + gates[..., D_MODEL:] * y_b
    return merged @ w_o, new_hist, v

def hier_moe(h, w_rg, b_rg, w_re, b_re, w_gate, w_up, w_down):
    B, T, D = h.shape
    hf = h.reshape(-1, D)
    lg = (hf @ w_rg + b_rg).astype(jnp.float32)
    pg = jax.nn.softmax(lg, axis=-1)
    gsel = jnp.argmax(lg, axis=-1)
    pgsel = jnp.take_along_axis(pg, gsel[:, None], axis=-1)
    le = (hf @ w_re + b_re).astype(jnp.float32).reshape(-1, N_GROUPS, EXPERTS_PER_GROUP)
    le_sel = jnp.take_along_axis(le, gsel[:, None, None], axis=1)[:, 0]
    pe = jax.nn.softmax(le_sel, axis=-1)
    top_p, top_i = lax.top_k(pe, TOP_K)
    top_w = pgsel * top_p / jnp.sum(top_p, axis=-1, keepdims=True)
    eidx = gsel[:, None] * EXPERTS_PER_GROUP + top_i
    combine = jnp.einsum('nk,nke->ne', top_w,
                         jax.nn.one_hot(eidx, N_EXPERTS, dtype=jnp.float32)).astype(h.dtype)
    out = jnp.zeros_like(hf)
    for e in range(N_EXPERTS):
        he = jax.nn.silu(hf @ w_gate[e]) * (hf @ w_up[e])
        out = out + combine[:, e:e + 1] * (he @ w_down[e])
    return out.reshape(B, T, D)

def block(x, c, conv_hist, w_ada, b_ada, g_norm1, g_norm2, w_in, b_in, conv_w, conv_b,
          ln_g, ln_b, w_a, v_ln_g, v_ln_b, w_s, b_s, w_b, w_o,
          w_rg, b_rg, w_re, b_re, w_gate, w_up, w_down):
    mod = (jax.nn.silu(c) @ w_ada + b_ada)[:, None, :]
    sh1, sc1, g1, sh2, sc2, g2 = jnp.split(mod, 6, axis=-1)
    h = modulate(rms_norm(x, g_norm1), sh1, sc1)
    m, new_hist, v = mixer_branch(h, conv_hist, w_in, b_in, conv_w, conv_b, ln_g, ln_b, w_a,
                                  v_ln_g, v_ln_b, w_s, b_s, w_b, w_o)
    x = x + g1 * m
    h = modulate(rms_norm(x, g_norm2), sh2, sc2)
    x = x + g2 * hier_moe(h, w_rg, b_rg, w_re, b_re, w_gate, w_up, w_down)
    return x, new_hist, v

def setup_inputs(seed: int = 0) -> dict:
    key = jax.random.key(seed)
    ks = jax.random.split(key, 40)
    f32 = jnp.float32
    nrm = lambda k, shape, s: jax.random.normal(k, shape, f32) * s
    L = DEPTH
    return {
        "x_prompt": nrm(ks[0], (BATCH, SEQ, D_MODEL), 1.0),
        "x_sample": nrm(ks[1], (DEC_BATCH, DEC_SEQ, D_MODEL), 1.0),
        "cache_conv": nrm(ks[2], (L, DEC_BATCH, CONV_WIDTH - 1, D_CONV), 1.0),
        "c_prompt": nrm(ks[3], (BATCH, D_MODEL), 1.0),
        "c_sample": nrm(ks[4], (DEC_BATCH, D_MODEL), 1.0),
        "w_ada": nrm(ks[5], (L, D_MODEL, 6 * D_MODEL), 0.5 * D_MODEL ** -0.5),
        "b_ada": nrm(ks[6], (L, 6 * D_MODEL), 0.02),
        "g_norm1": 1.0 + nrm(ks[7], (L, D_MODEL), 0.02),
        "g_norm2": 1.0 + nrm(ks[8], (L, D_MODEL), 0.02),
        "w_in": nrm(ks[9], (L, D_MODEL, D_IN), D_MODEL ** -0.5),
        "b_in": nrm(ks[10], (L, D_IN), 0.02),
        "conv_w": nrm(ks[11], (L, CONV_WIDTH, D_CONV), CONV_WIDTH ** -0.5),
        "conv_b": nrm(ks[12], (L, D_CONV), 0.02),
        "ln_g": 1.0 + nrm(ks[13], (L, D_CONV), 0.02),
        "ln_b": nrm(ks[14], (L, D_CONV), 0.02),
        "w_a": nrm(ks[15], (L, D_CONV, D_MODEL), D_CONV ** -0.5),
        "v_ln_g": 1.0 + nrm(ks[16], (L, D_GMLP), 0.02),
        "v_ln_b": nrm(ks[17], (L, D_GMLP), 0.02),
        "w_s": nrm(ks[18], (L, GMLP_GROUPS, GMLP_CHUNK, GMLP_CHUNK), GMLP_CHUNK ** -0.5),
        "b_s": 1.0 + nrm(ks[19], (L, GMLP_GROUPS, GMLP_CHUNK), 0.1),
        "w_b": nrm(ks[20], (L, D_GMLP, D_MODEL), D_GMLP ** -0.5),
        "w_o": nrm(ks[21], (L, D_MODEL, D_MODEL), D_MODEL ** -0.5),
        "w_rg": nrm(ks[22], (L, D_MODEL, N_GROUPS), D_MODEL ** -0.5),
        "b_rg": nrm(ks[23], (L, N_GROUPS), 0.01),
        "w_re": nrm(ks[24], (L, D_MODEL, N_EXPERTS), D_MODEL ** -0.5),
        "b_re": nrm(ks[25], (L, N_EXPERTS), 0.01),
        "w_gate": nrm(ks[26], (L, N_EXPERTS, D_MODEL, D_EXPERT), D_MODEL ** -0.5),
        "w_up": nrm(ks[27], (L, N_EXPERTS, D_MODEL, D_EXPERT), D_MODEL ** -0.5),
        "w_down": nrm(ks[28], (L, N_EXPERTS, D_EXPERT, D_MODEL), D_EXPERT ** -0.5),
        "g_final": 1.0 + nrm(ks[29], (D_MODEL,), 0.02),
        "w_ada_f": nrm(ks[30], (D_MODEL, 2 * D_MODEL), 0.5 * D_MODEL ** -0.5),
        "b_ada_f": nrm(ks[31], (2 * D_MODEL,), 0.02),
    }

def reference(x_prompt, x_sample, cache_conv, c_prompt, c_sample, w_ada, b_ada, g_norm1, g_norm2,
              w_in, b_in, conv_w, conv_b, ln_g, ln_b, w_a, v_ln_g, v_ln_b, w_s, b_s, w_b, w_o,
              w_rg, b_rg, w_re, b_re, w_gate, w_up, w_down, g_final, w_ada_f, b_ada_f):
    xp, xs = x_prompt, x_sample
    conv_p, conv_s, v_s = [], [], []
    for l in range(DEPTH):
        lp = (w_ada[l], b_ada[l], g_norm1[l], g_norm2[l], w_in[l], b_in[l], conv_w[l], conv_b[l],
              ln_g[l], ln_b[l], w_a[l], v_ln_g[l], v_ln_b[l], w_s[l], b_s[l], w_b[l], w_o[l],
              w_rg[l], b_rg[l], w_re[l], b_re[l], w_gate[l], w_up[l], w_down[l])
        zero_hist = jnp.zeros((xp.shape[0], CONV_WIDTH - 1, D_CONV), xp.dtype)
        xp, hist_p, _ = block(xp, c_prompt, zero_hist, *lp)
        xs, hist_s, vs = block(xs, c_sample, cache_conv[l], *lp)
        conv_p.append(hist_p)
        conv_s.append(hist_s)
        v_s.append(vs)

    def final(x, c):
        shf, scf = jnp.split((jax.nn.silu(c) @ w_ada_f + b_ada_f)[:, None, :], 2, axis=-1)
        return modulate(rms_norm(x, g_final), shf, scf)

    y_prompt = final(xp, c_prompt)
    y_sample = final(xs, c_sample)
    state_conv_prompt = jnp.stack(conv_p, axis=0)
    state_conv_sample = jnp.stack(conv_s, axis=0)
    state_gmlp_v_sample = jnp.stack(v_s, axis=0)
    return (y_prompt, y_sample, state_conv_prompt, state_conv_sample, state_gmlp_v_sample)


_drawn_inputs = setup_inputs


def setup_inputs(seed=0):
    import zlib

    import numpy as np

    out = dict(_drawn_inputs(seed))
    spreads = {}
    factors = {'g_norm2': 5.136,
     'b_in': 2.748,
     'conv_b': 8.0,
     'ln_g': 8.0,
     'ln_b': 8.0,
     'v_ln_g': 2.842,
     'v_ln_b': 2.873,
     'b_s': 4.05,
     'b_rg': 8.0,
     'b_re': 8.0,
     'g_final': 8.306,
     'b_ada_f': 2.812}
    for name, (base, spread) in spreads.items():
        noise = np.random.default_rng([zlib.crc32(name.encode()), seed]).standard_normal(out[name].shape)
        drawn = base * np.exp(spread * noise) if base else spread * noise
        out[name] = __import__('jax').numpy.asarray(drawn.astype(out[name].dtype))
    for name, factor in factors.items():
        out[name] = (out[name] * factor).astype(out[name].dtype)
    return out
```

```python
from contextlib import ExitStack

import numpy as np

import concourse.bass as bass
from concourse import mybir

F32 = mybir.dt.float32
I32 = mybir.dt.int32
U32 = mybir.dt.uint32
ALU = mybir.AluOpType
ACT = mybir.ActivationFunctionType
AX = mybir.AxisListType.X
ds = bass.ds

P = 128
D = 1024
KT = D // P
NPROMPT, NSAMPLE = 512, 32
T = NPROMPT + NSAMPLE
TT = 5
WIDTH = [P, P, P, P, NSAMPLE]
H = T // 2
TAPS = 31
HIST = TAPS - 1
FULL = T + 2 * HIST
CONV = FULL - HIST
CH = CONV // 2
SAMPLE0 = NPROMPT + HIST
EPS = 1e-6
NG, EPG, NE = 4, 8, 32
DE = 256
SLOTS = 64
OVER = 16
TILES = NE + OVER
STEPS = T // SLOTS
NLOG = NG + NE
BLK = 512
NMOD = 8 * D

O_X, O_H, O_A, O_C, O_S, O_U, O_V, O_W = 0, 5120, 9472, 14304, 18896, 23248, 27600, 32720
ARENA = 40912
H2_BANK = [6, 2, 4, 6, 2]


def build(nc, a, y_out, hist_p_out, hist_s_out, v_out):
    with ExitStack() as ctx:
        def sb(name, shape, dt=F32):
            return ctx.enter_context(nc.sbuf_tensor(name, shape, dt))

        def sem(name):
            return ctx.enter_context(nc.semaphore(name))

        PS = ctx.enter_context(nc.psum_tensor("PS", [P, 8, 512], F32))
        arena = sb("arena", [P, ARENA])

        def view(at, *dims):
            n = 1
            for d in dims:
                n *= d
            v = arena[:, at:at + n]
            if len(dims) == 2:
                v = v.rearrange("p (a b) -> p a b", b=dims[1])
            if len(dims) == 3:
                v = v.rearrange("p (a b c) -> p a b c", b=dims[1], c=dims[2])
            return v

        x = view(O_X, TT, D)
        hT = view(O_H, KT, T)
        aF = view(O_A, KT, FULL)
        cv = view(O_C, KT, CONV)
        aT = view(O_S, KT, T)
        uT = view(O_U, KT, T)
        v = view(O_V, TT, D)
        mT = view(O_V, KT, T)
        sq = view(O_V, KT, CONV)
        W = [view(O_W + 4096 * s, KT, BLK) for s in range(2)]
        WP = [view(O_W + 4096 * s, 4, KT, P) for s in range(2)]
        xn = view(O_U, 2, D)
        cacheR = view(O_S, 3, D)[:, 2, :]
        histR = view(O_S, 2, D)
        wsR = view(O_S + 3072, KT, P)
        VR = view(O_U + 2048, 4, P)
        WG = [view(O_A + 6144 * s, KT, DE) for s in range(2)]
        WU = [view(O_A + 6144 * s + 2048, KT, DE) for s in range(2)]
        WD = [view(O_A + 6144 * s + 4096, 2, D) for s in range(2)]
        g1b = [view(O_U, D), view(O_U + 1024, D)]
        a2b = [view(O_U + 2048, D), view(O_U + 3072, D)]
        sh2b = [view(O_H + 2048, D), view(O_H + 3072, D)]
        gn2b = view(O_A + 12288, D)
        h2 = view(O_H, 2, D)
        G = view(O_V, 2, D)
        hG = view(O_V + 2048, 2, KT * SLOTS)
        Y = view(O_V + 3072, 2, D)
        sil = view(O_U, 2, 2 * SLOTS)
        heT = view(O_U + 256, 4, SLOTS).rearrange("p (b k) s -> p b k s", b=2)
        pair_rows = [view(O_A + 5120 * k, TT, D) for k in range(2)]
        g2b = [view(O_W, D), view(O_W + 1024, D)]
        afb = [view(O_W + 2048, D), view(O_W + 3072, D)]
        shfb = [view(O_W + 4096, D), view(O_W + 5120, D)]
        gfb = view(O_W + 6144, D)
        at_w = [O_W]

        def table(*dims):
            n = 1
            for d in dims:
                n *= d
            r = view(at_w[0], *dims)
            at_w[0] += n
            return r

        ident = sb("ident", [P, P])
        meanm = sb("meanm", [P, P])
        before = sb("before", [P, P])
        ones = sb("ones", [P, P])
        eps = sb("eps", [P, 1])
        vecs = sb("vecs", [P, KT * T])
        bsb = vecs[:, 0:1024].rearrange("p (h t) -> p h t", t=P)
        bvb, vgb, vbb = (vecs[:, 1024 * n:1024 * (n + 1)] for n in (1, 2, 3))
        h2T = vecs[:, :].rearrange("p (k t) -> p k t", t=T)
        wsT = sb("wsT", [P, KT, P])
        tmp = sb("tmp", [P, 4, CONV])
        tmp2 = tmp[:, :, :].rearrange("p (a b) t -> p a (b t)", b=2)
        mg, sqj = tmp2[:, 0, 0:D], tmp2[:, 1, 0:D]
        rstdc = sb("rstdc", [P, CONV])
        VT = sb("VT", [P, 360])
        S1 = sb("S1", [P, 2, KT])
        c16 = sb("c16", [16, P])
        cT = sb("cT", [P, 2, KT])
        brow = sb("brow", [2, 2, BLK])
        mrow = sb("mrow", [2, 2, BLK])
        ss = sb("ss", [P, 8])
        sd = sb("sd", [P, 8])
        rs = sb("rs", [P, 8])
        vsd = sb("vsd", [P, 8])
        bn = sb("bn", [P, 2, 6])
        mv = sb("mv", [P, 2])
        wr = sb("wr", [P, KT, NLOG])
        brb = sb("brb", [P, NLOG])
        tokI = sb("tokI", [SLOTS, TILES], U32)
        pairI = sb("pairI", [SLOTS, TILES], U32)
        wslot = sb("wslot", [SLOTS, TILES])
        over_expert = sb("over_expert", [1, OVER], I32)
        gidx = [sb(f"gidx{b}", [SLOTS, 1], U32) for b in range(2)]
        sidx = [sb(f"sidx{b}", [SLOTS, 1], U32) for b in range(2)]
        COL_CB, COL_BIN, COL_LG, COL_LB, COL_G1, COL_MOD = 248, 256, 304, 312, 320, 328

        mod = nc.dram_tensor("mod", (2, NMOD), F32, kind="Internal").ap()
        h2d = nc.dram_tensor("h2d", (T, D), F32, kind="Internal").ap()
        pairs = nc.dram_tensor("pairs", (2 * T, D), F32, kind="Internal").ap()

        consts = sem("consts")
        c_in, x_in, vec_in, bc_in, rt_in = (sem(n) for n in ("c_in", "x_in", "vec_in", "bc_in", "rt_in"))
        ws_in, cache_in, ws_masked = sem("ws_in"), sem("cache_in"), sem("ws_masked")
        c_silu, x_sq, x_sd = sem("c_silu"), sem("x_sq"), sem("x_sd")
        start_ps, start_dr, xn_ready = sem("start_ps"), sem("start_dr"), sem("xn_ready")
        w_full = [sem("w_full0"), sem("w_full1")]
        w_used = sem("w_used")
        act_drained = sem("act_drained")
        mod_added = sem("mod_added")
        mod_stored = [sem("mod_stored0"), sem("mod_stored1")]
        loads_begun, turns_begun, gathers_begun, scatters_begun = (sem(n) for n in ("loads_begun", "turns_begun", "gathers_begun", "scatters_begun"))
        modr_in, h_ready = sem("modr_in"), sem("h_ready")
        dve_step = sem("dve_step")
        act_step = sem("act_step")
        aF_written, conv_step = sem("aF_written"), sem("conv_step")
        hist_ps, hist_copied, hist_stored = sem("hist_ps"), sem("hist_copied"), sem("hist_stored")
        v_ps, v_biased, v_gelu, v_norm, v_stored = (sem(n) for n in ("v_ps", "v_biased", "v_gelu", "v_norm", "v_stored"))
        mix_ps, dve_drained, stat_ps = sem("mix_ps"), sem("dve_drained"), sem("stat_ps")
        centred, squared, c_std, c_normed, a_ready = (sem(n) for n in ("centred", "squared", "c_std", "c_normed", "a_ready"))
        merged, mix_added, gated, v_var, v_sd = (sem(n) for n in ("merged", "mix_added", "gated", "v_var", "v_sd"))
        o_ps, o_drained = sem("o_ps"), sem("o_drained")
        mb_in, mb2_in = sem("mb_in"), sem("mb2_in")
        x1_ready, x1_sd, h2_ready, h2_ps, h2_copied = (sem(n) for n in ("x1_ready", "x1_sd", "h2_ready", "h2_ps", "h2_copied"))
        h2_stored = [sem("h2_stored0"), sem("h2_stored1")]
        log_ps, log_ready, e_ready, oh_ready, rank_ps, tab_ready, tab_ps = (sem(n) for n in ("log_ps", "log_ready", "e_ready", "oh_ready", "rank_ps", "tab_ready", "tab_ps"))
        routed = sem("routed")
        gu_full = [sem("gu_full0"), sem("gu_full1")]
        wd_full = [sem("wd_full0"), sem("wd_full1")]
        g_idx, s_idx = sem("g_idx"), sem("s_idx")
        gathered = [sem("gathered0"), sem("gathered1")]
        scattered = [sem("scattered0"), sem("scattered1")]
        t_ps, hg_ready, gu_done, sil_ready, he_ready, down_done = (sem(n) for n in ("t_ps", "hg_ready", "gu_done", "sil_ready", "he_ready", "down_done"))
        y_act, y_dve = sem("y_act"), sem("y_dve")
        fin_in, pair_in = sem("fin_in"), [sem(f"pair_in{t}") for t in range(TT)]
        f_sum, f_sd, f_out, f_stored = (sem(n) for n in ("f_sum", "f_sd", "f_out", "f_stored"))

        iotaI = sb("iotaI", [P, SLOTS], I32)
        iota = sb("iota", [P, SLOTS])
        tokidI = sb("tokidI", [P, TT], I32)
        tokid = sb("tokid", [P, TT])
        valid = sb("valid", [P, TT])
        steps = sb("steps", [P, STEPS])
        lg = table(TT, NLOG)
        one_g = table(TT, NG)
        one_e = table(2, TT, EPG)
        lsel = table(2, TT, EPG)
        prod = table(TT, NE)
        scr = table(TT, EPG)
        mx = table(4, TT)
        diffs = table(TT, NG + 1)
        exps = table(TT, NG + 1)
        wk = table(2, TT)
        OH = table(2, TT, NE)
        OHs = table(TT, NE)
        rank = table(2, TT)
        cmp = table(NE, STEPS)
        nov = table(NE)
        cum = table(2, NE)
        exc = table(NE)
        ovs = table(2, TT)
        eid = table(2, TT)
        q8 = table(2 * TT, STEPS)
        pid = table(2, TT)
        rev = table(1, EPG)
        q = table(2, TT)
        tile = table(2, TT)
        off = table(2, TT)
        TOH = table(2 * TT, TILES)
        FOH = table(2 * TT, SLOTS)
        R = table(2 * TT, 3 * TILES)
        un = table(TILES)
        ocmp = table(OVER, NE)
        oex = table(OVER)
        assert at_w[0] <= ARENA

        NCONST = 12 + STEPS
        block = ctx.enter_context(nc.Block())

        def full(eng, n):
            eng.wait_ge(w_full[n % 2], 32 * (n // 2 + 1))

        U_ADA1, U_A, U_U, U_V, U_ADA2, U_YB, U_YA, U_O = 0, 4, 12, 16, 18, 30, 38, 46
        Q_A, Q_U, Q_ADA2, Q_YB, Q_YA = 4, 12, 16, 28, 36

        w_ada = a["w_ada"][0].rearrange("(k p) n -> p k n", p=P)
        w_adaf = a["w_ada_f"].rearrange("(k p) n -> p k n", p=P)
        w_in = a["w_in"][0].rearrange("(k p) n -> p k n", p=P)
        w_a = a["w_a"][0].rearrange("(k p) n -> p k n", p=P)
        w_b = a["w_b"][0].rearrange("(k p) n -> p k n", p=P)
        w_o = a["w_o"][0].rearrange("(k p) n -> p k n", p=P)
        w_gate = a["w_gate"][0].rearrange("e (p k) n -> e p (k n)", p=P)
        w_up = a["w_up"][0].rearrange("e (p k) n -> e p (k n)", p=P)
        w_down = a["w_down"][0].rearrange("e (k p) n -> e p k n", p=P)

        @block.sync
        def _(sp):
            def load_block(s, src, bias, wait):
                for sm, val in wait:
                    sp.wait_ge(sm, val)
                sp.dma_start(W[s], src).then_inc(w_full[s], 16)
                sp.dma_start(brow[:, s, :], bias.to_broadcast([2, BLK])).then_inc(w_full[s], 16)

            for n in range(4):
                load_block(n % 2, w_ada[:, :, n * BLK:(n + 1) * BLK], a["b_ada"][:, n * BLK:(n + 1) * BLK],
                           [(w_used, n - 1), (mod_added, n - 1)] if n >= 2 else [])

            def pair_loads(base, left, left0, right, right0):
                with sp.Fori(0, 8 // 2) as half:
                    i = half * 2
                    for b in range(2):
                        c_left, c_right = sp.snap(i * P + (left0 + b * P)), sp.snap(i * P + (right0 + b * P))
                        sp.wait_ge(w_used, i + (base + b - 1))
                        sp.sem_inc(loads_begun)
                        sp.dma_start(WP[b][:, 0], left[:, :, ds(c_left, P)]).then_inc(w_full[b], 16)
                        sp.dma_start(WP[b][:, 1], right[:, :, ds(c_right, P)]).then_inc(w_full[b], 16)

            pair_loads(U_A, w_in, 0, w_in, D)
            with sp.Fori(0, 4 // 2) as half:
                i = half * 2
                for b in range(2):
                    sp.wait_ge(w_used, i + (U_U + b - 1))
                    sp.sem_inc(loads_begun)
                    for m in range(2):
                        sp.dma_start(WP[b][:, m], w_in[:, :, ds(i * (2 * P) + (2 * D + (2 * b + m) * P), P)]).then_inc(w_full[b], 16)

            def halves(base, src, col0):
                for b in range(2):
                    sp.wait_ge(w_used, base + b - 1)
                    for m in range(2):
                        sp.dma_start(W[b][:, 4 * m:4 * m + 4, :], src[:, 4 * m:4 * m + 4, col0 + b * BLK:col0 + (b + 1) * BLK]).then_inc(w_full[b], 16)

            halves(U_V, w_in, 3 * D)

            def ada_loop(first, count, src, bias, col0):
                with sp.Fori(0, count // 2) as half:
                    i = half * 2
                    for b in range(2):
                        sp.wait_ge(w_used, i + (U_ADA2 + first + b - 1))
                        sp.sem_inc(loads_begun)
                        sp.wait_ge(mod_added, i + (4 + first + b - 1))
                        sp.sem_inc(loads_begun)
                        sp.dma_start(W[b], src[:, :, ds(i * BLK + (col0 + b * BLK), BLK)]).then_inc(w_full[b], 16)
                        sp.dma_start(brow[:, b, :], bias[:, ds(i * BLK + (col0 + b * BLK), BLK)].to_broadcast([2, BLK])).then_inc(w_full[b], 16)

            ada_loop(0, 8, w_ada, a["b_ada"], 4 * BLK)
            ada_loop(8, 4, w_adaf, a["b_ada_f"].rearrange("(o n) -> o n", o=1), 0)
            pair_loads(U_YB, w_in, 5 * D, w_b, 0)
            pair_loads(U_YA, w_in, 4 * D, w_a, 0)
            halves(U_O, w_o, 0)

            def mod_vec(n, rows, s):
                return mod[s:s + 1, n * D:(n + 1) * D].to_broadcast([rows, D])

            for p in range(2):
                sp.wait_ge(mod_stored[p], 16 * 8)
            sp.wait_ge(w_used, U_YB + 8)
            for s, rows in ((0, P), (1, NSAMPLE)):
                sp.dma_start(g1b[s][0:rows, :], mod_vec(2, rows, s)).then_inc(mb_in, 16)
                sp.dma_start(a2b[s][0:rows, :], mod_vec(4, rows, s)).then_inc(mb_in, 16)
            sp.wait_ge(w_used, U_YA + 8)
            sp.dma_start(gn2b, a["g_norm2"].to_broadcast([P, D])).then_inc(mb2_in, 16)
            for s, rows in ((0, P), (1, NSAMPLE)):
                sp.dma_start(sh2b[s][0:rows, :], mod_vec(3, rows, s)).then_inc(mb2_in, 16)
            sp.wait_ge(a_ready, 2 * KT)
            sp.wait_ge(hist_ps, 2)

            def load_gu(b, e):
                sp.dma_start(WG[b].rearrange("p k n -> p (k n)"), w_gate[e].rearrange("o p n -> (o p) n")).then_inc(gu_full[b], 16)
                sp.dma_start(WU[b].rearrange("p k n -> p (k n)"), w_up[e].rearrange("o p n -> (o p) n")).then_inc(gu_full[b], 16)

            def load_d(b, e):
                sp.dma_start(WD[b], w_down[e].rearrange("o p k n -> (o p) k n")).then_inc(wd_full[b], 16)

            for b in range(2):
                load_gu(b, ds(b, 1))
                load_d(b, ds(b, 1))
            with sp.Fori(0, (NE - 2) // 2) as half:
                t = half * 2 + 2
                for b in range(2):
                    sp.wait_ge(gu_done, t + (b - 1))
                    sp.sem_inc(loads_begun)
                    load_gu(b, ds(t + b, 1))
                    sp.wait_ge(down_done, t + (b - 1))
                    sp.sem_inc(loads_begun)
                    load_d(b, ds(t + b, 1))
            sp.wait_ge(routed, 1)
            with sp.Fori(0, OVER // 2) as half:
                t = half * 2
                for b in range(2):
                    e = sp.value_load(over_expert[0:1, ds(t + b, 1)], min_val=0, max_val=NE - 1)
                    sp.wait_ge(gu_done, t + (NE + b - 1))
                    sp.sem_inc(loads_begun)
                    load_gu(b, ds(e, 1))
                    sp.wait_ge(down_done, t + (NE + b - 1))
                    sp.sem_inc(loads_begun)
                    load_d(b, ds(e, 1))
            sp.dma_start(gfb, a["g_final"].rearrange("(o n) -> o n", o=1).to_broadcast([P, D])).then_inc(fin_in, 16)
            for s, rows in ((0, P), (1, NSAMPLE)):
                for n, dst in ((5, g2b), (6, shfb), (7, afb)):
                    sp.dma_start(dst[s][0:rows, :], mod_vec(n, rows, s)).then_inc(fin_in, 16)
            sp.wait_ge(down_done, TILES)
            for b in range(2):
                sp.wait_ge(scattered[b], 8 * TILES)
            for t in range(TT):
                for k in range(2):
                    sp.dma_start(pair_rows[k][0:WIDTH[t], t, :], pairs[k * T + t * P:k * T + t * P + WIDTH[t], :]).then_inc(pair_in[t], 16)
            for t in range(TT):
                sp.wait_ge(f_out, t + 1)
                sp.dma_start(y_out[t * P:t * P + WIDTH[t], :], pair_rows[0][0:WIDTH[t], t, :]).then_inc(f_stored, 16)
            sp.wait_ge(f_stored, 16 * TT)
            sp.wait_ge(hist_stored, 32)
            sp.wait_ge(v_stored, 16)

        @block.tensor
        def _(pe):
            def product(bank, tile_w, act):
                for k in range(KT):
                    for h in range(2):
                        last = pe.matmul(PS[:, bank + h, 0:H], tile_w[:, k, :], act[:, k, h * H:(h + 1) * H],
                                         start=(k == 0), stop=(k == KT - 1))
                return last

            def ada(b):
                for k in range(KT):
                    last = pe.matmul(PS[0:2, 4 * b, :], cT[:, :, k], W[b][:, k, :], start=(k == 0), stop=(k == KT - 1))
                return last

            pe.wait_ge(consts, NCONST)
            pe.wait_ge(c_silu, 1)
            pe.transpose(PS[:, 0, 0:16], c16[:, :], ident[0:16, 0:16]).then_inc(start_ps, 1)
            pe.wait_ge(vec_in, 16 * 7)
            pe.transpose(PS[:, 1, 0:128], VR[:, 0, :], ident[:, :])
            pe.transpose(PS[:, 1, 128:256], VR[:, 1, :], ident[:, :])
            pe.transpose(PS[:, 1, 256:328], VR[0:72, 2, :], ident[0:72, 0:72]).then_inc(start_ps, 1)
            pe.wait_ge(cache_in, 16)
            for j in range(KT):
                last = pe.transpose(PS[:, 2, j * HIST:(j + 1) * HIST], cacheR[0:HIST, j * P:(j + 1) * P], ident[0:HIST, 0:HIST])
            last.then_inc(start_ps, 1)
            pe.wait_ge(ws_masked, KT)
            for h in range(KT):
                last = pe.transpose(PS[:, 4 + h // 4, (h % 4) * P:(h % 4 + 1) * P], wsR[:, h, :], ident[:, :])
            last.then_inc(start_ps, 1)
            for t in range(TT):
                w = WIDTH[t]
                bank = 6 if t % 2 == 0 else 2
                if t >= 1:
                    pe.wait_ge(start_dr, t + 3)
                pe.wait_ge(xn_ready, t + 1)
                for j in range(KT):
                    last = pe.transpose(PS[:, bank + j // 4, (j % 4) * P:(j % 4) * P + w],
                                        xn[0:w, t % 2, j * P:(j + 1) * P], ident[0:w, 0:w])
                last.then_inc(start_ps, 1)
            pe.wait_ge(start_dr, 4)
            for n in range(4):
                full(pe, n)
                if n >= 2:
                    pe.wait_ge(act_drained, n - 1)
                ada(n % 2).then_inc(w_used, 1)
            pe.wait_ge(modr_in, 32)
            pe.transpose(PS[:, 1, 0:32], VR[0:32, 3, :], ident[0:32, 0:32]).then_inc(start_ps, 1)
            pe.wait_ge(h_ready, 2 * KT)

            def pair_products(base, q0, left_act, right_act):
                with pe.Fori(0, 8 // 2) as half:
                    i = half * 2
                    for b in range(2):
                        pe.wait_ge(w_full[b], i * 16 + 32 * (base // 2 + 1))
                        pe.wait_ge(act_drained, i + (q0 + b - 1))
                        if base >= U_YB:
                            pe.wait_ge(dve_drained, i + (base - U_YB + 9 + b))
                        product(4 * b, WP[b][:, 0], left_act)
                        product(4 * b + 2, WP[b][:, 1], right_act).then_inc(w_used, 1)

            pair_products(U_A, Q_A, hT, hT)
            with pe.Fori(0, 4 // 2) as half:
                i = half * 2
                for b in range(2):
                    pe.wait_ge(w_full[b], i * 16 + 32 * (U_U // 2 + 1))
                    pe.wait_ge(act_drained, i + (Q_U + b - 1))
                    for m in range(2):
                        last = product(4 * b + 2 * m, WP[b][:, m], hT)
                    last.then_inc(w_used, 1)

            def histories(first):
                for j in range(KT):
                    last = pe.transpose(PS[0:HIST, 6 + j // 4, (j % 4) * P:(j % 4 + 1) * P], aF[:, j, first:first + HIST], ident[:, :])
                last.then_inc(hist_ps, 1)

            pe.wait_ge(act_drained, Q_U + 4)
            pe.wait_ge(aF_written, 4 + 2 * KT)
            pe.wait_ge(start_dr, 3)
            histories(NPROMPT)
            full(pe, U_V)
            full(pe, U_V + 1)
            for t in range(TT):
                for hf in range(2):
                    g = 2 * t + hf
                    if g >= 6:
                        pe.wait_ge(v_biased, g - 5)
                    for k in range(KT):
                        last = pe.matmul(PS[0:WIDTH[t], g % 6, :], hT[:, k, t * P:t * P + WIDTH[t]], W[hf][:, k, :],
                                         start=(k == 0), stop=(k == KT - 1))
                    if g < 2 * TT - 1:
                        last.then_inc(v_ps, 1)
            last.then_inc(w_used, 2)
            pe.wait_ge(hist_copied, 1)
            histories(FULL - HIST)
            pe.wait_ge(v_norm, TT)
            for h in range(KT):
                b = h % 2
                if h >= 2:
                    pe.wait_ge(dve_drained, h - 1)
                for t in range(4):
                    pe.matmul(PS[:, 2 * b, t * P:(t + 1) * P], v[:, t, h * P:(h + 1) * P], wsT[:, h, :], start=True, stop=True)
                pe.matmul(PS[:, 2 * b + 1, 0:NSAMPLE], v[0:NSAMPLE, 4, h * P:(h + 1) * P],
                          wsT[0:NSAMPLE, h, 0:NSAMPLE], start=True, stop=True).then_inc(mix_ps, 1)

            def over_features(bank, src):
                for j in range(KT):
                    for h in range(2):
                        last = pe.matmul(PS[:, bank + h, 0:CH], meanm[:, :], src[:, j, h * CH:(h + 1) * CH],
                                         start=(j == 0), stop=(j == KT - 1))
                last.then_inc(stat_ps, 1)

            pe.wait_ge(conv_step, TAPS * KT)
            pe.wait_ge(hist_copied, 2)
            over_features(6, cv)
            pe.wait_ge(dve_drained, KT)
            with pe.Fori(0, 12 // 2) as half:
                i = half * 2
                for b in range(2):
                    pe.wait_ge(w_full[b], i * 16 + 32 * (U_ADA2 // 2 + 1))
                    pe.wait_ge(act_drained, i + (Q_ADA2 + b - 1))
                    ada(b).then_inc(w_used, 1)
            pe.wait_ge(squared, KT)
            pe.wait_ge(act_drained, Q_YB)
            over_features(4, sq)
            pair_products(U_YB, Q_YB, hT, uT)
            pe.wait_ge(a_ready, 2 * KT)
            pair_products(U_YA, Q_YA, hT, aT)
            full(pe, U_O)
            full(pe, U_O + 1)
            pe.wait_ge(merged, 2 * KT)
            pe.wait_ge(act_drained, Q_YA + 8)

            def project(t):
                if t == 3:
                    pe.wait_ge(h2_copied, 1)
                if t == 4:
                    pe.wait_ge(o_drained, 2)
                for hf in range(2):
                    for k in range(KT):
                        last = pe.matmul(PS[0:WIDTH[t], (2 * t + hf) % 8, :], mT[:, k, t * P:t * P + WIDTH[t]], W[hf][:, k, :],
                                         start=(k == 0), stop=(k == KT - 1))
                    if t < 4 or hf == 0:
                        last.then_inc(o_ps, 1)
                    else:
                        last.then_inc(w_used, 2)

            def turn_h2(t):
                bank = H2_BANK[t]
                pe.wait_ge(h2_ready, t + 1)
                if t == 4:
                    pe.wait_ge(h2_copied, 2)
                for j in range(KT):
                    last = pe.transpose(PS[:, bank + j // 4, (j % 4) * P:(j % 4) * P + WIDTH[t]],
                                        h2[0:WIDTH[t], t % 2, j * P:(j + 1) * P], ident[0:WIDTH[t], 0:WIDTH[t]])
                last.then_inc(h2_ps, 1)

            project(0)
            for t in range(1, TT):
                project(t)
                turn_h2(t - 1)
            turn_h2(TT - 1)
            pe.wait_ge(rt_in, 64)
            pe.wait_ge(h2_copied, TT)
            for t in range(TT):
                for k in range(KT):
                    last = pe.matmul(PS[0:WIDTH[t], 0, t * NLOG:(t + 1) * NLOG], h2T[:, k, t * P:t * P + WIDTH[t]], wr[:, k, :],
                                     start=(k == 0), stop=(k == KT - 1))
            last.then_inc(log_ps, 1)
            pe.wait_ge(oh_ready, 1)
            for t in range(TT):
                for s in range(t + 1):
                    pe.matmul(PS[:, 1, t * NE:(t + 1) * NE], before[:, :] if s == t else ones[:, :], OHs[:, s, :],
                              start=(s == 0), stop=(s == t))
            for s in range(TT):
                last = pe.matmul(PS[:, 1, TT * NE:(TT + 1) * NE], ones[:, :], OHs[:, s, :], start=(s == 0), stop=(s == TT - 1))
            last.then_inc(rank_ps, 1)
            pe.wait_ge(tab_ready, 1)
            for n in range(2 * TT):
                last = pe.matmul(PS[0:SLOTS, 2, 0:3 * TILES], FOH[:, n, :], R[:, n, :], start=(n == 0), stop=(n == 2 * TT - 1))
            last.then_inc(tab_ps, 1)

            def turn_rows(t, b, landed):
                pe.wait_ge(gathered[b], landed)
                pe.sem_inc(turns_begun)
                for k in range(KT):
                    last = pe.transpose(PS[:, b, k * SLOTS:(k + 1) * SLOTS], G[0:SLOTS, b, k::KT], ident[0:SLOTS, 0:SLOTS])
                last.then_inc(t_ps, 1)

            def gate_up(t, b, landed):
                pe.wait_ge(gu_full[b], landed)
                pe.wait_ge(hg_ready, t)
                for n in range(4):
                    w = (WG, WU)[n // 2][b]
                    for k in range(KT):
                        last = pe.matmul(PS[:, 2 + b, n * SLOTS:(n + 1) * SLOTS], w[:, k, (n % 2) * P:(n % 2 + 1) * P],
                                         hG[:, b, k * SLOTS:(k + 1) * SLOTS], start=(k == 0), stop=(k == KT - 1))
                last.then_inc(gu_done, 1)

            def down(t, b, landed):
                pe.wait_ge(wd_full[b], landed)
                pe.wait_ge(he_ready, t)
                for hf in range(2):
                    for k in range(2):
                        last = pe.matmul(PS[0:SLOTS, 4 + 2 * b + hf, :], heT[:, b, k, :], WD[b][:, k, hf * 512:(hf + 1) * 512],
                                         start=(k == 0), stop=(k == 1))
                last.then_inc(down_done, 1)

            pe.wait_ge(routed, 1)
            turn_rows(1, 0, 16)
            with pe.Fori(0, (TILES - 2) // 2) as half:
                i = half * 2
                gate_up(i + 1, 0, i * 16 + 32)
                turn_rows(i + 2, 1, i * 8 + 16)
                down(i + 1, 0, i * 8 + 16)
                gate_up(i + 2, 1, i * 16 + 32)
                turn_rows(i + 3, 0, i * 8 + 32)
                down(i + 2, 1, i * 8 + 16)
            gate_up(TILES - 1, 0, 16 * TILES)
            turn_rows(TILES, 1, 8 * TILES)
            down(TILES - 1, 0, 8 * TILES)
            gate_up(TILES, 1, 16 * TILES)
            down(TILES, 1, 8 * TILES)

        @block.scalar
        def _(act):
            act.dma_start(c16[0:8, :], a["c_prompt"].rearrange("o (k p) -> (o k) p", p=P)).then_inc(c_in, 16)
            act.dma_start(c16[8:16, :], a["c_sample"].rearrange("o (k p) -> (o k) p", p=P)).then_inc(c_in, 16)
            for t in range(4):
                act.dma_start(x[:, t, :], a["x_prompt"][0, t * P:(t + 1) * P, :]).then_inc(x_in, 16)
            act.dma_start(x[0:NSAMPLE, 4, :], a["x_sample"][0]).then_inc(x_in, 16)
            taps = a["conv_w"][0].rearrange("t (j p) -> (t j) p", p=P)
            act.dma_start(VR[:, 0, :], taps[0:P, :]).then_inc(vec_in, 16)
            act.dma_start(VR[0:TAPS * KT - P, 1, :], taps[P:TAPS * KT, :]).then_inc(vec_in, 16)

            def rows(name):
                return a[name].rearrange("o (j p) -> (o j) p", p=P)

            act.dma_start(VR[TAPS * KT - P:P, 1, :], rows("conv_b")).then_inc(vec_in, 16)
            act.dma_start(VR[0:48, 2, :], rows("b_in")).then_inc(vec_in, 16)
            act.dma_start(VR[48:56, 2, :], rows("ln_g")).then_inc(vec_in, 16)
            act.dma_start(VR[56:64, 2, :], rows("ln_b")).then_inc(vec_in, 16)
            act.dma_start(VR[64:72, 2, :], rows("g_norm1")).then_inc(vec_in, 16)
            act.dma_start(cacheR[0:HIST, :], a["cache_conv"][0, 0]).then_inc(cache_in, 16)
            act.dma_start(wsR, a["w_s"][0].rearrange("h t s -> t h s")).then_inc(ws_in, 16)
            act.dma_start(vecs[:, 0:D], a["b_s"].rearrange("o h t -> o (h t)").to_broadcast([P, D])).then_inc(bc_in, 16)
            act.dma_start(bvb, a["b_in"][:, 3 * D:4 * D].to_broadcast([P, D])).then_inc(bc_in, 16)
            act.dma_start(vgb, a["v_ln_g"].to_broadcast([P, D])).then_inc(bc_in, 16)
            act.dma_start(vbb, a["v_ln_b"].to_broadcast([P, D])).then_inc(bc_in, 16)
            act.dma_start(wr[:, :, 0:NG], a["w_rg"][0].rearrange("(k p) n -> p k n", p=P)).then_inc(rt_in, 16)
            act.dma_start(wr[:, :, NG:NLOG], a["w_re"][0].rearrange("(k p) n -> p k n", p=P)).then_inc(rt_in, 16)
            act.dma_start(brb[:, 0:NG], a["b_rg"].to_broadcast([P, NG])).then_inc(rt_in, 16)
            act.dma_start(brb[:, NG:NLOG], a["b_re"].to_broadcast([P, NE])).then_inc(rt_in, 16)

            act.wait_ge(c_in, 32)
            act.activation(c16[:, :], c16[:, :], ACT.Silu).then_inc(c_silu, 1)
            act.wait_ge(x_in, 16 * TT)
            act.wait_ge(consts, NCONST)
            for t in range(TT):
                if t:
                    act.wait_ge(x_sq, t)
                act.activation(mg[0:WIDTH[t], :], x[0:WIDTH[t], t, :], ACT.Square, accum_out=ss[0:WIDTH[t], t:t + 1]).then_inc(x_sq, 1)
            act.wait_ge(x_sq, TT)
            act.activation(sd[:, 0:TT], ss[:, 0:TT], ACT.Sqrt, bias=eps[:, :], scale=1.0 / D).then_inc(x_sd, 1)
            for n in range(4):
                act.wait_ge(w_used, n + 1)
                if n >= 2:
                    act.wait_ge(mod_stored[n % 2], 16)
                act.activation(mrow[:, n % 2, :], PS[0:2, 4 * (n % 2), :], ACT.Copy).then_inc(act_drained, 1)
            for b in range(2):
                act.wait_ge(mod_stored[b], 32)
            for s in range(2):
                act.dma_start(VR[16 * s:16 * s + 16, 3, :], mod[s:s + 1, 0:2 * D].rearrange("o (j p) -> (o j) p", p=P)).then_inc(modr_in, 16)

            def two(ap):
                return ap.rearrange("p (h t) -> p h t", h=2)

            def tile_of(buf, j, c0, n):
                return buf[:, ds(j, 1), c0:c0 + n].rearrange("p o t -> p (o t)")

            with act.Fori(0, KT // 2) as half:
                i = half * 2
                for b in range(2):
                    act.wait_ge(w_used, i + (U_A + b + 1))
                    act.wait_ge(aF_written, i * 2 + (2 + 2 * b))
                    act.activation(two(tmp[:, b, 0:T]), PS[:, 4 * b:4 * b + 2, 0:H], ACT.Identity, bias=VT[:, ds(i + (COL_BIN + b), 1)])
                    act.activation(two(tmp[:, 2 + b, 0:T]), PS[:, 4 * b + 2:4 * b + 4, 0:H], ACT.Sigmoid,
                                   bias=VT[:, ds(i + (COL_BIN + KT + b), 1)]).then_inc(act_drained, 1)
            for n in range(4):
                b = n % 2
                act.wait_ge(w_used, U_U + n + 1)
                for m in range(2):
                    j = 2 * n + m
                    last = act.activation(two(uT[:, j, :]), PS[:, 4 * b + 2 * m:4 * b + 2 * m + 2, 0:H], ACT.Gelu_apprx_tanh,
                                          bias=VT[:, COL_BIN + 2 * KT + j:COL_BIN + 2 * KT + j + 1])
                last.then_inc(act_drained, 1)

            def store_history(n, dst):
                act.wait_ge(hist_ps, n + 1)
                act.activation(histR[0:HIST, n, :], PS[0:HIST, 6:8, :].rearrange("p b c -> p (b c)"), ACT.Copy).then_inc(hist_copied, 1)
                act.wait_ge(hist_copied, n + 1)
                act.dma_start(dst, histR[0:HIST, n, :]).then_inc(hist_stored, 16)

            def v_deviation(t):
                act.wait_ge(v_var, t + 1)
                col = vsd[0:WIDTH[t], t:t + 1]
                act.activation(col, col, ACT.Sqrt, bias=eps[0:WIDTH[t], :]).then_inc(v_sd, 1)

            store_history(0, hist_p_out)
            for t in range(TT):
                for hf in range(2):
                    act.wait_ge(v_biased, 2 * t + hf + 1)
                    vh = v[0:WIDTH[t], t, hf * 512:(hf + 1) * 512]
                    act.activation(vh, vh, ACT.Gelu_apprx_tanh).then_inc(v_gelu, 1)
                if t:
                    v_deviation(t - 1)
            v_deviation(TT - 1)
            store_history(1, hist_s_out)
            with act.Fori(0, 12 // 2) as half:
                i = half * 2
                for b in range(2):
                    act.wait_ge(w_used, i + (U_ADA2 + b + 1))
                    act.wait_ge(mod_stored[b], i * 8 + 32)
                    act.activation(mrow[:, b, :], PS[0:2, 4 * b, :], ACT.Copy).then_inc(act_drained, 1)
            act.wait_ge(stat_ps, 2)
            act.activation(two(rstdc[:, :]), PS[:, 4:6, 0:CH], ACT.Sqrt, bias=eps[:, :]).then_inc(c_std, 1)
            act.wait_ge(hist_stored, 32)
            with act.Fori(0, KT) as j:
                act.wait_ge(c_normed, j + 1)
                for at, n, first in ((0, NPROMPT, 0), (NPROMPT, NSAMPLE, SAMPLE0)):
                    act.activation(tile_of(aT, j, at, n), tile_of(cv, j, first, n), ACT.Silu,
                                   bias=VT[:, ds(j + COL_LB, 1)], scale=VT[:, ds(j + COL_LG, 1)]).then_inc(a_ready, 1)
            for base, q0, col in ((U_YB, Q_YB, 5 * KT), (U_YA, Q_YA, 4 * KT)):
                with act.Fori(0, KT // 2) as half:
                    i = half * 2
                    for b in range(2):
                        act.wait_ge(w_used, i + (base + b + 1))
                        act.wait_ge(dve_drained, i + (base - U_YB + 9 + b))
                        act.activation(two(tmp[:, b, 0:T]), PS[:, 4 * b:4 * b + 2, 0:H], ACT.Sigmoid,
                                       bias=VT[:, ds(i + (COL_BIN + col + b), 1)]).then_inc(act_drained, 1)

            def copy_h2(t):
                w = WIDTH[t]
                act.wait_ge(h2_ps, t + 1)
                act.activation(h2T[:, :, t * P:t * P + w],
                               PS[:, H2_BANK[t]:H2_BANK[t] + 2, :].rearrange("p b (j c) -> p (b j) c", c=P)[:, :, 0:w],
                               ACT.Copy).then_inc(h2_copied, 1)

            def deviation(t, done, summed, signal, scratch):
                w = WIDTH[t]
                act.wait_ge(summed, t + 1)
                act.activation(scratch[0:w, :], x[0:w, t, :], ACT.Square, accum_out=ss[0:w, t:t + 1]).then_inc(act_step, 1)
                act.wait_ge(act_step, done + t + 1)
                act.activation(sd[0:w, t:t + 1], ss[0:w, t:t + 1], ACT.Sqrt, bias=eps[0:w, :], scale=1.0 / D).then_inc(signal, 1)

            for t in range(TT):
                deviation(t, 0, x1_ready, x1_sd, sqj)
                if t:
                    copy_h2(t - 1)
                act.wait_ge(h2_ready, t + 1)
                act.dma_start(h2d[t * P:t * P + WIDTH[t], :], h2[0:WIDTH[t], t % 2, :]).then_inc(h2_stored[t % 2], 16)
            copy_h2(TT - 1)
            act.wait_ge(log_ready, 1)
            act.activation(exps, diffs, ACT.Exp).then_inc(e_ready, 1)
            def expert_tile(t, b, col, scattered_before):
                act.wait_ge(gu_done, t)
                act.activation(sil[:, b, :], PS[:, 2 + b, 0:2 * SLOTS], ACT.Silu).then_inc(sil_ready, 1)
                act.wait_ge(down_done, t)
                if scattered_before is not None:
                    act.wait_ge(scattered[b], scattered_before)
                act.activation(Y[0:SLOTS, b, 0:512], PS[0:SLOTS, 4 + 2 * b, :], ACT.Copy, scale=col).then_inc(y_act, 1)

            for b in range(2):
                expert_tile(b + 1, b, wslot[:, b:b + 1], None)
            with act.Fori(0, (TILES - 2) // 2) as half:
                i = half * 2
                for b in range(2):
                    expert_tile(i + (b + 3), b, wslot[:, ds(i + (2 + b), 1)], i * 8 + 16)
            for t in range(TT):
                deviation(t, TT, f_sum, f_sd, sqj)

        @block.vector
        def _(dve):
            steps_done = [0]

            def then(ins):
                steps_done[0] += 1
                ins.then_inc(dve_step, 1)
                dve.wait_ge(dve_step, steps_done[0])

            def rows_of(banks, w):
                return banks.rearrange("p b (j c) -> p (b j) c", c=P)[:, :, 0:w]

            def two(ap):
                return ap.rearrange("p (h t) -> p h t", h=2)

            dve.wait_ge(consts, NCONST)
            then(dve.tensor_copy(iota[:, :], iotaI[:, :]))
            then(dve.tensor_copy(tokid[:, :], tokidI[:, :]))
            dve.wait_ge(start_ps, 1)
            dve.tensor_copy(cT.rearrange("p s k -> p (s k)"), PS[:, 0, 0:16]).then_inc(start_dr, 1)
            dve.wait_ge(start_ps, 2)
            dve.tensor_copy(VT[:, 0:328], PS[:, 1, 0:328]).then_inc(start_dr, 1)
            dve.wait_ge(start_ps, 3)
            dve.tensor_copy(aF[:, :, HIST + NPROMPT:2 * HIST + NPROMPT],
                            PS[:, 2, 0:KT * HIST].rearrange("p (j c) -> p j c", c=HIST)).then_inc(start_dr, 1)
            dve.wait_ge(start_ps, 4)
            dve.tensor_copy(wsT[:, :, :].rearrange("p h t -> p (h t)"), PS[:, 4:6, :].rearrange("p b c -> p (b c)")).then_inc(start_dr, 1)
            dve.wait_ge(x_sd, 1)
            then(dve.reciprocal(rs[:, 0:TT], sd[:, 0:TT]))
            for t in range(TT):
                w = WIDTH[t]
                bank = 6 if t % 2 == 0 else 2
                dve.tensor_scalar(xn[0:w, t % 2, :], x[0:w, t, :], rs[0:w, t:t + 1], None, ALU.mult).then_inc(xn_ready, 1)
                dve.wait_ge(start_ps, 5 + t)
                dve.tensor_copy(hT[:, :, t * P:t * P + w], rows_of(PS[:, bank:bank + 2, :], w)).then_inc(start_dr, 1)
            dve.wait_ge(start_ps, 5 + TT)
            then(dve.tensor_copy(VT[:, COL_MOD:COL_MOD + 32], PS[:, 1, 0:32]))
            for s in range(2):
                c0 = COL_MOD + 16 * s
                then(dve.scalar_tensor_tensor(out=S1[:, s, :], in0=VT[:, c0 + KT:c0 + 2 * KT], scalar=1.0,
                                              in1=VT[:, COL_G1:COL_G1 + KT], op0=ALU.add, op1=ALU.mult))
            dve.wait_ge(start_dr, 4 + TT)
            for j in range(KT):
                for s, (c0, c1) in enumerate(((0, NPROMPT), (NPROMPT, T))):
                    dve.tensor_scalar(hT[:, j, c0:c1], hT[:, j, c0:c1], S1[:, s, j:j + 1],
                                      VT[:, COL_MOD + 16 * s + j:COL_MOD + 16 * s + j + 1], ALU.mult, ALU.add).then_inc(h_ready, 1)

            def tile_of(buf, j, c0, n):
                return buf[:, ds(j, 1), c0:c0 + n].rearrange("p o t -> p (o t)")

            with dve.Fori(0, KT // 2) as half:
                i = half * 2
                dve.wait_ge(aF_written, i * 2 + 8)
                for k in range(TAPS):
                    for b in range(2):
                        acc, src = tile_of(cv, i + b, 0, CONV), tile_of(aF, i + b, k, CONV)
                        tap = VT[:, ds(i + (k * KT + b), 1)]
                        if k == 0:
                            dve.tensor_scalar(acc, src, tap, VT[:, ds(i + (COL_CB + b), 1)], ALU.mult, ALU.add).then_inc(conv_step, 1)
                        else:
                            dve.wait_ge(conv_step, i * TAPS + (2 * (k - 1) + b + 1))
                            dve.scalar_tensor_tensor(out=acc, in0=src, scalar=tap, in1=acc, op0=ALU.mult, op1=ALU.add).then_inc(conv_step, 1)

            def normalise_v(t):
                w = WIDTH[t]
                vt = v[0:w, t, :]
                dve.wait_ge(v_gelu, 2 * t + 2)
                for hf in range(2):
                    then(dve.bn_stats(bn[0:w, hf, :], v[0:w, t, hf * 512:(hf + 1) * 512]))
                then(dve.bn_aggr(mv[0:w, :], bn[0:w, :, :].rearrange("p a b -> p (a b)")))
                dve.tensor_copy(vsd[0:w, t:t + 1], mv[0:w, 1:2]).then_inc(v_var, 1)
                dve.wait_ge(v_sd, t + 1)
                then(dve.reciprocal(vsd[0:w, t:t + 1], vsd[0:w, t:t + 1]))
                then(dve.tensor_scalar(vt, vt, mv[0:w, 0:1], vsd[0:w, t:t + 1], ALU.subtract, ALU.mult))
                then(dve.tensor_tensor(vt, vt, vgb[0:w, :], ALU.mult))
                dve.tensor_tensor(vt, vt, vbb[0:w, :], ALU.add).then_inc(v_norm, 1)

            dve.wait_ge(bc_in, 64)
            for t in range(TT):
                w = WIDTH[t]
                for hf in range(2):
                    g = 2 * t + hf
                    if g < 2 * TT - 1:
                        dve.wait_ge(v_ps, g + 1)
                    else:
                        dve.wait_ge(w_used, U_V + 2)
                    cols = slice(hf * 512, (hf + 1) * 512)
                    dve.tensor_tensor(v[0:w, t, cols], PS[0:w, g % 6, :], bvb[0:w, cols], ALU.add).then_inc(v_biased, 1)
                if t:
                    normalise_v(t - 1)
            normalise_v(TT - 1)
            for h in range(KT):
                b = h % 2
                dve.wait_ge(mix_ps, h + 1)
                if h >= 2:
                    dve.wait_ge(gated, h - 1)
                dve.tensor_tensor(tmp[:, b, 0:NPROMPT].rearrange("p (c t) -> p c t", t=P),
                                  PS[:, 2 * b, :].rearrange("p (c t) -> p c t", t=P),
                                  bsb[:, h:h + 1, :].to_broadcast([P, 4, P]), ALU.add).then_inc(mix_added, 1)
                dve.tensor_tensor(tmp[:, b, NPROMPT:T], PS[:, 2 * b + 1, 0:NSAMPLE], bsb[:, h, 0:NSAMPLE], ALU.add).then_inc(dve_drained, 1)
                dve.wait_ge(mix_added, h + 1)
                dve.wait_ge(dve_drained, h + 1)
                dve.tensor_tensor(uT[:, h, :], uT[:, h, :], tmp[:, b, 0:T], ALU.mult).then_inc(gated, 1)
            dve.wait_ge(stat_ps, 1)
            for j in range(KT):
                dve.tensor_tensor(two(cv[:, j, :]), two(cv[:, j, :]), PS[:, 6:8, 0:CH], ALU.subtract).then_inc(centred, 1)
            dve.wait_ge(centred, KT)
            dve.wait_ge(c_std, 1)
            dve.reciprocal(rstdc[:, :], rstdc[:, :]).then_inc(dve_drained, 2)
            dve.wait_ge(dve_drained, KT + 2)
            dve.wait_ge(squared, KT)
            for j in range(KT):
                dve.tensor_tensor(cv[:, j, :], cv[:, j, :], rstdc[:, :], ALU.mult).then_inc(c_normed, 1)
            with dve.Fori(0, KT // 2) as half:
                i = half * 2
                for b in range(2):
                    m_j = mT[:, ds(i + b, 1), :].rearrange("p o (h t) -> p (o h) t", h=2)
                    dve.wait_ge(act_drained, i + (Q_YB + b + 1))
                    dve.tensor_tensor(m_j, PS[:, 4 * b + 2:4 * b + 4, 0:H], two(tmp[:, b, 0:T]), ALU.mult).then_inc(dve_drained, 1)
            with dve.Fori(0, KT // 2) as half:
                i = half * 2
                for b in range(2):
                    m_j = mT[:, ds(i + b, 1), :].rearrange("p o (h t) -> p (o h) t", h=2)
                    dve.wait_ge(act_drained, i + (Q_YA + b + 1))
                    dve.tensor_tensor(two(tmp[:, 2 + b, 0:T]), PS[:, 4 * b + 2:4 * b + 4, 0:H], two(tmp[:, b, 0:T]), ALU.mult).then_inc(dve_drained, 1)
                    dve.wait_ge(dve_drained, i + (10 + KT + b + 1))
                    dve.tensor_tensor(m_j, m_j, two(tmp[:, 2 + b, 0:T]), ALU.add).then_inc(merged, 2)
            dve.wait_ge(mb_in, 64)
            dve.wait_ge(mb2_in, 48)
            for s, rows in ((0, P), (1, NSAMPLE)):
                then(dve.scalar_tensor_tensor(out=a2b[s][0:rows, :], in0=a2b[s][0:rows, :], scalar=1.0, in1=gn2b[0:rows, :],
                                              op0=ALU.add, op1=ALU.mult))
            for t in range(TT):
                w, s = WIDTH[t], t // 4
                for hf in range(2):
                    if t < 4 or hf == 0:
                        dve.wait_ge(o_ps, 2 * t + hf + 1)
                    else:
                        dve.wait_ge(w_used, U_O + 2)
                    cols = slice(hf * 512, (hf + 1) * 512)
                    dve.tensor_tensor(mg[0:w, cols], PS[0:w, (2 * t + hf) % 8, :], g1b[s][0:w, cols], ALU.mult).then_inc(o_drained, 1)
                dve.wait_ge(o_drained, 2 * t + 2)
                dve.tensor_tensor(x[0:w, t, :], x[0:w, t, :], mg[0:w, :], ALU.add).then_inc(x1_ready, 1)
                dve.wait_ge(x1_ready, t + 1)
                dve.wait_ge(x1_sd, t + 1)
                then(dve.reciprocal(rs[0:w, t:t + 1], sd[0:w, t:t + 1]))
                if t >= 2:
                    dve.wait_ge(h2_ps, t - 1)
                    dve.wait_ge(h2_stored[t % 2], 16 * (t // 2))
                then(dve.scalar_tensor_tensor(out=h2[0:w, t % 2, :], in0=x[0:w, t, :], scalar=rs[0:w, t:t + 1], in1=a2b[s][0:w, :],
                                              op0=ALU.mult, op1=ALU.mult))
                dve.tensor_tensor(h2[0:w, t % 2, :], h2[0:w, t % 2, :], sh2b[s][0:w, :], ALU.add).then_inc(h2_ready, 1)

            def wide(ap, *shape):
                return ap.to_broadcast(list(shape))

            def first_one(out, logits, n, best):
                then(dve.tensor_reduce(best, logits, AX, ALU.max))
                then(dve.tensor_tensor(scr[:, :, 0:n], logits, wide(best.unsqueeze(2), P, TT, n), ALU.is_equal))
                then(dve.tensor_tensor(scr[:, :, 0:n], scr[:, :, 0:n], wide(rev[:, 0:1, EPG - n:EPG], P, TT, n), ALU.mult))
                then(dve.tensor_reduce(mx[:, 3, :], scr[:, :, 0:n], AX, ALU.max))
                then(dve.tensor_tensor(out, scr[:, :, 0:n], wide(mx[:, 3, :].unsqueeze(2), P, TT, n), ALU.is_equal))

            then(dve.tensor_scalar(rev[:, 0, :], iota[:, 0:EPG], -1.0, float(EPG), ALU.mult, ALU.add))
            then(dve.memset(lg, 0.0))
            dve.wait_ge(log_ps, 1)
            then(dve.tensor_tensor(lg[:, 0:4, :], PS[:, 0, 0:4 * NLOG].rearrange("p (t n) -> p t n", n=NLOG),
                                   wide(brb[:, :].unsqueeze(1), P, 4, NLOG), ALU.add))
            then(dve.tensor_tensor(lg[0:NSAMPLE, 4, :], PS[0:NSAMPLE, 0, 4 * NLOG:5 * NLOG], brb[0:NSAMPLE, :], ALU.add))
            groups = lg[:, :, 0:NG]
            first_one(one_g, groups, NG, mx[:, 0, :])
            then(dve.tensor_tensor(diffs[:, :, 0:NG], groups, wide(mx[:, 0, :].unsqueeze(2), P, TT, NG), ALU.subtract))
            for g in range(NG):
                one = wide(one_g[:, :, g:g + 1], P, TT, EPG)
                mine = lg[:, :, NG + g * EPG:NG + (g + 1) * EPG]
                if g == 0:
                    then(dve.tensor_tensor(lsel[:, 0], mine, one, ALU.mult))
                else:
                    then(dve.tensor_tensor(scr, mine, one, ALU.mult))
                    then(dve.tensor_tensor(lsel[:, 0], lsel[:, 0], scr, ALU.add))
            first_one(one_e[:, 0], lsel[:, 0], EPG, mx[:, 1, :])
            then(dve.scalar_tensor_tensor(out=lsel[:, 1], in0=one_e[:, 0], scalar=-3.0e38, in1=lsel[:, 0], op0=ALU.mult, op1=ALU.add))
            first_one(one_e[:, 1], lsel[:, 1], EPG, mx[:, 2, :])
            dve.tensor_tensor(diffs[:, :, NG], mx[:, 2, :], mx[:, 1, :], ALU.subtract).then_inc(log_ready, 1)
            for k in range(2):
                for g in range(NG):
                    then(dve.tensor_tensor(OH[:, k, :, g * EPG:(g + 1) * EPG], one_e[:, k], wide(one_g[:, :, g:g + 1], P, TT, EPG), ALU.mult))
                then(dve.tensor_tensor(OH[:, k], OH[:, k], wide(valid[:, :].unsqueeze(2), P, TT, NE), ALU.mult))
            dve.tensor_tensor(OHs, OH[:, 0], OH[:, 1], ALU.add).then_inc(oh_ready, 1)
            dve.wait_ge(e_ready, 1)
            then(dve.tensor_reduce(mx[:, 0, :], exps[:, :, 0:NG], AX, ALU.add))
            then(dve.scalar_tensor_tensor(out=mx[:, 0, :], in0=exps[:, :, NG], scalar=1.0, in1=mx[:, 0, :], op0=ALU.add, op1=ALU.mult))
            then(dve.reciprocal(wk[:, 0, :], mx[:, 0, :]))
            then(dve.tensor_tensor(wk[:, 1, :], wk[:, 0, :], exps[:, :, NG], ALU.mult))
            dve.wait_ge(rank_ps, 1)
            earlier = PS[:, 1, 0:TT * NE].rearrange("p (t e) -> p t e", e=NE)
            for k in range(2):
                then(dve.tensor_tensor(prod, OH[:, k], earlier, ALU.mult))
                then(dve.tensor_reduce(rank[:, k, :], prod, AX, ALU.add))
            then(dve.tensor_tensor(cmp, wide(PS[:, 1, TT * NE:(TT + 1) * NE].unsqueeze(2), P, NE, STEPS),
                                   wide(steps[:, :].unsqueeze(1), P, NE, STEPS), ALU.is_gt))
            then(dve.tensor_reduce(nov, cmp, AX, ALU.add))
            then(dve.tensor_copy(cum[:, 0, :], nov))
            at, step = 0, 1
            while step < NE:
                then(dve.tensor_copy(cum[:, 1 - at, 0:step], cum[:, at, 0:step]))
                then(dve.tensor_tensor(cum[:, 1 - at, step:NE], cum[:, at, step:NE], cum[:, at, 0:NE - step], ALU.add))
                at, step = 1 - at, 2 * step
            upto = cum[:, at, :]
            then(dve.tensor_tensor(exc, upto, nov, ALU.subtract))
            then(dve.tensor_tensor(ocmp, wide(upto.unsqueeze(1), P, OVER, NE), wide(iota[:, 0:OVER].unsqueeze(2), P, OVER, NE), ALU.is_le))
            then(dve.tensor_reduce(oex, ocmp, AX, ALU.add))
            then(dve.tensor_scalar(over_expert[0:1, :], oex[0:1, :], float(NE - 1), None, ALU.min))
            for k in range(2):
                then(dve.tensor_tensor(prod, OH[:, k], wide(exc.unsqueeze(1), P, TT, NE), ALU.mult))
                then(dve.tensor_reduce(ovs[:, k, :], prod, AX, ALU.add))
                then(dve.tensor_tensor(prod, OH[:, k], wide(iota[:, 0:NE].unsqueeze(1), P, TT, NE), ALU.mult))
                then(dve.tensor_reduce(eid[:, k, :], prod, AX, ALU.add))
            flat = {n: ap.rearrange("p a b -> p (a b)") for n, ap in
                    (("rank", rank), ("ovs", ovs), ("eid", eid), ("q", q), ("tile", tile), ("off", off), ("wk", wk))}
            then(dve.tensor_tensor(q8, wide(flat["rank"].unsqueeze(2), P, 2 * TT, STEPS), wide(steps[:, :].unsqueeze(1), P, 2 * TT, STEPS), ALU.is_ge))
            then(dve.tensor_reduce(flat["q"], q8, AX, ALU.add))
            then(dve.scalar_tensor_tensor(out=flat["off"], in0=flat["q"], scalar=-float(SLOTS), in1=flat["rank"], op0=ALU.mult, op1=ALU.add))
            then(dve.tensor_tensor(flat["ovs"], flat["ovs"], flat["q"], ALU.add))
            then(dve.scalar_tensor_tensor(out=flat["ovs"], in0=flat["ovs"], scalar=float(NE - 1), in1=flat["eid"], op0=ALU.add, op1=ALU.subtract))
            then(dve.tensor_scalar(flat["q"], flat["q"], 1.0, None, ALU.min))
            then(dve.tensor_tensor(flat["ovs"], flat["ovs"], flat["q"], ALU.mult))
            then(dve.tensor_tensor(flat["tile"], flat["eid"], flat["ovs"], ALU.add))
            then(dve.tensor_tensor(TOH, wide(flat["tile"].unsqueeze(2), P, 2 * TT, TILES), wide(iota[:, 0:TILES].unsqueeze(1), P, 2 * TT, TILES), ALU.is_equal))
            for k in range(2):
                then(dve.tensor_tensor(TOH[:, k * TT:(k + 1) * TT, :], TOH[:, k * TT:(k + 1) * TT, :], wide(valid[:, :].unsqueeze(2), P, TT, TILES), ALU.mult))
            then(dve.tensor_tensor(FOH, wide(flat["off"].unsqueeze(2), P, 2 * TT, SLOTS), wide(iota[:, 0:SLOTS].unsqueeze(1), P, 2 * TT, SLOTS), ALU.is_equal))
            for k in range(2):
                then(dve.tensor_scalar(pid[:, k, :], tokid[:, :], 1.0, float(k * T + 1), ALU.mult, ALU.add))
                half = slice(k * TT, (k + 1) * TT)
                for n, what in enumerate((tokid[:, :], pid[:, k, :], wk[:, k, :])):
                    last = dve.tensor_tensor(R[:, half, n * TILES:(n + 1) * TILES], TOH[:, half, :], wide(what.unsqueeze(2), P, TT, TILES), ALU.mult)
                    if k == 0 or n < 2:
                        then(last)
            last.then_inc(tab_ready, 1)
            dve.wait_ge(tab_ps, 1)
            then(dve.tensor_copy(tokI[:, :], PS[0:SLOTS, 2, 0:TILES]))
            then(dve.tensor_copy(wslot[:, :], PS[0:SLOTS, 2, 2 * TILES:3 * TILES]))
            then(dve.tensor_scalar(un[0:SLOTS, :], PS[0:SLOTS, 2, TILES:2 * TILES], 0.0, 4096.0, ALU.is_equal, ALU.mult))
            dve.scalar_tensor_tensor(out=pairI[:, :], in0=PS[0:SLOTS, 2, TILES:2 * TILES], scalar=-1.0, in1=un[0:SLOTS, :],
                                     op0=ALU.add, op1=ALU.add).then_inc(routed, 1)
            dve.wait_ge(routed, 1)

            def take_rows(t, b):
                dve.wait_ge(t_ps, t)
                dve.tensor_copy(hG[:, b, :], PS[:, b, :]).then_inc(hg_ready, 1)

            def hidden(t, b):
                dve.wait_ge(sil_ready, t)
                dve.tensor_tensor(heT[:, b, :, :].rearrange("p k s -> p (k s)"), PS[:, 2 + b, 2 * SLOTS:4 * SLOTS], sil[:, b, :], ALU.mult).then_inc(he_ready, 1)

            def weigh(t, b, col, scattered_before):
                dve.wait_ge(down_done, t)
                if scattered_before is not None:
                    dve.wait_ge(scattered[b], scattered_before)
                dve.tensor_scalar(Y[0:SLOTS, b, 512:1024], PS[0:SLOTS, 5 + 2 * b, :], col, None, ALU.mult).then_inc(y_dve, 1)

            take_rows(1, 0)
            for b in range(2):
                take_rows(b + 2, 1 - b)
                hidden(b + 1, b)
                weigh(b + 1, b, wslot[:, b:b + 1], None)
            with dve.Fori(0, (TILES - 4) // 2) as half:
                i = half * 2
                for b in range(2):
                    take_rows(i + (b + 4), 1 - b)
                    hidden(i + (b + 3), b)
                    weigh(i + (b + 3), b, wslot[:, ds(i + (b + 2), 1)], i * 8 + 16)
            take_rows(TILES, 1)
            hidden(TILES - 1, 0)
            weigh(TILES - 1, 0, wslot[:, TILES - 2:TILES - 1], 8 * (TILES - 2))
            hidden(TILES, 1)
            weigh(TILES, 1, wslot[:, TILES - 1:TILES], 8 * (TILES - 2))

            dve.wait_ge(fin_in, 16 * 7)
            for s, rows in ((0, P), (1, NSAMPLE)):
                then(dve.scalar_tensor_tensor(out=afb[s][0:rows, :], in0=afb[s][0:rows, :], scalar=1.0, in1=gfb[0:rows, :],
                                              op0=ALU.add, op1=ALU.mult))

            def finish(t):
                w, s = WIDTH[t], t // 4
                o = pair_rows[0][0:w, t, :]
                dve.wait_ge(f_sd, t + 1)
                then(dve.reciprocal(rs[0:w, t:t + 1], sd[0:w, t:t + 1]))
                then(dve.scalar_tensor_tensor(out=o, in0=x[0:w, t, :], scalar=rs[0:w, t:t + 1], in1=afb[s][0:w, :],
                                              op0=ALU.mult, op1=ALU.mult))
                dve.tensor_tensor(o, o, shfb[s][0:w, :], ALU.add).then_inc(f_out, 1)

            for t in range(TT):
                w, s = WIDTH[t], t // 4
                o = pair_rows[0][0:w, t, :]
                dve.wait_ge(pair_in[t], 32)
                then(dve.tensor_tensor(o, o, pair_rows[1][0:w, t, :], ALU.add))
                then(dve.tensor_tensor(o, o, g2b[s][0:w, :], ALU.mult))
                dve.tensor_tensor(x[0:w, t, :], x[0:w, t, :], o, ALU.add).then_inc(f_sum, 1)
                if t:
                    finish(t - 1)
            finish(TT - 1)

        @block.gpsimd
        def _(pool):
            pool.memset(ident[:, :], 0.0).then_inc(consts, 1)
            pool.memset(before[:, :], 1.0).then_inc(consts, 1)
            pool.memset(valid[:, :], 1.0).then_inc(consts, 1)
            pool.wait_ge(consts, 3)
            pool.affine_select(out=ident[:, :], in_=ident[:, :], compare_op=ALU.not_equal, fill=1.0, base=0,
                               pattern=[[-1, P]], channel_multiplier=1).then_inc(consts, 1)
            pool.affine_select(out=before[:, :], in_=before[:, :], compare_op=ALU.is_gt, fill=0.0, base=0,
                               pattern=[[1, P]], channel_multiplier=-1).then_inc(consts, 1)
            pool.affine_select(out=valid[:, :], in_=valid[:, :], compare_op=ALU.is_gt, fill=0.0, base=T,
                               pattern=[[-P, TT]], channel_multiplier=-1).then_inc(consts, 1)
            pool.iota(iotaI[:, :], pattern=[[1, SLOTS]], base=0, channel_multiplier=0).then_inc(consts, 1)
            pool.iota(tokidI[:, :], pattern=[[P, TT]], base=0, channel_multiplier=1).then_inc(consts, 1)
            pool.memset(meanm[:, :], 1.0 / D).then_inc(consts, 1)
            pool.memset(ones[:, :], 1.0).then_inc(consts, 1)
            pool.memset(eps[:, :], EPS).then_inc(consts, 1)
            pool.memset(ss[:, :], 1.0).then_inc(consts, 1)
            for m in range(STEPS):
                pool.memset(steps[:, m:m + 1], float(SLOTS * (m + 1))).then_inc(consts, 1)
            pool.memset(aF[:, :, 0:HIST], 0.0).then_inc(aF_written, 4)
            pool.wait_ge(ws_in, 16)
            for h in range(KT):
                pool.affine_select(out=wsR[:, h, :], in_=wsR[:, h, :], compare_op=ALU.is_ge, fill=0.0, base=0,
                                   pattern=[[-1, P]], channel_multiplier=1).then_inc(ws_masked, 1)

            def add_bias(b, drained, landed, added, cols):
                pool.wait_ge(act_drained, drained)
                pool.wait_ge(w_full[b], landed)
                pool.tensor_tensor(mrow[:, b, :], mrow[:, b, :], brow[:, b, :], ALU.add).then_inc(mod_added, 1)
                pool.wait_ge(mod_added, added)
                pool.dma_start(mod[:, cols], mrow[:, b, :]).then_inc(mod_stored[b], 16)

            for m in range(4):
                add_bias(m % 2, m + 1, 32 * (m // 2 + 1), m + 1, slice(m * BLK, (m + 1) * BLK))
            with pool.Fori(0, KT // 2) as half:
                i = half * 2
                for b in range(2):
                    pool.wait_ge(act_drained, i + (Q_A + b + 1))
                    for at, n, first in ((HIST, NPROMPT, 0), (2 * HIST + NPROMPT, NSAMPLE, NPROMPT)):
                        pool.tensor_tensor(aF[:, ds(i + b, 1), at:at + n].rearrange("p o t -> p (o t)"), tmp[:, b, first:first + n],
                                           tmp[:, 2 + b, first:first + n], ALU.mult).then_inc(aF_written, 1)
            pool.wait_ge(v_norm, TT)
            pool.dma_start(v_out, v[0:NSAMPLE, 4, :]).then_inc(v_stored, 16)
            pool.wait_ge(v_stored, 16)
            for j in range(KT):
                pool.wait_ge(centred, j + 1)
                pool.tensor_tensor(sq[:, j, :], cv[:, j, :], cv[:, j, :], ALU.mult).then_inc(squared, 1)
            with pool.Fori(0, 12 // 2) as half:
                i = half * 2
                for b in range(2):
                    add_bias(b, i + (Q_ADA2 + b + 1), i * 16 + 32 * (U_ADA2 // 2 + 1), i + (5 + b), ds(i * BLK + (4 + b) * BLK, BLK))

            pool.wait_ge(routed, 1)
            pool.wait_ge(h2_stored[0], 48)
            pool.wait_ge(h2_stored[1], 32)

            last_token, last_pair = pool.to_reg(T - 1), pool.to_reg(2 * T - 1)

            def gather(b, col, t):
                pool.tensor_copy(gidx[b][:, :], col).then_inc(g_idx, 1)
                pool.wait_ge(g_idx, t)
                pool.sem_inc(gathers_begun)
                pool.indirect_dma_start(out=G[0:SLOTS, b, :], out_offset=None, in_=h2d,
                                        in_offset=bass.IndirectOffsetOnAxis(ap=gidx[b][:, 0:1], axis=0),
                                        bounds_check=last_token, oob_is_err=True).then_inc(gathered[b], 16)

            def scatter(b, col, t, scattered_before):
                if scattered_before is not None:
                    pool.wait_ge(scattered[b], scattered_before)
                pool.tensor_copy(sidx[b][:, :], col).then_inc(s_idx, 1)
                pool.wait_ge(s_idx, t)
                pool.wait_ge(y_act, t)
                pool.wait_ge(y_dve, t)
                pool.sem_inc(scatters_begun)
                pool.indirect_dma_start(out=pairs, out_offset=bass.IndirectOffsetOnAxis(ap=sidx[b][:, 0:1], axis=0),
                                        in_=Y[0:SLOTS, b, :], in_offset=None,
                                        bounds_check=last_pair, oob_is_err=False).then_inc(scattered[b], 16)

            gather(0, tokI[:, 0:1], 1)
            gather(1, tokI[:, 1:2], 2)
            for b in range(2):
                scatter(b, pairI[:, b:b + 1], b + 1, None)
                gather(b, tokI[:, 2 + b:3 + b], b + 3)
            with pool.Fori(0, (TILES - 4) // 2) as half:
                i = half * 2
                for b in range(2):
                    scatter(b, pairI[:, ds(i + (2 + b), 1)], i + (b + 3), i * 8 + 16)
                    gather(b, tokI[:, ds(i + (b + 4), 1)], i + (b + 5))
            for b in range(2):
                scatter(b, pairI[:, TILES - 2 + b:TILES - 1 + b], TILES - 1 + b, 8 * (TILES - 2))
            for b in range(2):
                pool.wait_ge(scattered[b], 8 * TILES)


_INS = ["x_prompt", "x_sample", "cache_conv", "c_prompt", "c_sample", "w_ada", "b_ada", "g_norm1", "g_norm2",
        "w_in", "b_in", "conv_w", "conv_b", "ln_g", "ln_b", "w_a", "v_ln_g", "v_ln_b", "w_s", "b_s", "w_b", "w_o",
        "w_rg", "b_rg", "w_re", "b_re", "w_gate", "w_up", "w_down", "g_final", "w_ada_f", "b_ada_f"]


def kernel(**inputs):
    import concourse.bacc as bacc
    from concourse.bass_utils import run_bass_kernel_spmd

    nc = bacc.Bacc("TRN2", target_bir_lowering=False, num_devices=1)
    arrays = {name: np.ascontiguousarray(inputs[name]) for name in _INS}
    aps = {name: nc.dram_tensor(name, arr.shape, mybir.dt.from_np(arr.dtype), kind="ExternalInput").ap()
           for name, arr in arrays.items()}
    outs = [nc.dram_tensor(name, shape, F32, kind="ExternalOutput").ap() for name, shape in
            (("y", (T, D)), ("hist_prompt", (HIST, D)), ("hist_sample", (HIST, D)), ("v_rows", (NSAMPLE, D)))]
    build(nc, aps, *outs)
    r = run_bass_kernel_spmd(nc, [arrays], core_ids=[0]).results[0]
    y = r["y"]
    return (y[:NPROMPT].reshape(1, NPROMPT, D), y[NPROMPT:].reshape(1, NSAMPLE, D),
            r["hist_prompt"].reshape(1, 1, HIST, D), r["hist_sample"].reshape(1, 1, HIST, D),
            r["v_rows"].reshape(1, 1, NSAMPLE, D))
```

```python
from contextlib import ExitStack

import numpy as np

import concourse.bass as bass
from concourse import mybir

F32 = mybir.dt.float32
I32 = mybir.dt.int32
U32 = mybir.dt.uint32
ALU = mybir.AluOpType
ACT = mybir.ActivationFunctionType
AX = mybir.AxisListType.X
ds = bass.ds

P = 128
D = 1024
KT = D // P
NPROMPT, NSAMPLE = 512, 32
T = NPROMPT + NSAMPLE
TT = 5
WIDTH = [P, P, P, P, NSAMPLE]
H = T // 2
TAPS = 31
HIST = TAPS - 1
FULL = T + 2 * HIST
CONV = FULL - HIST
CH = CONV // 2
SAMPLE0 = NPROMPT + HIST
EPS = 1e-6
NG, EPG, NE = 4, 8, 32
DE = 256
SLOTS = 128
OVER = 2 * T // SLOTS
TILES = NE + OVER
ALWAYS = NE + 2
STEPS = T // SLOTS
NLOG = NG + NE
BLK = 512
NMOD = 8 * D

O_X, O_H, O_A, O_C, O_S, O_U, O_V, O_W = 0, 5120, 9472, 14304, 18896, 23248, 27600, 32720
ARENA = 40912
H2_BANK = [6, 2, 4, 6, 2]


def build(nc, a, y_out, hist_p_out, hist_s_out, v_out):
    with ExitStack() as ctx:
        def sb(name, shape, dt=F32):
            return ctx.enter_context(nc.sbuf_tensor(name, shape, dt))

        def sem(name):
            return ctx.enter_context(nc.semaphore(name))

        PS = ctx.enter_context(nc.psum_tensor("PS", [P, 8, 512], F32))
        arena = sb("arena", [P, ARENA])

        def view(at, *dims):
            n = 1
            for d in dims:
                n *= d
            v = arena[:, at:at + n]
            if len(dims) == 2:
                v = v.rearrange("p (a b) -> p a b", b=dims[1])
            if len(dims) == 3:
                v = v.rearrange("p (a b c) -> p a b c", b=dims[1], c=dims[2])
            return v

        x = view(O_X, TT, D)
        hT = view(O_H, KT, T)
        aF = view(O_A, KT, FULL)
        cv = view(O_C, KT, CONV)
        aT = view(O_S, KT, T)
        uT = view(O_U, KT, T)
        v = view(O_V, TT, D)
        mT = view(O_V, KT, T)
        sq = view(O_V, KT, CONV)
        W = [view(O_W + 4096 * s, KT, BLK) for s in range(2)]
        WP = [view(O_W + 4096 * s, 4, KT, P) for s in range(2)]
        xn = view(O_U, 2, D)
        cacheR = view(O_S, 3, D)[:, 2, :]
        histR = view(O_S, 2, D)
        wsR = view(O_S + 3072, KT, P)
        VR = view(O_U + 2048, 4, P)
        WG = [view(O_A + 6144 * s, KT, DE) for s in range(2)]
        WU = [view(O_A + 6144 * s + 2048, KT, DE) for s in range(2)]
        WD = [view(O_A + 6144 * s + 4096, 2, D) for s in range(2)]
        g1b = [view(O_U, D), view(O_U + 1024, D)]
        a2b = [view(O_U + 2048, D), view(O_U + 3072, D)]
        sh2b = [view(O_H + 2048, D), view(O_H + 3072, D)]
        gn2b = view(O_A + 12288, D)
        h2 = view(O_H, 2, D)
        G = view(O_V, 2, D)
        hG = view(O_V + 2048, 2, KT * SLOTS)
        Y = view(O_U + 1024, 2, D)
        sil = view(O_U, DE)
        he = view(O_U + DE, DE)
        heT = view(O_U + 2 * DE, 2, SLOTS)
        pair_rows = [view(O_A + 5120 * k, TT, D) for k in range(2)]
        g2b = [view(O_W, D), view(O_W + 1024, D)]
        afb = [view(O_W + 2048, D), view(O_W + 3072, D)]
        shfb = [view(O_W + 4096, D), view(O_W + 5120, D)]
        gfb = view(O_W + 6144, D)
        at_w = [O_W]

        def table(*dims):
            n = 1
            for d in dims:
                n *= d
            r = view(at_w[0], *dims)
            at_w[0] += n
            return r

        ident = sb("ident", [P, P])
        meanm = sb("meanm", [P, P])
        before = sb("before", [P, P])
        ones = sb("ones", [P, P])
        eps = sb("eps", [P, 1])
        vecs = sb("vecs", [P, KT * T])
        bsb = vecs[:, 0:1024].rearrange("p (h t) -> p h t", t=P)
        bvb, vgb, vbb = (vecs[:, 1024 * n:1024 * (n + 1)] for n in (1, 2, 3))
        h2T = vecs[:, :].rearrange("p (k t) -> p k t", t=T)
        wsT = sb("wsT", [P, KT, P])
        tmp = sb("tmp", [P, 4, CONV])
        tmp2 = tmp[:, :, :].rearrange("p (a b) t -> p a (b t)", b=2)
        mg, sqj = tmp2[:, 0, 0:D], tmp2[:, 1, 0:D]
        rstdc = sb("rstdc", [P, CONV])
        VT = sb("VT", [P, 360])
        S1 = sb("S1", [P, 2, KT])
        c16 = sb("c16", [16, P])
        cT = sb("cT", [P, 2, KT])
        brow = sb("brow", [2, 2, BLK])
        mrow = sb("mrow", [2, 2, BLK])
        ss = sb("ss", [P, 8])
        sd = sb("sd", [P, 8])
        rs = sb("rs", [P, 8])
        vsd = sb("vsd", [P, 8])
        bn = sb("bn", [P, 2, 6])
        mv = sb("mv", [P, 2])
        wr = sb("wr", [P, KT, NLOG])
        brb = sb("brb", [P, NLOG])
        tokI = sb("tokI", [SLOTS, TILES], U32)
        pairI = sb("pairI", [SLOTS, TILES], U32)
        wslot = sb("wslot", [SLOTS, TILES])
        over_expert = sb("over_expert", [1, OVER + 1], I32)
        gidx = [sb(f"gidx{b}", [SLOTS, 1], U32) for b in range(2)]
        sidx = [sb(f"sidx{b}", [SLOTS, 1], U32) for b in range(2)]
        COL_CB, COL_BIN, COL_LG, COL_LB, COL_G1, COL_MOD = 248, 256, 304, 312, 320, 328

        mod = nc.dram_tensor("mod", (2, NMOD), F32, kind="Internal").ap()
        h2d = nc.dram_tensor("h2d", (T, D), F32, kind="Internal").ap()
        pairs = nc.dram_tensor("pairs", (2 * T, D), F32, kind="Internal").ap()

        consts = sem("consts")
        c_in, x_in, vec_in, bc_in, rt_in = (sem(n) for n in ("c_in", "x_in", "vec_in", "bc_in", "rt_in"))
        ws_in, cache_in, ws_masked = sem("ws_in"), sem("cache_in"), sem("ws_masked")
        c_silu, x_sq, x_sd = sem("c_silu"), sem("x_sq"), sem("x_sd")
        start_ps, start_dr, xn_ready = sem("start_ps"), sem("start_dr"), sem("xn_ready")
        w_full = [sem("w_full0"), sem("w_full1")]
        w_used = sem("w_used")
        act_drained = sem("act_drained")
        mod_added = sem("mod_added")
        mod_stored = [sem("mod_stored0"), sem("mod_stored1")]
        loads_begun, turns_begun, gathers_begun, scatters_begun = (sem(n) for n in ("loads_begun", "turns_begun", "gathers_begun", "scatters_begun"))
        modr_in, h_ready = sem("modr_in"), sem("h_ready")
        dve_step = sem("dve_step")
        act_step = sem("act_step")
        aF_written, conv_step = sem("aF_written"), sem("conv_step")
        hist_ps, hist_copied, hist_stored = sem("hist_ps"), sem("hist_copied"), sem("hist_stored")
        v_ps, v_biased, v_gelu, v_norm, v_stored = (sem(n) for n in ("v_ps", "v_biased", "v_gelu", "v_norm", "v_stored"))
        mix_ps, dve_drained, stat_ps = sem("mix_ps"), sem("dve_drained"), sem("stat_ps")
        centred, squared, c_std, c_normed, a_ready = (sem(n) for n in ("centred", "squared", "c_std", "c_normed", "a_ready"))
        merged, mix_added, gated, v_var, v_sd = (sem(n) for n in ("merged", "mix_added", "gated", "v_var", "v_sd"))
        o_ps, o_drained = sem("o_ps"), sem("o_drained")
        mb_in, mb2_in = sem("mb_in"), sem("mb2_in")
        x1_ready, x1_sd, h2_ready, h2_ps, h2_copied = (sem(n) for n in ("x1_ready", "x1_sd", "h2_ready", "h2_ps", "h2_copied"))
        h2_stored = [sem("h2_stored0"), sem("h2_stored1")]
        log_ps, log_ready, e_ready, oh_ready, rank_ps, tab_ready, tab_ps = (sem(n) for n in ("log_ps", "log_ready", "e_ready", "oh_ready", "rank_ps", "tab_ready", "tab_ps"))
        routed = sem("routed")
        gu_full = [sem("gu_full0"), sem("gu_full1")]
        wd_full = [sem("wd_full0"), sem("wd_full1")]
        g_idx, s_idx = sem("g_idx"), sem("s_idx")
        gathered = [sem("gathered0"), sem("gathered1")]
        scattered = [sem("scattered0"), sem("scattered1")]
        t_ps, hg_ready, gu_done, sil_ready, he_ready, he_ps, het_ready, down_done = (sem(n) for n in ("t_ps", "hg_ready", "gu_done", "sil_ready", "he_ready", "he_ps", "het_ready", "down_done"))
        experts_done = sem("experts_done")
        y_act, y_dve = sem("y_act"), sem("y_dve")
        fin_in, pair_in = sem("fin_in"), [sem(f"pair_in{t}") for t in range(TT)]
        f_sum, f_sd, f_out, f_stored = (sem(n) for n in ("f_sum", "f_sd", "f_out", "f_stored"))

        iotaI = sb("iotaI", [P, SLOTS], I32)
        iota = sb("iota", [P, SLOTS])
        tokidI = sb("tokidI", [P, TT], I32)
        tokid = sb("tokid", [P, TT])
        valid = sb("valid", [P, TT])
        steps = sb("steps", [P, STEPS])
        lg = table(TT, NLOG)
        one_g = table(TT, NG)
        one_e = table(2, TT, EPG)
        lsel = table(2, TT, EPG)
        prod = table(TT, NE)
        scr = table(TT, EPG)
        mx = table(4, TT)
        diffs = table(TT, NG + 1)
        exps = table(TT, NG + 1)
        wk = table(2, TT)
        OH = table(2, TT, NE)
        OHs = table(TT, NE)
        rank = table(2, TT)
        cmp = table(NE, STEPS)
        nov = table(NE)
        cum = table(2, NE)
        exc = table(NE)
        ovs = table(2, TT)
        eid = table(2, TT)
        q8 = table(2 * TT, STEPS)
        pid = table(2, TT)
        rev = table(1, EPG)
        q = table(2, TT)
        tile = table(2, TT)
        off = table(2, TT)
        TOH = table(2 * TT, TILES)
        FOH = table(2 * TT, SLOTS)
        R = table(2 * TT, 3 * TILES)
        un = table(TILES)
        ocmp = table(OVER, NE)
        oex = table(OVER)
        assert at_w[0] <= ARENA

        NCONST = 12 + STEPS
        block = ctx.enter_context(nc.Block())

        def cnt(i, c, per=1, more=0):
            return c * per + more if i is None else i * per + (c * per + more)

        def col(i, c):
            return slice(c, c + 1) if i is None else ds(i + c, 1)

        def tiles(eng, first, last, step):
            with eng.Fori(0, (last + 1 - first) // 2) as half:
                i = half * 2
                for m in range(2):
                    step(i, first + m, (first + m + 1) % 2)

        def some_overflow(eng):
            n = eng.value_load(over_expert[0:1, OVER:OVER + 1], min_val=0, max_val=OVER)
            return eng.If(n > ALWAYS - NE)

        def full(eng, n):
            eng.wait_ge(w_full[n % 2], 32 * (n // 2 + 1))

        U_ADA1, U_A, U_U, U_V, U_ADA2, U_YB, U_YA, U_O = 0, 4, 12, 16, 18, 30, 38, 46
        Q_A, Q_U, Q_ADA2, Q_YB, Q_YA = 4, 12, 16, 28, 36

        w_ada = a["w_ada"][0].rearrange("(k p) n -> p k n", p=P)
        w_adaf = a["w_ada_f"].rearrange("(k p) n -> p k n", p=P)
        w_in = a["w_in"][0].rearrange("(k p) n -> p k n", p=P)
        w_a = a["w_a"][0].rearrange("(k p) n -> p k n", p=P)
        w_b = a["w_b"][0].rearrange("(k p) n -> p k n", p=P)
        w_o = a["w_o"][0].rearrange("(k p) n -> p k n", p=P)
        w_gate = a["w_gate"][0].rearrange("e (p k) n -> e p (k n)", p=P)
        w_up = a["w_up"][0].rearrange("e (p k) n -> e p (k n)", p=P)
        w_down = a["w_down"][0].rearrange("e (k p) n -> e p k n", p=P)

        @block.sync
        def _(sp):
            def load_block(s, src, bias, wait):
                for sm, val in wait:
                    sp.wait_ge(sm, val)
                sp.dma_start(W[s], src).then_inc(w_full[s], 16)
                sp.dma_start(brow[:, s, :], bias.to_broadcast([2, BLK])).then_inc(w_full[s], 16)

            for n in range(4):
                load_block(n % 2, w_ada[:, :, n * BLK:(n + 1) * BLK], a["b_ada"][:, n * BLK:(n + 1) * BLK],
                           [(w_used, n - 1), (mod_added, n - 1)] if n >= 2 else [])

            def pair_loads(base, left, left0, right, right0):
                with sp.Fori(0, 8 // 2) as half:
                    i = half * 2
                    for b in range(2):
                        c_left, c_right = sp.snap(i * P + (left0 + b * P)), sp.snap(i * P + (right0 + b * P))
                        sp.wait_ge(w_used, i + (base + b - 1))
                        sp.sem_inc(loads_begun)
                        sp.dma_start(WP[b][:, 0], left[:, :, ds(c_left, P)]).then_inc(w_full[b], 16)
                        sp.dma_start(WP[b][:, 1], right[:, :, ds(c_right, P)]).then_inc(w_full[b], 16)

            pair_loads(U_A, w_in, 0, w_in, D)
            with sp.Fori(0, 4 // 2) as half:
                i = half * 2
                for b in range(2):
                    sp.wait_ge(w_used, i + (U_U + b - 1))
                    sp.sem_inc(loads_begun)
                    for m in range(2):
                        sp.dma_start(WP[b][:, m], w_in[:, :, ds(i * (2 * P) + (2 * D + (2 * b + m) * P), P)]).then_inc(w_full[b], 16)

            def halves(base, src, col0):
                for b in range(2):
                    sp.wait_ge(w_used, base + b - 1)
                    for m in range(2):
                        sp.dma_start(W[b][:, 4 * m:4 * m + 4, :], src[:, 4 * m:4 * m + 4, col0 + b * BLK:col0 + (b + 1) * BLK]).then_inc(w_full[b], 16)

            halves(U_V, w_in, 3 * D)

            def ada_loop(first, count, src, bias, col0):
                with sp.Fori(0, count // 2) as half:
                    i = half * 2
                    for b in range(2):
                        sp.wait_ge(w_used, i + (U_ADA2 + first + b - 1))
                        sp.sem_inc(loads_begun)
                        sp.wait_ge(mod_added, i + (4 + first + b - 1))
                        sp.sem_inc(loads_begun)
                        sp.dma_start(W[b], src[:, :, ds(i * BLK + (col0 + b * BLK), BLK)]).then_inc(w_full[b], 16)
                        sp.dma_start(brow[:, b, :], bias[:, ds(i * BLK + (col0 + b * BLK), BLK)].to_broadcast([2, BLK])).then_inc(w_full[b], 16)

            ada_loop(0, 8, w_ada, a["b_ada"], 4 * BLK)
            ada_loop(8, 4, w_adaf, a["b_ada_f"].rearrange("(o n) -> o n", o=1), 0)
            pair_loads(U_YB, w_in, 5 * D, w_b, 0)
            pair_loads(U_YA, w_in, 4 * D, w_a, 0)
            halves(U_O, w_o, 0)

            def mod_vec(n, rows, s):
                return mod[s:s + 1, n * D:(n + 1) * D].to_broadcast([rows, D])

            for p in range(2):
                sp.wait_ge(mod_stored[p], 16 * 8)
            sp.wait_ge(w_used, U_YB + 8)
            for s, rows in ((0, P), (1, NSAMPLE)):
                sp.dma_start(g1b[s][0:rows, :], mod_vec(2, rows, s)).then_inc(mb_in, 16)
                sp.dma_start(a2b[s][0:rows, :], mod_vec(4, rows, s)).then_inc(mb_in, 16)
            sp.wait_ge(w_used, U_YA + 8)
            sp.dma_start(gn2b, a["g_norm2"].to_broadcast([P, D])).then_inc(mb2_in, 16)
            for s, rows in ((0, P), (1, NSAMPLE)):
                sp.dma_start(sh2b[s][0:rows, :], mod_vec(3, rows, s)).then_inc(mb2_in, 16)
            sp.wait_ge(a_ready, 2 * KT)
            sp.wait_ge(hist_ps, 2)

            def load_gu(i, t, b, e=None):
                e = col(i, t - 1) if e is None else e
                if t >= 3:
                    sp.wait_ge(gu_done, cnt(i, t, 1, -2))
                    sp.sem_inc(loads_begun)
                sp.dma_start(WG[b].rearrange("p k n -> p (k n)"), w_gate[e].rearrange("o p n -> (o p) n")).then_inc(gu_full[b], 16)
                sp.dma_start(WU[b].rearrange("p k n -> p (k n)"), w_up[e].rearrange("o p n -> (o p) n")).then_inc(gu_full[b], 16)

            def load_d(i, t, b, e=None):
                e = col(i, t - 1) if e is None else e
                if t >= 3:
                    sp.wait_ge(down_done, cnt(i, t, 1, -2))
                    sp.sem_inc(loads_begun)
                sp.dma_start(WD[b], w_down[e].rearrange("o p k n -> (o p) k n")).then_inc(wd_full[b], 16)

            def owner(i, t):
                e = sp.value_load(over_expert[0:1, col(i, t - 1 - NE)], min_val=0, max_val=NE - 1)
                return ds(e, 1)

            load_gu(None, 1, 0)
            load_gu(None, 2, 1)
            load_d(None, 1, 0)
            for t in (3, 4):
                load_gu(None, t, (t + 1) % 2)
                load_d(None, t - 1, t % 2)

            def own(i, t, b):
                load_gu(i, t, b)
                load_d(i, t - 1, 1 - b)

            def over(i, t, b):
                load_gu(i, t, b, owner(i, t))
                load_d(i, t - 1, 1 - b, owner(i, t - 1))

            tiles(sp, 5, NE, own)
            sp.wait_ge(routed, 1)
            load_gu(None, NE + 1, 0, owner(None, NE + 1))
            load_d(None, NE, 1)
            over(None, NE + 2, 1)
            load_d(None, ALWAYS, 1, owner(None, ALWAYS))
            sp.dma_start(gfb, a["g_final"].rearrange("(o n) -> o n", o=1).to_broadcast([P, D])).then_inc(fin_in, 16)
            for s, rows in ((0, P), (1, NSAMPLE)):
                for n, dst in ((5, g2b), (6, shfb), (7, afb)):
                    sp.dma_start(dst[s][0:rows, :], mod_vec(n, rows, s)).then_inc(fin_in, 16)
            with some_overflow(sp):
                load_gu(None, ALWAYS + 1, 0, owner(None, ALWAYS + 1))
                tiles(sp, ALWAYS + 2, TILES - 1, over)
                over(None, TILES, 1)
                load_d(None, TILES, 1, owner(None, TILES))
            sp.wait_ge(experts_done, 1)
            for t in range(TT):
                for k in range(2):
                    sp.dma_start(pair_rows[k][0:WIDTH[t], t, :], pairs[k * T + t * P:k * T + t * P + WIDTH[t], :]).then_inc(pair_in[t], 16)
            for t in range(TT):
                sp.wait_ge(f_out, t + 1)
                sp.dma_start(y_out[t * P:t * P + WIDTH[t], :], pair_rows[0][0:WIDTH[t], t, :]).then_inc(f_stored, 16)
            sp.wait_ge(f_stored, 16 * TT)
            sp.wait_ge(hist_stored, 32)
            sp.wait_ge(v_stored, 16)

        @block.tensor
        def _(pe):
            def product(bank, tile_w, act):
                for k in range(KT):
                    for h in range(2):
                        last = pe.matmul(PS[:, bank + h, 0:H], tile_w[:, k, :], act[:, k, h * H:(h + 1) * H],
                                         start=(k == 0), stop=(k == KT - 1))
                return last

            def ada(b):
                for k in range(KT):
                    last = pe.matmul(PS[0:2, 4 * b, :], cT[:, :, k], W[b][:, k, :], start=(k == 0), stop=(k == KT - 1))
                return last

            pe.wait_ge(consts, NCONST)
            pe.wait_ge(c_silu, 1)
            pe.transpose(PS[:, 0, 0:16], c16[:, :], ident[0:16, 0:16]).then_inc(start_ps, 1)
            pe.wait_ge(vec_in, 16 * 7)
            pe.transpose(PS[:, 1, 0:128], VR[:, 0, :], ident[:, :])
            pe.transpose(PS[:, 1, 128:256], VR[:, 1, :], ident[:, :])
            pe.transpose(PS[:, 1, 256:328], VR[0:72, 2, :], ident[0:72, 0:72]).then_inc(start_ps, 1)
            pe.wait_ge(cache_in, 16)
            for j in range(KT):
                last = pe.transpose(PS[:, 2, j * HIST:(j + 1) * HIST], cacheR[0:HIST, j * P:(j + 1) * P], ident[0:HIST, 0:HIST])
            last.then_inc(start_ps, 1)
            pe.wait_ge(ws_masked, KT)
            for h in range(KT):
                last = pe.transpose(PS[:, 4 + h // 4, (h % 4) * P:(h % 4 + 1) * P], wsR[:, h, :], ident[:, :])
            last.then_inc(start_ps, 1)
            for t in range(TT):
                w = WIDTH[t]
                bank = 6 if t % 2 == 0 else 2
                if t >= 1:
                    pe.wait_ge(start_dr, t + 3)
                pe.wait_ge(xn_ready, t + 1)
                for j in range(KT):
                    last = pe.transpose(PS[:, bank + j // 4, (j % 4) * P:(j % 4) * P + w],
                                        xn[0:w, t % 2, j * P:(j + 1) * P], ident[0:w, 0:w])
                last.then_inc(start_ps, 1)
            pe.wait_ge(start_dr, 4)
            for n in range(4):
                full(pe, n)
                if n >= 2:
                    pe.wait_ge(act_drained, n - 1)
                ada(n % 2).then_inc(w_used, 1)
            pe.wait_ge(modr_in, 32)
            pe.transpose(PS[:, 1, 0:32], VR[0:32, 3, :], ident[0:32, 0:32]).then_inc(start_ps, 1)
            pe.wait_ge(h_ready, 2 * KT)

            def pair_products(base, q0, left_act, right_act):
                with pe.Fori(0, 8 // 2) as half:
                    i = half * 2
                    for b in range(2):
                        pe.wait_ge(w_full[b], i * 16 + 32 * (base // 2 + 1))
                        pe.wait_ge(act_drained, i + (q0 + b - 1))
                        if base >= U_YB:
                            pe.wait_ge(dve_drained, i + (base - U_YB + 9 + b))
                        product(4 * b, WP[b][:, 0], left_act)
                        product(4 * b + 2, WP[b][:, 1], right_act).then_inc(w_used, 1)

            pair_products(U_A, Q_A, hT, hT)
            with pe.Fori(0, 4 // 2) as half:
                i = half * 2
                for b in range(2):
                    pe.wait_ge(w_full[b], i * 16 + 32 * (U_U // 2 + 1))
                    pe.wait_ge(act_drained, i + (Q_U + b - 1))
                    for m in range(2):
                        last = product(4 * b + 2 * m, WP[b][:, m], hT)
                    last.then_inc(w_used, 1)

            def histories(first):
                for j in range(KT):
                    last = pe.transpose(PS[0:HIST, 6 + j // 4, (j % 4) * P:(j % 4 + 1) * P], aF[:, j, first:first + HIST], ident[:, :])
                last.then_inc(hist_ps, 1)

            pe.wait_ge(act_drained, Q_U + 4)
            pe.wait_ge(aF_written, 4 + 2 * KT)
            pe.wait_ge(start_dr, 3)
            histories(NPROMPT)
            full(pe, U_V)
            full(pe, U_V + 1)
            for t in range(TT):
                for hf in range(2):
                    g = 2 * t + hf
                    if g >= 6:
                        pe.wait_ge(v_biased, g - 5)
                    for k in range(KT):
                        last = pe.matmul(PS[0:WIDTH[t], g % 6, :], hT[:, k, t * P:t * P + WIDTH[t]], W[hf][:, k, :],
                                         start=(k == 0), stop=(k == KT - 1))
                    if g < 2 * TT - 1:
                        last.then_inc(v_ps, 1)
            last.then_inc(w_used, 2)
            pe.wait_ge(hist_copied, 1)
            histories(FULL - HIST)
            pe.wait_ge(v_norm, TT)
            for h in range(KT):
                b = h % 2
                if h >= 2:
                    pe.wait_ge(dve_drained, h - 1)
                for t in range(4):
                    pe.matmul(PS[:, 2 * b, t * P:(t + 1) * P], v[:, t, h * P:(h + 1) * P], wsT[:, h, :], start=True, stop=True)
                pe.matmul(PS[:, 2 * b + 1, 0:NSAMPLE], v[0:NSAMPLE, 4, h * P:(h + 1) * P],
                          wsT[0:NSAMPLE, h, 0:NSAMPLE], start=True, stop=True).then_inc(mix_ps, 1)

            def over_features(bank, src):
                for j in range(KT):
                    for h in range(2):
                        last = pe.matmul(PS[:, bank + h, 0:CH], meanm[:, :], src[:, j, h * CH:(h + 1) * CH],
                                         start=(j == 0), stop=(j == KT - 1))
                last.then_inc(stat_ps, 1)

            pe.wait_ge(conv_step, TAPS * KT)
            pe.wait_ge(hist_copied, 2)
            over_features(6, cv)
            pe.wait_ge(dve_drained, KT)
            with pe.Fori(0, 12 // 2) as half:
                i = half * 2
                for b in range(2):
                    pe.wait_ge(w_full[b], i * 16 + 32 * (U_ADA2 // 2 + 1))
                    pe.wait_ge(act_drained, i + (Q_ADA2 + b - 1))
                    ada(b).then_inc(w_used, 1)
            pe.wait_ge(squared, KT)
            pe.wait_ge(act_drained, Q_YB)
            over_features(4, sq)
            pair_products(U_YB, Q_YB, hT, uT)
            pe.wait_ge(a_ready, 2 * KT)
            pair_products(U_YA, Q_YA, hT, aT)
            full(pe, U_O)
            full(pe, U_O + 1)
            pe.wait_ge(merged, 2 * KT)
            pe.wait_ge(act_drained, Q_YA + 8)

            def project(t):
                if t == 3:
                    pe.wait_ge(h2_copied, 1)
                if t == 4:
                    pe.wait_ge(o_drained, 2)
                for hf in range(2):
                    for k in range(KT):
                        last = pe.matmul(PS[0:WIDTH[t], (2 * t + hf) % 8, :], mT[:, k, t * P:t * P + WIDTH[t]], W[hf][:, k, :],
                                         start=(k == 0), stop=(k == KT - 1))
                    if t < 4 or hf == 0:
                        last.then_inc(o_ps, 1)
                    else:
                        last.then_inc(w_used, 2)

            def turn_h2(t):
                bank = H2_BANK[t]
                pe.wait_ge(h2_ready, t + 1)
                if t == 4:
                    pe.wait_ge(h2_copied, 2)
                for j in range(KT):
                    last = pe.transpose(PS[:, bank + j // 4, (j % 4) * P:(j % 4) * P + WIDTH[t]],
                                        h2[0:WIDTH[t], t % 2, j * P:(j + 1) * P], ident[0:WIDTH[t], 0:WIDTH[t]])
                last.then_inc(h2_ps, 1)

            project(0)
            for t in range(1, TT):
                project(t)
                turn_h2(t - 1)
            turn_h2(TT - 1)
            pe.wait_ge(rt_in, 64)
            pe.wait_ge(h2_copied, TT)
            for t in range(TT):
                for k in range(KT):
                    last = pe.matmul(PS[0:WIDTH[t], 0, t * NLOG:(t + 1) * NLOG], h2T[:, k, t * P:t * P + WIDTH[t]], wr[:, k, :],
                                     start=(k == 0), stop=(k == KT - 1))
            last.then_inc(log_ps, 1)
            pe.wait_ge(oh_ready, 1)
            for t in range(TT):
                for s in range(t + 1):
                    pe.matmul(PS[:, 1, t * NE:(t + 1) * NE], before[:, :] if s == t else ones[:, :], OHs[:, s, :],
                              start=(s == 0), stop=(s == t))
            for s in range(TT):
                last = pe.matmul(PS[:, 1, TT * NE:(TT + 1) * NE], ones[:, :], OHs[:, s, :], start=(s == 0), stop=(s == TT - 1))
            last.then_inc(rank_ps, 1)
            pe.wait_ge(tab_ready, 1)
            for n in range(2 * TT):
                last = pe.matmul(PS[0:SLOTS, 2, 0:3 * TILES], FOH[:, n, :], R[:, n, :], start=(n == 0), stop=(n == 2 * TT - 1))
            last.then_inc(tab_ps, 1)

            def turn_rows(i, t, b):
                pe.wait_ge(gathered[b], cnt(i, t, 8, 8 * (1 - b)))
                pe.sem_inc(turns_begun)
                if t >= 2:
                    pe.wait_ge(hg_ready, cnt(i, t, 2, -2))
                    pe.sem_inc(turns_begun)
                for k in range(KT):
                    last = pe.transpose(PS[:, k // 4, (k % 4) * SLOTS:(k % 4 + 1) * SLOTS], G[:, b, k::KT], ident[:, :])
                last.then_inc(t_ps, 1)

            def gate_up(i, t, b):
                pe.wait_ge(gu_full[b], cnt(i, t, 16, 16 * (1 - b)))
                pe.wait_ge(hg_ready, cnt(i, t, 2))
                for n, w in enumerate((WG[b], WU[b])):
                    for k in range(KT):
                        last = pe.matmul(PS[:, 2, n * DE:(n + 1) * DE], hG[:, b, k * SLOTS:(k + 1) * SLOTS], w[:, k, :],
                                         start=(k == 0), stop=(k == KT - 1))
                last.then_inc(gu_done, 1)

            def turn_hidden(i, t):
                pe.wait_ge(he_ready, cnt(i, t))
                pe.sem_inc(turns_begun)
                for k in range(2):
                    last = pe.transpose(PS[:, 3, k * SLOTS:(k + 1) * SLOTS], he[:, k * P:(k + 1) * P], ident[:, :])
                last.then_inc(he_ps, 1)

            def down(i, t, b):
                pe.wait_ge(wd_full[b], cnt(i, t, 8, 8 * (1 - b)))
                pe.wait_ge(het_ready, cnt(i, t))
                for hf in range(2):
                    for k in range(2):
                        last = pe.matmul(PS[:, 4 + 2 * b + hf, :], heT[:, k, :], WD[b][:, k, hf * 512:(hf + 1) * 512],
                                         start=(k == 0), stop=(k == 1))
                last.then_inc(down_done, 1)

            def expert_tile(i, t, b):
                gate_up(i, t, b)
                turn_rows(i, t + 1, 1 - b)
                down(i, t - 1, 1 - b)
                turn_hidden(i, t)

            def expert_tiles(first, last):
                turn_rows(None, first, 0)
                gate_up(None, first, 0)
                turn_rows(None, first + 1, 1)
                turn_hidden(None, first)
                tiles(pe, first + 1, last - 1, expert_tile)
                gate_up(None, last, 1)
                down(None, last - 1, 0)
                turn_hidden(None, last)
                down(None, last, 1)

            pe.wait_ge(routed, 1)
            expert_tiles(1, ALWAYS)
            with some_overflow(pe):
                expert_tiles(ALWAYS + 1, TILES)
        @block.scalar
        def _(act):
            act.dma_start(c16[0:8, :], a["c_prompt"].rearrange("o (k p) -> (o k) p", p=P)).then_inc(c_in, 16)
            act.dma_start(c16[8:16, :], a["c_sample"].rearrange("o (k p) -> (o k) p", p=P)).then_inc(c_in, 16)
            for t in range(4):
                act.dma_start(x[:, t, :], a["x_prompt"][0, t * P:(t + 1) * P, :]).then_inc(x_in, 16)
            act.dma_start(x[0:NSAMPLE, 4, :], a["x_sample"][0]).then_inc(x_in, 16)
            taps = a["conv_w"][0].rearrange("t (j p) -> (t j) p", p=P)
            act.dma_start(VR[:, 0, :], taps[0:P, :]).then_inc(vec_in, 16)
            act.dma_start(VR[0:TAPS * KT - P, 1, :], taps[P:TAPS * KT, :]).then_inc(vec_in, 16)

            def rows(name):
                return a[name].rearrange("o (j p) -> (o j) p", p=P)

            act.dma_start(VR[TAPS * KT - P:P, 1, :], rows("conv_b")).then_inc(vec_in, 16)
            act.dma_start(VR[0:48, 2, :], rows("b_in")).then_inc(vec_in, 16)
            act.dma_start(VR[48:56, 2, :], rows("ln_g")).then_inc(vec_in, 16)
            act.dma_start(VR[56:64, 2, :], rows("ln_b")).then_inc(vec_in, 16)
            act.dma_start(VR[64:72, 2, :], rows("g_norm1")).then_inc(vec_in, 16)
            act.dma_start(cacheR[0:HIST, :], a["cache_conv"][0, 0]).then_inc(cache_in, 16)
            act.dma_start(wsR, a["w_s"][0].rearrange("h t s -> t h s")).then_inc(ws_in, 16)
            act.dma_start(vecs[:, 0:D], a["b_s"].rearrange("o h t -> o (h t)").to_broadcast([P, D])).then_inc(bc_in, 16)
            act.dma_start(bvb, a["b_in"][:, 3 * D:4 * D].to_broadcast([P, D])).then_inc(bc_in, 16)
            act.dma_start(vgb, a["v_ln_g"].to_broadcast([P, D])).then_inc(bc_in, 16)
            act.dma_start(vbb, a["v_ln_b"].to_broadcast([P, D])).then_inc(bc_in, 16)
            act.dma_start(wr[:, :, 0:NG], a["w_rg"][0].rearrange("(k p) n -> p k n", p=P)).then_inc(rt_in, 16)
            act.dma_start(wr[:, :, NG:NLOG], a["w_re"][0].rearrange("(k p) n -> p k n", p=P)).then_inc(rt_in, 16)
            act.dma_start(brb[:, 0:NG], a["b_rg"].to_broadcast([P, NG])).then_inc(rt_in, 16)
            act.dma_start(brb[:, NG:NLOG], a["b_re"].to_broadcast([P, NE])).then_inc(rt_in, 16)

            act.wait_ge(c_in, 32)
            act.activation(c16[:, :], c16[:, :], ACT.Silu).then_inc(c_silu, 1)
            act.wait_ge(x_in, 16 * TT)
            act.wait_ge(consts, NCONST)
            for t in range(TT):
                if t:
                    act.wait_ge(x_sq, t)
                act.activation(mg[0:WIDTH[t], :], x[0:WIDTH[t], t, :], ACT.Square, accum_out=ss[0:WIDTH[t], t:t + 1]).then_inc(x_sq, 1)
            act.wait_ge(x_sq, TT)
            act.activation(sd[:, 0:TT], ss[:, 0:TT], ACT.Sqrt, bias=eps[:, :], scale=1.0 / D).then_inc(x_sd, 1)
            for n in range(4):
                act.wait_ge(w_used, n + 1)
                if n >= 2:
                    act.wait_ge(mod_stored[n % 2], 16)
                act.activation(mrow[:, n % 2, :], PS[0:2, 4 * (n % 2), :], ACT.Copy).then_inc(act_drained, 1)
            for b in range(2):
                act.wait_ge(mod_stored[b], 32)
            for s in range(2):
                act.dma_start(VR[16 * s:16 * s + 16, 3, :], mod[s:s + 1, 0:2 * D].rearrange("o (j p) -> (o j) p", p=P)).then_inc(modr_in, 16)

            def two(ap):
                return ap.rearrange("p (h t) -> p h t", h=2)

            def tile_of(buf, j, c0, n):
                return buf[:, ds(j, 1), c0:c0 + n].rearrange("p o t -> p (o t)")

            with act.Fori(0, KT // 2) as half:
                i = half * 2
                for b in range(2):
                    act.wait_ge(w_used, i + (U_A + b + 1))
                    act.wait_ge(aF_written, i * 2 + (2 + 2 * b))
                    act.activation(two(tmp[:, b, 0:T]), PS[:, 4 * b:4 * b + 2, 0:H], ACT.Identity, bias=VT[:, ds(i + (COL_BIN + b), 1)])
                    act.activation(two(tmp[:, 2 + b, 0:T]), PS[:, 4 * b + 2:4 * b + 4, 0:H], ACT.Sigmoid,
                                   bias=VT[:, ds(i + (COL_BIN + KT + b), 1)]).then_inc(act_drained, 1)
            for n in range(4):
                b = n % 2
                act.wait_ge(w_used, U_U + n + 1)
                for m in range(2):
                    j = 2 * n + m
                    last = act.activation(two(uT[:, j, :]), PS[:, 4 * b + 2 * m:4 * b + 2 * m + 2, 0:H], ACT.Gelu_apprx_tanh,
                                          bias=VT[:, COL_BIN + 2 * KT + j:COL_BIN + 2 * KT + j + 1])
                last.then_inc(act_drained, 1)

            def store_history(n, dst):
                act.wait_ge(hist_ps, n + 1)
                act.activation(histR[0:HIST, n, :], PS[0:HIST, 6:8, :].rearrange("p b c -> p (b c)"), ACT.Copy).then_inc(hist_copied, 1)
                act.wait_ge(hist_copied, n + 1)
                act.dma_start(dst, histR[0:HIST, n, :]).then_inc(hist_stored, 16)

            def v_deviation(t):
                act.wait_ge(v_var, t + 1)
                dev_col = vsd[0:WIDTH[t], t:t + 1]
                act.activation(dev_col, dev_col, ACT.Sqrt, bias=eps[0:WIDTH[t], :]).then_inc(v_sd, 1)

            store_history(0, hist_p_out)
            for t in range(TT):
                for hf in range(2):
                    act.wait_ge(v_biased, 2 * t + hf + 1)
                    vh = v[0:WIDTH[t], t, hf * 512:(hf + 1) * 512]
                    act.activation(vh, vh, ACT.Gelu_apprx_tanh).then_inc(v_gelu, 1)
                if t:
                    v_deviation(t - 1)
            v_deviation(TT - 1)
            store_history(1, hist_s_out)
            with act.Fori(0, 12 // 2) as half:
                i = half * 2
                for b in range(2):
                    act.wait_ge(w_used, i + (U_ADA2 + b + 1))
                    act.wait_ge(mod_stored[b], i * 8 + 32)
                    act.activation(mrow[:, b, :], PS[0:2, 4 * b, :], ACT.Copy).then_inc(act_drained, 1)
            act.wait_ge(stat_ps, 2)
            act.activation(two(rstdc[:, :]), PS[:, 4:6, 0:CH], ACT.Sqrt, bias=eps[:, :]).then_inc(c_std, 1)
            act.wait_ge(hist_stored, 32)
            with act.Fori(0, KT) as j:
                act.wait_ge(c_normed, j + 1)
                for at, n, first in ((0, NPROMPT, 0), (NPROMPT, NSAMPLE, SAMPLE0)):
                    act.activation(tile_of(aT, j, at, n), tile_of(cv, j, first, n), ACT.Silu,
                                   bias=VT[:, ds(j + COL_LB, 1)], scale=VT[:, ds(j + COL_LG, 1)]).then_inc(a_ready, 1)
            for base, q0, gate_col in ((U_YB, Q_YB, 5 * KT), (U_YA, Q_YA, 4 * KT)):
                with act.Fori(0, KT // 2) as half:
                    i = half * 2
                    for b in range(2):
                        act.wait_ge(w_used, i + (base + b + 1))
                        act.wait_ge(dve_drained, i + (base - U_YB + 9 + b))
                        act.activation(two(tmp[:, b, 0:T]), PS[:, 4 * b:4 * b + 2, 0:H], ACT.Sigmoid,
                                       bias=VT[:, ds(i + (COL_BIN + gate_col + b), 1)]).then_inc(act_drained, 1)

            def copy_h2(t):
                w = WIDTH[t]
                act.wait_ge(h2_ps, t + 1)
                act.activation(h2T[:, :, t * P:t * P + w],
                               PS[:, H2_BANK[t]:H2_BANK[t] + 2, :].rearrange("p b (j c) -> p (b j) c", c=P)[:, :, 0:w],
                               ACT.Copy).then_inc(h2_copied, 1)

            def deviation(t, done, summed, signal, scratch):
                w = WIDTH[t]
                act.wait_ge(summed, t + 1)
                act.activation(scratch[0:w, :], x[0:w, t, :], ACT.Square, accum_out=ss[0:w, t:t + 1]).then_inc(act_step, 1)
                act.wait_ge(act_step, done + t + 1)
                act.activation(sd[0:w, t:t + 1], ss[0:w, t:t + 1], ACT.Sqrt, bias=eps[0:w, :], scale=1.0 / D).then_inc(signal, 1)

            for t in range(TT):
                deviation(t, 0, x1_ready, x1_sd, sqj)
                if t:
                    copy_h2(t - 1)
                act.wait_ge(h2_ready, t + 1)
                act.dma_start(h2d[t * P:t * P + WIDTH[t], :], h2[0:WIDTH[t], t % 2, :]).then_inc(h2_stored[t % 2], 16)
            copy_h2(TT - 1)
            act.wait_ge(log_ready, 1)
            act.activation(exps, diffs, ACT.Exp).then_inc(e_ready, 1)
            def take_rows(i, t, b):
                act.wait_ge(t_ps, cnt(i, t))
                act.activation(hG[:, b, 0:512], PS[:, 0, :], ACT.Copy).then_inc(hg_ready, 1)

            def swish_gate(i, t):
                act.wait_ge(gu_done, cnt(i, t))
                act.activation(sil, PS[:, 2, 0:DE], ACT.Silu).then_inc(sil_ready, 1)

            def weigh(i, t, b):
                act.wait_ge(down_done, cnt(i, t))
                if t >= 3:
                    act.wait_ge(scattered[b], cnt(i, t, 8, -8 * (1 + b)))
                act.activation(Y[:, b, 0:512], PS[:, 4 + 2 * b, :], ACT.Copy, scale=wslot[:, col(i, t - 1)]).then_inc(y_act, 1)

            def expert_tile(i, t, b):
                swish_gate(i, t)
                take_rows(i, t + 1, 1 - b)
                weigh(i, t - 1, 1 - b)

            def expert_tiles(first, last, peeled):
                take_rows(None, first, 0)
                swish_gate(None, first)
                take_rows(None, first + 1, 1)
                for t in range(first + 1, first + 1 + peeled):
                    expert_tile(None, t, (t + 1) % 2)
                tiles(act, first + 1 + peeled, last - 1, expert_tile)
                swish_gate(None, last)
                weigh(None, last - 1, 0)
                weigh(None, last, 1)

            act.wait_ge(routed, 1)
            expert_tiles(1, ALWAYS, 2)
            with some_overflow(act):
                expert_tiles(ALWAYS + 1, TILES, 0)
            for t in range(TT):
                deviation(t, TT, f_sum, f_sd, sqj)

        @block.vector
        def _(dve):
            steps_done = [0]

            def then(ins):
                steps_done[0] += 1
                ins.then_inc(dve_step, 1)
                dve.wait_ge(dve_step, steps_done[0])

            def rows_of(banks, w):
                return banks.rearrange("p b (j c) -> p (b j) c", c=P)[:, :, 0:w]

            def two(ap):
                return ap.rearrange("p (h t) -> p h t", h=2)

            dve.wait_ge(consts, NCONST)
            then(dve.tensor_copy(iota[:, :], iotaI[:, :]))
            then(dve.tensor_copy(tokid[:, :], tokidI[:, :]))
            dve.wait_ge(start_ps, 1)
            dve.tensor_copy(cT.rearrange("p s k -> p (s k)"), PS[:, 0, 0:16]).then_inc(start_dr, 1)
            dve.wait_ge(start_ps, 2)
            dve.tensor_copy(VT[:, 0:328], PS[:, 1, 0:328]).then_inc(start_dr, 1)
            dve.wait_ge(start_ps, 3)
            dve.tensor_copy(aF[:, :, HIST + NPROMPT:2 * HIST + NPROMPT],
                            PS[:, 2, 0:KT * HIST].rearrange("p (j c) -> p j c", c=HIST)).then_inc(start_dr, 1)
            dve.wait_ge(start_ps, 4)
            dve.tensor_copy(wsT[:, :, :].rearrange("p h t -> p (h t)"), PS[:, 4:6, :].rearrange("p b c -> p (b c)")).then_inc(start_dr, 1)
            dve.wait_ge(x_sd, 1)
            then(dve.reciprocal(rs[:, 0:TT], sd[:, 0:TT]))
            for t in range(TT):
                w = WIDTH[t]
                bank = 6 if t % 2 == 0 else 2
                dve.tensor_scalar(xn[0:w, t % 2, :], x[0:w, t, :], rs[0:w, t:t + 1], None, ALU.mult).then_inc(xn_ready, 1)
                dve.wait_ge(start_ps, 5 + t)
                dve.tensor_copy(hT[:, :, t * P:t * P + w], rows_of(PS[:, bank:bank + 2, :], w)).then_inc(start_dr, 1)
            dve.wait_ge(start_ps, 5 + TT)
            then(dve.tensor_copy(VT[:, COL_MOD:COL_MOD + 32], PS[:, 1, 0:32]))
            for s in range(2):
                c0 = COL_MOD + 16 * s
                then(dve.scalar_tensor_tensor(out=S1[:, s, :], in0=VT[:, c0 + KT:c0 + 2 * KT], scalar=1.0,
                                              in1=VT[:, COL_G1:COL_G1 + KT], op0=ALU.add, op1=ALU.mult))
            dve.wait_ge(start_dr, 4 + TT)
            for j in range(KT):
                for s, (c0, c1) in enumerate(((0, NPROMPT), (NPROMPT, T))):
                    dve.tensor_scalar(hT[:, j, c0:c1], hT[:, j, c0:c1], S1[:, s, j:j + 1],
                                      VT[:, COL_MOD + 16 * s + j:COL_MOD + 16 * s + j + 1], ALU.mult, ALU.add).then_inc(h_ready, 1)

            def tile_of(buf, j, c0, n):
                return buf[:, ds(j, 1), c0:c0 + n].rearrange("p o t -> p (o t)")

            with dve.Fori(0, KT // 2) as half:
                i = half * 2
                dve.wait_ge(aF_written, i * 2 + 8)
                for k in range(TAPS):
                    for b in range(2):
                        acc, src = tile_of(cv, i + b, 0, CONV), tile_of(aF, i + b, k, CONV)
                        tap = VT[:, ds(i + (k * KT + b), 1)]
                        if k == 0:
                            dve.tensor_scalar(acc, src, tap, VT[:, ds(i + (COL_CB + b), 1)], ALU.mult, ALU.add).then_inc(conv_step, 1)
                        else:
                            dve.wait_ge(conv_step, i * TAPS + (2 * (k - 1) + b + 1))
                            dve.scalar_tensor_tensor(out=acc, in0=src, scalar=tap, in1=acc, op0=ALU.mult, op1=ALU.add).then_inc(conv_step, 1)

            def normalise_v(t):
                w = WIDTH[t]
                vt = v[0:w, t, :]
                dve.wait_ge(v_gelu, 2 * t + 2)
                for hf in range(2):
                    then(dve.bn_stats(bn[0:w, hf, :], v[0:w, t, hf * 512:(hf + 1) * 512]))
                then(dve.bn_aggr(mv[0:w, :], bn[0:w, :, :].rearrange("p a b -> p (a b)")))
                dve.tensor_copy(vsd[0:w, t:t + 1], mv[0:w, 1:2]).then_inc(v_var, 1)
                dve.wait_ge(v_sd, t + 1)
                then(dve.reciprocal(vsd[0:w, t:t + 1], vsd[0:w, t:t + 1]))
                then(dve.tensor_scalar(vt, vt, mv[0:w, 0:1], vsd[0:w, t:t + 1], ALU.subtract, ALU.mult))
                then(dve.tensor_tensor(vt, vt, vgb[0:w, :], ALU.mult))
                dve.tensor_tensor(vt, vt, vbb[0:w, :], ALU.add).then_inc(v_norm, 1)

            dve.wait_ge(bc_in, 64)
            for t in range(TT):
                w = WIDTH[t]
                for hf in range(2):
                    g = 2 * t + hf
                    if g < 2 * TT - 1:
                        dve.wait_ge(v_ps, g + 1)
                    else:
                        dve.wait_ge(w_used, U_V + 2)
                    cols = slice(hf * 512, (hf + 1) * 512)
                    dve.tensor_tensor(v[0:w, t, cols], PS[0:w, g % 6, :], bvb[0:w, cols], ALU.add).then_inc(v_biased, 1)
                if t:
                    normalise_v(t - 1)
            normalise_v(TT - 1)
            for h in range(KT):
                b = h % 2
                dve.wait_ge(mix_ps, h + 1)
                if h >= 2:
                    dve.wait_ge(gated, h - 1)
                dve.tensor_tensor(tmp[:, b, 0:NPROMPT].rearrange("p (c t) -> p c t", t=P),
                                  PS[:, 2 * b, :].rearrange("p (c t) -> p c t", t=P),
                                  bsb[:, h:h + 1, :].to_broadcast([P, 4, P]), ALU.add).then_inc(mix_added, 1)
                dve.tensor_tensor(tmp[:, b, NPROMPT:T], PS[:, 2 * b + 1, 0:NSAMPLE], bsb[:, h, 0:NSAMPLE], ALU.add).then_inc(dve_drained, 1)
                dve.wait_ge(mix_added, h + 1)
                dve.wait_ge(dve_drained, h + 1)
                dve.tensor_tensor(uT[:, h, :], uT[:, h, :], tmp[:, b, 0:T], ALU.mult).then_inc(gated, 1)
            dve.wait_ge(stat_ps, 1)
            for j in range(KT):
                dve.tensor_tensor(two(cv[:, j, :]), two(cv[:, j, :]), PS[:, 6:8, 0:CH], ALU.subtract).then_inc(centred, 1)
            dve.wait_ge(centred, KT)
            dve.wait_ge(c_std, 1)
            dve.reciprocal(rstdc[:, :], rstdc[:, :]).then_inc(dve_drained, 2)
            dve.wait_ge(dve_drained, KT + 2)
            dve.wait_ge(squared, KT)
            for j in range(KT):
                dve.tensor_tensor(cv[:, j, :], cv[:, j, :], rstdc[:, :], ALU.mult).then_inc(c_normed, 1)
            with dve.Fori(0, KT // 2) as half:
                i = half * 2
                for b in range(2):
                    m_j = mT[:, ds(i + b, 1), :].rearrange("p o (h t) -> p (o h) t", h=2)
                    dve.wait_ge(act_drained, i + (Q_YB + b + 1))
                    dve.tensor_tensor(m_j, PS[:, 4 * b + 2:4 * b + 4, 0:H], two(tmp[:, b, 0:T]), ALU.mult).then_inc(dve_drained, 1)
            with dve.Fori(0, KT // 2) as half:
                i = half * 2
                for b in range(2):
                    m_j = mT[:, ds(i + b, 1), :].rearrange("p o (h t) -> p (o h) t", h=2)
                    dve.wait_ge(act_drained, i + (Q_YA + b + 1))
                    dve.tensor_tensor(two(tmp[:, 2 + b, 0:T]), PS[:, 4 * b + 2:4 * b + 4, 0:H], two(tmp[:, b, 0:T]), ALU.mult).then_inc(dve_drained, 1)
                    dve.wait_ge(dve_drained, i + (10 + KT + b + 1))
                    dve.tensor_tensor(m_j, m_j, two(tmp[:, 2 + b, 0:T]), ALU.add).then_inc(merged, 2)
            dve.wait_ge(mb_in, 64)
            dve.wait_ge(mb2_in, 48)
            for s, rows in ((0, P), (1, NSAMPLE)):
                then(dve.scalar_tensor_tensor(out=a2b[s][0:rows, :], in0=a2b[s][0:rows, :], scalar=1.0, in1=gn2b[0:rows, :],
                                              op0=ALU.add, op1=ALU.mult))
            for t in range(TT):
                w, s = WIDTH[t], t // 4
                for hf in range(2):
                    if t < 4 or hf == 0:
                        dve.wait_ge(o_ps, 2 * t + hf + 1)
                    else:
                        dve.wait_ge(w_used, U_O + 2)
                    cols = slice(hf * 512, (hf + 1) * 512)
                    dve.tensor_tensor(mg[0:w, cols], PS[0:w, (2 * t + hf) % 8, :], g1b[s][0:w, cols], ALU.mult).then_inc(o_drained, 1)
                dve.wait_ge(o_drained, 2 * t + 2)
                dve.tensor_tensor(x[0:w, t, :], x[0:w, t, :], mg[0:w, :], ALU.add).then_inc(x1_ready, 1)
                dve.wait_ge(x1_ready, t + 1)
                dve.wait_ge(x1_sd, t + 1)
                then(dve.reciprocal(rs[0:w, t:t + 1], sd[0:w, t:t + 1]))
                if t >= 2:
                    dve.wait_ge(h2_ps, t - 1)
                    dve.wait_ge(h2_stored[t % 2], 16 * (t // 2))
                then(dve.scalar_tensor_tensor(out=h2[0:w, t % 2, :], in0=x[0:w, t, :], scalar=rs[0:w, t:t + 1], in1=a2b[s][0:w, :],
                                              op0=ALU.mult, op1=ALU.mult))
                dve.tensor_tensor(h2[0:w, t % 2, :], h2[0:w, t % 2, :], sh2b[s][0:w, :], ALU.add).then_inc(h2_ready, 1)

            def wide(ap, *shape):
                return ap.to_broadcast(list(shape))

            def first_one(out, logits, n, best):
                then(dve.tensor_reduce(best, logits, AX, ALU.max))
                then(dve.tensor_tensor(scr[:, :, 0:n], logits, wide(best.unsqueeze(2), P, TT, n), ALU.is_equal))
                then(dve.tensor_tensor(scr[:, :, 0:n], scr[:, :, 0:n], wide(rev[:, 0:1, EPG - n:EPG], P, TT, n), ALU.mult))
                then(dve.tensor_reduce(mx[:, 3, :], scr[:, :, 0:n], AX, ALU.max))
                then(dve.tensor_tensor(out, scr[:, :, 0:n], wide(mx[:, 3, :].unsqueeze(2), P, TT, n), ALU.is_equal))

            then(dve.tensor_scalar(rev[:, 0, :], iota[:, 0:EPG], -1.0, float(EPG), ALU.mult, ALU.add))
            then(dve.memset(lg, 0.0))
            dve.wait_ge(log_ps, 1)
            then(dve.tensor_tensor(lg[:, 0:4, :], PS[:, 0, 0:4 * NLOG].rearrange("p (t n) -> p t n", n=NLOG),
                                   wide(brb[:, :].unsqueeze(1), P, 4, NLOG), ALU.add))
            then(dve.tensor_tensor(lg[0:NSAMPLE, 4, :], PS[0:NSAMPLE, 0, 4 * NLOG:5 * NLOG], brb[0:NSAMPLE, :], ALU.add))
            groups = lg[:, :, 0:NG]
            first_one(one_g, groups, NG, mx[:, 0, :])
            then(dve.tensor_tensor(diffs[:, :, 0:NG], groups, wide(mx[:, 0, :].unsqueeze(2), P, TT, NG), ALU.subtract))
            for g in range(NG):
                one = wide(one_g[:, :, g:g + 1], P, TT, EPG)
                mine = lg[:, :, NG + g * EPG:NG + (g + 1) * EPG]
                if g == 0:
                    then(dve.tensor_tensor(lsel[:, 0], mine, one, ALU.mult))
                else:
                    then(dve.tensor_tensor(scr, mine, one, ALU.mult))
                    then(dve.tensor_tensor(lsel[:, 0], lsel[:, 0], scr, ALU.add))
            first_one(one_e[:, 0], lsel[:, 0], EPG, mx[:, 1, :])
            then(dve.scalar_tensor_tensor(out=lsel[:, 1], in0=one_e[:, 0], scalar=-3.0e38, in1=lsel[:, 0], op0=ALU.mult, op1=ALU.add))
            first_one(one_e[:, 1], lsel[:, 1], EPG, mx[:, 2, :])
            dve.tensor_tensor(diffs[:, :, NG], mx[:, 2, :], mx[:, 1, :], ALU.subtract).then_inc(log_ready, 1)
            for k in range(2):
                for g in range(NG):
                    then(dve.tensor_tensor(OH[:, k, :, g * EPG:(g + 1) * EPG], one_e[:, k], wide(one_g[:, :, g:g + 1], P, TT, EPG), ALU.mult))
                then(dve.tensor_tensor(OH[:, k], OH[:, k], wide(valid[:, :].unsqueeze(2), P, TT, NE), ALU.mult))
            dve.tensor_tensor(OHs, OH[:, 0], OH[:, 1], ALU.add).then_inc(oh_ready, 1)
            dve.wait_ge(e_ready, 1)
            then(dve.tensor_reduce(mx[:, 0, :], exps[:, :, 0:NG], AX, ALU.add))
            then(dve.scalar_tensor_tensor(out=mx[:, 0, :], in0=exps[:, :, NG], scalar=1.0, in1=mx[:, 0, :], op0=ALU.add, op1=ALU.mult))
            then(dve.reciprocal(wk[:, 0, :], mx[:, 0, :]))
            then(dve.tensor_tensor(wk[:, 1, :], wk[:, 0, :], exps[:, :, NG], ALU.mult))
            dve.wait_ge(rank_ps, 1)
            earlier = PS[:, 1, 0:TT * NE].rearrange("p (t e) -> p t e", e=NE)
            for k in range(2):
                then(dve.tensor_tensor(prod, OH[:, k], earlier, ALU.mult))
                then(dve.tensor_reduce(rank[:, k, :], prod, AX, ALU.add))
            then(dve.tensor_tensor(cmp, wide(PS[:, 1, TT * NE:(TT + 1) * NE].unsqueeze(2), P, NE, STEPS),
                                   wide(steps[:, :].unsqueeze(1), P, NE, STEPS), ALU.is_gt))
            then(dve.tensor_reduce(nov, cmp, AX, ALU.add))
            then(dve.tensor_copy(cum[:, 0, :], nov))
            at, step = 0, 1
            while step < NE:
                then(dve.tensor_copy(cum[:, 1 - at, 0:step], cum[:, at, 0:step]))
                then(dve.tensor_tensor(cum[:, 1 - at, step:NE], cum[:, at, step:NE], cum[:, at, 0:NE - step], ALU.add))
                at, step = 1 - at, 2 * step
            upto = cum[:, at, :]
            then(dve.tensor_tensor(exc, upto, nov, ALU.subtract))
            then(dve.tensor_tensor(ocmp, wide(upto.unsqueeze(1), P, OVER, NE), wide(iota[:, 0:OVER].unsqueeze(2), P, OVER, NE), ALU.is_le))
            then(dve.tensor_reduce(oex, ocmp, AX, ALU.add))
            then(dve.tensor_scalar(over_expert[0:1, 0:OVER], oex[0:1, :], float(NE - 1), None, ALU.min))
            then(dve.tensor_copy(over_expert[0:1, OVER:OVER + 1], upto[0:1, NE - 1:NE]))
            for k in range(2):
                then(dve.tensor_tensor(prod, OH[:, k], wide(exc.unsqueeze(1), P, TT, NE), ALU.mult))
                then(dve.tensor_reduce(ovs[:, k, :], prod, AX, ALU.add))
                then(dve.tensor_tensor(prod, OH[:, k], wide(iota[:, 0:NE].unsqueeze(1), P, TT, NE), ALU.mult))
                then(dve.tensor_reduce(eid[:, k, :], prod, AX, ALU.add))
            flat = {n: ap.rearrange("p a b -> p (a b)") for n, ap in
                    (("rank", rank), ("ovs", ovs), ("eid", eid), ("q", q), ("tile", tile), ("off", off), ("wk", wk))}
            then(dve.tensor_tensor(q8, wide(flat["rank"].unsqueeze(2), P, 2 * TT, STEPS), wide(steps[:, :].unsqueeze(1), P, 2 * TT, STEPS), ALU.is_ge))
            then(dve.tensor_reduce(flat["q"], q8, AX, ALU.add))
            then(dve.scalar_tensor_tensor(out=flat["off"], in0=flat["q"], scalar=-float(SLOTS), in1=flat["rank"], op0=ALU.mult, op1=ALU.add))
            then(dve.tensor_tensor(flat["ovs"], flat["ovs"], flat["q"], ALU.add))
            then(dve.scalar_tensor_tensor(out=flat["ovs"], in0=flat["ovs"], scalar=float(NE - 1), in1=flat["eid"], op0=ALU.add, op1=ALU.subtract))
            then(dve.tensor_scalar(flat["q"], flat["q"], 1.0, None, ALU.min))
            then(dve.tensor_tensor(flat["ovs"], flat["ovs"], flat["q"], ALU.mult))
            then(dve.tensor_tensor(flat["tile"], flat["eid"], flat["ovs"], ALU.add))
            then(dve.tensor_tensor(TOH, wide(flat["tile"].unsqueeze(2), P, 2 * TT, TILES), wide(iota[:, 0:TILES].unsqueeze(1), P, 2 * TT, TILES), ALU.is_equal))
            for k in range(2):
                then(dve.tensor_tensor(TOH[:, k * TT:(k + 1) * TT, :], TOH[:, k * TT:(k + 1) * TT, :], wide(valid[:, :].unsqueeze(2), P, TT, TILES), ALU.mult))
            then(dve.tensor_tensor(FOH, wide(flat["off"].unsqueeze(2), P, 2 * TT, SLOTS), wide(iota[:, 0:SLOTS].unsqueeze(1), P, 2 * TT, SLOTS), ALU.is_equal))
            for k in range(2):
                then(dve.tensor_scalar(pid[:, k, :], tokid[:, :], 1.0, float(k * T + 1), ALU.mult, ALU.add))
                half = slice(k * TT, (k + 1) * TT)
                for n, what in enumerate((tokid[:, :], pid[:, k, :], wk[:, k, :])):
                    last = dve.tensor_tensor(R[:, half, n * TILES:(n + 1) * TILES], TOH[:, half, :], wide(what.unsqueeze(2), P, TT, TILES), ALU.mult)
                    if k == 0 or n < 2:
                        then(last)
            last.then_inc(tab_ready, 1)
            dve.wait_ge(tab_ps, 1)
            then(dve.tensor_copy(tokI[:, :], PS[0:SLOTS, 2, 0:TILES]))
            then(dve.tensor_copy(wslot[:, :], PS[0:SLOTS, 2, 2 * TILES:3 * TILES]))
            then(dve.tensor_scalar(un[0:SLOTS, :], PS[0:SLOTS, 2, TILES:2 * TILES], 0.0, 4096.0, ALU.is_equal, ALU.mult))
            dve.scalar_tensor_tensor(out=pairI[:, :], in0=PS[0:SLOTS, 2, TILES:2 * TILES], scalar=-1.0, in1=un[0:SLOTS, :],
                                     op0=ALU.add, op1=ALU.add).then_inc(routed, 1)
            dve.wait_ge(routed, 1)

            def take_rows(i, t, b):
                dve.wait_ge(t_ps, cnt(i, t))
                dve.tensor_copy(hG[:, b, 512:1024], PS[:, 1, :]).then_inc(hg_ready, 1)

            def gate_hidden(i, t):
                dve.wait_ge(sil_ready, cnt(i, t))
                dve.tensor_tensor(he, PS[:, 2, DE:2 * DE], sil, ALU.mult).then_inc(he_ready, 1)

            def take_hidden(i, t):
                dve.wait_ge(he_ps, cnt(i, t))
                dve.tensor_copy(heT.rearrange("p k s -> p (k s)"), PS[:, 3, 0:2 * SLOTS]).then_inc(het_ready, 1)

            def weigh(i, t, b):
                dve.wait_ge(down_done, cnt(i, t))
                if t >= 3:
                    dve.wait_ge(scattered[b], cnt(i, t, 8, -8 * (1 + b)))
                dve.tensor_scalar(Y[:, b, 512:1024], PS[:, 5 + 2 * b, :], wslot[:, col(i, t - 1)], None, ALU.mult).then_inc(y_dve, 1)

            def expert_tile(i, t, b):
                gate_hidden(i, t)
                take_rows(i, t + 1, 1 - b)
                weigh(i, t - 1, 1 - b)
                take_hidden(i, t)

            def expert_tiles(first, last, peeled):
                take_rows(None, first, 0)
                gate_hidden(None, first)
                take_rows(None, first + 1, 1)
                take_hidden(None, first)
                for t in range(first + 1, first + 1 + peeled):
                    expert_tile(None, t, (t + 1) % 2)
                tiles(dve, first + 1 + peeled, last - 1, expert_tile)
                gate_hidden(None, last)
                weigh(None, last - 1, 0)
                take_hidden(None, last)
                weigh(None, last, 1)

            expert_tiles(1, ALWAYS, 2)
            with some_overflow(dve):
                expert_tiles(ALWAYS + 1, TILES, 0)

            dve.wait_ge(fin_in, 16 * 7)
            for s, rows in ((0, P), (1, NSAMPLE)):
                then(dve.scalar_tensor_tensor(out=afb[s][0:rows, :], in0=afb[s][0:rows, :], scalar=1.0, in1=gfb[0:rows, :],
                                              op0=ALU.add, op1=ALU.mult))

            def finish(t):
                w, s = WIDTH[t], t // 4
                o = pair_rows[0][0:w, t, :]
                dve.wait_ge(f_sd, t + 1)
                then(dve.reciprocal(rs[0:w, t:t + 1], sd[0:w, t:t + 1]))
                then(dve.scalar_tensor_tensor(out=o, in0=x[0:w, t, :], scalar=rs[0:w, t:t + 1], in1=afb[s][0:w, :],
                                              op0=ALU.mult, op1=ALU.mult))
                dve.tensor_tensor(o, o, shfb[s][0:w, :], ALU.add).then_inc(f_out, 1)

            for t in range(TT):
                w, s = WIDTH[t], t // 4
                o = pair_rows[0][0:w, t, :]
                dve.wait_ge(pair_in[t], 32)
                then(dve.tensor_tensor(o, o, pair_rows[1][0:w, t, :], ALU.add))
                then(dve.tensor_tensor(o, o, g2b[s][0:w, :], ALU.mult))
                dve.tensor_tensor(x[0:w, t, :], x[0:w, t, :], o, ALU.add).then_inc(f_sum, 1)
                if t:
                    finish(t - 1)
            finish(TT - 1)

        @block.gpsimd
        def _(pool):
            pool.memset(ident[:, :], 0.0).then_inc(consts, 1)
            pool.memset(before[:, :], 1.0).then_inc(consts, 1)
            pool.memset(valid[:, :], 1.0).then_inc(consts, 1)
            pool.wait_ge(consts, 3)
            pool.affine_select(out=ident[:, :], in_=ident[:, :], compare_op=ALU.not_equal, fill=1.0, base=0,
                               pattern=[[-1, P]], channel_multiplier=1).then_inc(consts, 1)
            pool.affine_select(out=before[:, :], in_=before[:, :], compare_op=ALU.is_gt, fill=0.0, base=0,
                               pattern=[[1, P]], channel_multiplier=-1).then_inc(consts, 1)
            pool.affine_select(out=valid[:, :], in_=valid[:, :], compare_op=ALU.is_gt, fill=0.0, base=T,
                               pattern=[[-P, TT]], channel_multiplier=-1).then_inc(consts, 1)
            pool.iota(iotaI[:, :], pattern=[[1, SLOTS]], base=0, channel_multiplier=0).then_inc(consts, 1)
            pool.iota(tokidI[:, :], pattern=[[P, TT]], base=0, channel_multiplier=1).then_inc(consts, 1)
            pool.memset(meanm[:, :], 1.0 / D).then_inc(consts, 1)
            pool.memset(ones[:, :], 1.0).then_inc(consts, 1)
            pool.memset(eps[:, :], EPS).then_inc(consts, 1)
            pool.memset(ss[:, :], 1.0).then_inc(consts, 1)
            for m in range(STEPS):
                pool.memset(steps[:, m:m + 1], float(SLOTS * (m + 1))).then_inc(consts, 1)
            pool.memset(aF[:, :, 0:HIST], 0.0).then_inc(aF_written, 4)
            pool.wait_ge(ws_in, 16)
            for h in range(KT):
                pool.affine_select(out=wsR[:, h, :], in_=wsR[:, h, :], compare_op=ALU.is_ge, fill=0.0, base=0,
                                   pattern=[[-1, P]], channel_multiplier=1).then_inc(ws_masked, 1)

            def add_bias(b, drained, landed, added, cols):
                pool.wait_ge(act_drained, drained)
                pool.wait_ge(w_full[b], landed)
                pool.tensor_tensor(mrow[:, b, :], mrow[:, b, :], brow[:, b, :], ALU.add).then_inc(mod_added, 1)
                pool.wait_ge(mod_added, added)
                pool.dma_start(mod[:, cols], mrow[:, b, :]).then_inc(mod_stored[b], 16)

            for m in range(4):
                add_bias(m % 2, m + 1, 32 * (m // 2 + 1), m + 1, slice(m * BLK, (m + 1) * BLK))
            with pool.Fori(0, KT // 2) as half:
                i = half * 2
                for b in range(2):
                    pool.wait_ge(act_drained, i + (Q_A + b + 1))
                    for at, n, first in ((HIST, NPROMPT, 0), (2 * HIST + NPROMPT, NSAMPLE, NPROMPT)):
                        pool.tensor_tensor(aF[:, ds(i + b, 1), at:at + n].rearrange("p o t -> p (o t)"), tmp[:, b, first:first + n],
                                           tmp[:, 2 + b, first:first + n], ALU.mult).then_inc(aF_written, 1)
            pool.wait_ge(v_norm, TT)
            pool.dma_start(v_out, v[0:NSAMPLE, 4, :]).then_inc(v_stored, 16)
            pool.wait_ge(v_stored, 16)
            for j in range(KT):
                pool.wait_ge(centred, j + 1)
                pool.tensor_tensor(sq[:, j, :], cv[:, j, :], cv[:, j, :], ALU.mult).then_inc(squared, 1)
            with pool.Fori(0, 12 // 2) as half:
                i = half * 2
                for b in range(2):
                    add_bias(b, i + (Q_ADA2 + b + 1), i * 16 + 32 * (U_ADA2 // 2 + 1), i + (5 + b), ds(i * BLK + (4 + b) * BLK, BLK))

            pool.wait_ge(routed, 1)
            pool.wait_ge(h2_stored[0], 48)
            pool.wait_ge(h2_stored[1], 32)

            last_token, last_pair = pool.to_reg(T - 1), pool.to_reg(2 * T - 1)

            def gather(i, t, b):
                if t >= 3:
                    pool.wait_ge(t_ps, cnt(i, t, 1, -2))
                pool.tensor_copy(gidx[b][:, :], tokI[:, col(i, t - 1)]).then_inc(g_idx, 1)
                pool.wait_ge(g_idx, cnt(i, t))
                pool.sem_inc(gathers_begun)
                pool.indirect_dma_start(out=G[:, b, :], out_offset=None, in_=h2d,
                                        in_offset=bass.IndirectOffsetOnAxis(ap=gidx[b][:, 0:1], axis=0),
                                        bounds_check=last_token, oob_is_err=True).then_inc(gathered[b], 16)

            def scatter(i, t, b):
                if t >= 3:
                    pool.wait_ge(scattered[b], cnt(i, t, 8, -8 * (1 + b)))
                pool.tensor_copy(sidx[b][:, :], pairI[:, col(i, t - 1)]).then_inc(s_idx, 1)
                pool.wait_ge(s_idx, cnt(i, t))
                pool.wait_ge(y_act, cnt(i, t))
                pool.wait_ge(y_dve, cnt(i, t))
                pool.sem_inc(scatters_begun)
                pool.indirect_dma_start(out=pairs, out_offset=bass.IndirectOffsetOnAxis(ap=sidx[b][:, 0:1], axis=0),
                                        in_=Y[:, b, :], in_offset=None,
                                        bounds_check=last_pair, oob_is_err=False).then_inc(scattered[b], 16)

            def rows_in_and_out(i, t, b):
                gather(i, t + 3, 1 - b)
                scatter(i, t, b)

            def expert_tiles(first, last):
                for t in range(first, first + 3):
                    gather(None, t, (t + 1) % 2)
                for t in range(first, first + 3):
                    rows_in_and_out(None, t, (t + 1) % 2)
                if first + 3 <= last - 3:
                    tiles(pool, first + 3, last - 3, rows_in_and_out)
                scatter(None, last - 2, 1)
                scatter(None, last - 1, 0)
                scatter(None, last, 1)
                for b in range(2):
                    pool.wait_ge(scattered[b], 8 * last)

            expert_tiles(1, ALWAYS)
            with some_overflow(pool):
                expert_tiles(ALWAYS + 1, TILES)
            pool.sem_inc(experts_done)


_INS = ["x_prompt", "x_sample", "cache_conv", "c_prompt", "c_sample", "w_ada", "b_ada", "g_norm1", "g_norm2",
        "w_in", "b_in", "conv_w", "conv_b", "ln_g", "ln_b", "w_a", "v_ln_g", "v_ln_b", "w_s", "b_s", "w_b", "w_o",
        "w_rg", "b_rg", "w_re", "b_re", "w_gate", "w_up", "w_down", "g_final", "w_ada_f", "b_ada_f"]


def kernel(**inputs):
    import concourse.bacc as bacc
    from concourse.bass_utils import run_bass_kernel_spmd

    nc = bacc.Bacc("TRN2", target_bir_lowering=False, num_devices=1)
    arrays = {name: np.ascontiguousarray(inputs[name]) for name in _INS}
    aps = {name: nc.dram_tensor(name, arr.shape, mybir.dt.from_np(arr.dtype), kind="ExternalInput").ap()
           for name, arr in arrays.items()}
    outs = [nc.dram_tensor(name, shape, F32, kind="ExternalOutput").ap() for name, shape in
            (("y", (T, D)), ("hist_prompt", (HIST, D)), ("hist_sample", (HIST, D)), ("v_rows", (NSAMPLE, D)))]
    build(nc, aps, *outs)
    r = run_bass_kernel_spmd(nc, [arrays], core_ids=[0]).results[0]
    y = r["y"]
    return (y[:NPROMPT].reshape(1, NPROMPT, D), y[NPROMPT:].reshape(1, NSAMPLE, D),
            r["hist_prompt"].reshape(1, 1, HIST, D), r["hist_sample"].reshape(1, 1, HIST, D),
            r["v_rows"].reshape(1, 1, NSAMPLE, D))
```

```python
from contextlib import ExitStack

import numpy as np

import concourse.bass as bass
from concourse import mybir

F32 = mybir.dt.float32
F32R = mybir.dt.float32r
I32 = mybir.dt.int32
BF16 = mybir.dt.bfloat16
U32 = mybir.dt.uint32
ALU = mybir.AluOpType
ACT = mybir.ActivationFunctionType
AX = mybir.AxisListType.X
ds = bass.ds

P = 128
D = 1024
KT = D // P
NPROMPT, NSAMPLE = 512, 32
T = NPROMPT + NSAMPLE
TT = 5
WIDTH = [P, P, P, P, NSAMPLE]
H = T // 2
TAPS = 31
HIST = TAPS - 1
FULL = T + 2 * HIST
CONV = FULL - HIST
CH = CONV // 2
SAMPLE0 = NPROMPT + HIST
EPS = 1e-6
NG, EPG, NE = 4, 8, 32
DE = 256
SLOTS = 128
OVER = 2 * T // SLOTS
TILES = NE + OVER
ALWAYS = NE + 1
STEPS = T // SLOTS
NLOG = NG + NE
BLK = 512
NMOD = 8 * D

O_X, O_H, O_A, O_C, O_S, O_U, O_V, O_W = 0, 5120, 9472, 14304, 18896, 23248, 27600, 32720
ARENA = 40912
H2_BANK = [6, 2, 4, 6, 2]
ADA1_BANK = [0, 1, 4, 5]


def build(nc, a, y_out, hist_p_out, hist_s_out, v_out):
    with ExitStack() as ctx:
        def sb(name, shape, dt=F32):
            return ctx.enter_context(nc.sbuf_tensor(name, shape, dt))

        def sem(name):
            return ctx.enter_context(nc.semaphore(name))

        PS = ctx.enter_context(nc.psum_tensor("PS", [P, 8, 512], F32))
        def split_parts(name, at, *dims):
            n = 1
            for d in dims:
                n *= d
            with ExitStack() as place:
                if at:
                    place.enter_context(nc.sbuf_tensor(f"{name}_before", [P, at], F32))
                r = place.enter_context(nc.sbuf_tensor(name, [P, n], F32R))[:, :]
            if len(dims) == 2:
                return r.rearrange("p (a b) -> p a b", b=dims[1])
            return r.rearrange("p (a b c) -> p a b c", b=dims[1], c=dims[2])

        hH, hL = split_parts("hH", O_A, KT, T), split_parts("hL", O_H, KT, T)
        wH = [split_parts(f"wH{s}", O_W + 4096 * s + 2048, KT, P) for s in range(2)]
        wL = [split_parts(f"wL{s}", O_W + 4096 * s, KT, P) for s in range(2)]
        gH, gL = split_parts("gH", O_S, KT, T), split_parts("gL", O_V, KT, T)
        wH2 = [split_parts(f"wH2{s}", O_W + 4096 * s + 2048, 2, KT, P) for s in range(2)]
        wL2 = [split_parts(f"wL2{s}", O_W + 4096 * s, 2, KT, P) for s in range(2)]
        arena = sb("arena", [P, ARENA])

        def view(at, *dims):
            n = 1
            for d in dims:
                n *= d
            v = arena[:, at:at + n]
            if len(dims) == 2:
                v = v.rearrange("p (a b) -> p a b", b=dims[1])
            if len(dims) == 3:
                v = v.rearrange("p (a b c) -> p a b c", b=dims[1], c=dims[2])
            return v

        x = view(O_X, TT, D)
        hT = view(O_H, KT, T)
        aF = view(O_A, KT, FULL)
        cv = view(O_C, KT, CONV)
        aT = view(O_S, KT, T)
        uT = view(O_U, KT, T)
        v = view(O_V, TT, D)
        mT = view(O_V, KT, T)
        sq = view(O_V, KT, CONV)
        W = [view(O_W + 4096 * s, KT, BLK) for s in range(2)]
        WP = [view(O_W + 4096 * s, 4, KT, P) for s in range(2)]
        WC = [view(O_C + 1024 * c, 2, BLK) for c in range(4)]
        WU0 = view(O_S + 2048, 2, KT, P)
        before = view(O_U + 2560, P)
        xn = view(O_U, 2, D)
        cacheR = view(O_S, 3, D)[:, 2, :]
        histR = view(O_S, 2, D)
        wsR = view(O_S + 3072, KT, P)
        VR = view(O_U + 2048, 3, P)
        W1 = [view(at, KT, BLK) for at in (O_V, O_C, O_W, O_W + 4096)]
        mod1 = view(O_S, 4 * BLK)
        WG = [view(O_A + 6144 * s, KT, DE) for s in range(2)]
        WU = [view(O_A + 6144 * s + 2048, KT, DE) for s in range(2)]
        WD = [view(O_A + 6144 * s + 4096, 2, D) for s in range(2)]
        g1b = [view(O_U, D), view(O_U + 1024, D)]
        a2b = [view(O_U + 2048, D), view(O_U + 3072, D)]
        sh2b = [view(O_H + 2048, D), view(O_H + 3072, D)]
        gn2b = view(O_A + 12288, D)
        h2 = view(O_H, 2, D)
        G = view(O_V, 2, D)
        hG = view(O_V + 2048, 2, KT * SLOTS)
        Y = view(O_U + 1024, 2, D)
        sil = view(O_U, DE)
        he = view(O_U + DE, DE)
        heT = view(O_U + 2 * DE, 2, SLOTS)
        pair_rows = [view(O_A + 5120 * k, TT, D) for k in range(2)]
        g2b = [view(O_W, D), view(O_W + 1024, D)]
        afb = [view(O_W + 2048, D), view(O_W + 3072, D)]
        shfb = [view(O_W + 4096, D), view(O_W + 5120, D)]
        gfb = view(O_W + 6144, D)
        at_w = [O_W]

        def table(*dims):
            n = 1
            for d in dims:
                n *= d
            r = view(at_w[0], *dims)
            at_w[0] += n
            return r

        ident = sb("ident", [P, P])
        meanm = sb("meanm", [P, P])
        beforeB = sb("beforeB", [P, P], BF16)
        onesB = sb("onesB", [P, P], BF16)
        eps = sb("eps", [P, 1])
        pick = sb("pick", [P, 2, 2])
        vecs = sb("vecs", [P, KT * T])
        bsb = vecs[:, 0:1024].rearrange("p (h t) -> p h t", t=P)
        bvb, vgb, vbb = (vecs[:, 1024 * n:1024 * (n + 1)] for n in (1, 2, 3))
        h2T = vecs[:, :].rearrange("p (k t) -> p k t", t=T)
        mod_sum = vecs[:, 0:4 * BLK].rearrange("p (b s n) -> p b s n", b=2, s=2)
        wsT = sb("wsT", [P, KT, P])
        tmp = sb("tmp", [P, 4, CONV])
        tmp2 = tmp[:, :, :].rearrange("p (a b) t -> p a (b t)", b=2)
        mg, sqj = tmp2[:, 0, 0:D], tmp2[:, 1, 0:D]
        rstdc = sb("rstdc", [P, CONV])
        VT = sb("VT", [P, 360])
        S1 = sb("S1", [P, 2, KT])
        c16 = sb("c16", [16, P])
        cT = sb("cT", [P, 2, KT])
        brow = sb("brow", [2, 2, BLK])
        mrow = sb("mrow", [2, 2, BLK])
        ss = sb("ss", [P, 8])
        sd = sb("sd", [P, 8])
        rs = sb("rs", [P, 8])
        vsd = sb("vsd", [P, 8])
        bn = sb("bn", [P, 2, 6])
        mv = sb("mv", [P, TT, 2])
        wr = sb("wr", [P, KT, NLOG])
        brb = sb("brb", [P, NLOG])
        tokI = sb("tokI", [SLOTS, TILES], U32)
        pairI = sb("pairI", [SLOTS, TILES], U32)
        wslot = sb("wslot", [SLOTS, TILES])
        over_expert = sb("over_expert", [1, OVER + 1], I32)
        gidx = [sb(f"gidx{b}", [SLOTS, 1], U32) for b in range(2)]
        sidx = [sb(f"sidx{b}", [SLOTS, 1], U32) for b in range(2)]
        COL_CB, COL_BIN, COL_LG, COL_LB, COL_G1, COL_MOD = 248, 256, 304, 312, 320, 328

        mod = nc.dram_tensor("mod", (2, NMOD), F32, kind="Internal").ap()
        h2d = nc.dram_tensor("h2d", (T, D), F32, kind="Internal").ap()
        pairs = nc.dram_tensor("pairs", (2 * T, D), F32, kind="Internal").ap()

        consts = sem("consts")
        c_in, x_in, vec_in, bc_in, rt_in = (sem(n) for n in ("c_in", "x_in", "vec_in", "bc_in", "rt_in"))
        ws_in, cache_in, ws_masked = sem("ws_in"), sem("cache_in"), sem("ws_masked")
        c_silu, x_sq, x_sd = sem("c_silu"), sem("x_sq"), sem("x_sd")
        start_ps, start_dr, xn_ready = sem("start_ps"), sem("start_dr"), sem("xn_ready")
        w_full = [sem("w_full0"), sem("w_full1")]
        o_early = sem("o_early")
        w_used = sem("w_used")
        act_drained = sem("act_drained")
        mod_in = [sem(f"mod_in{c}") for c in range(4)]
        bias_in = [sem("bias_in0"), sem("bias_in1")]
        mod_step = sem("mod_step")
        mod_added = sem("mod_added")
        mod_stored = [sem("mod_stored0"), sem("mod_stored1")]
        loads_begun, turns_begun, gathers_begun, scatters_begun, mod_loads_begun = (sem(n) for n in ("loads_begun", "turns_begun", "gathers_begun", "scatters_begun", "mod_loads_begun"))
        ada1_in = [sem(f"ada1_in{n}") for n in range(4)]
        ada1_bias_in, ada1_ready, mod1_ps = (sem(n) for n in ("ada1_bias_in", "ada1_ready", "mod1_ps"))
        xt_ps, xt_copied, s1_ready = (sem(n) for n in ("xt_ps", "xt_copied", "s1_ready"))
        h_even, h_odd = sem("h_even"), sem("h_odd")
        ws_ps, ws_copied = sem("ws_ps"), sem("ws_copied")
        g_high, g_split = sem("g_high"), [sem("g_split0"), sem("g_split1")]
        gw_high, gw_split = sem("gw_high"), sem("gw_split")
        h_high, h_split, w_high, w_split = (sem(n) for n in ("h_high", "h_split", "w_high", "w_split"))
        dve_step = sem("dve_step")
        act_step = sem("act_step")
        aF_written = sem("aF_written")
        conv_step = sem("conv_step")
        hist_ps, hist_copied, hist_stored = sem("hist_ps"), sem("hist_copied"), sem("hist_stored")
        v_copied, v_scaled, v_gained = sem("v_copied"), sem("v_scaled"), sem("v_gained")
        v_ps, v_biased, v_gelu, v_norm, v_stored = (sem(n) for n in ("v_ps", "v_biased", "v_gelu", "v_norm", "v_stored"))
        mix_ps, dve_drained, stat_ps = sem("mix_ps"), sem("dve_drained"), sem("stat_ps")
        centred, squared, c_std, c_normed, a_ready = (sem(n) for n in ("centred", "squared", "c_std", "c_normed", "a_ready"))
        merged, mix_added, gated, v_var, v_sd = (sem(n) for n in ("merged", "mix_added", "gated", "v_var", "v_sd"))
        o_ps, o_drained = sem("o_ps"), sem("o_drained")
        mb_in, mb2_in = sem("mb_in"), sem("mb2_in")
        x1_ready, x1_sd, h2_ready, h2_ps, h2_copied = (sem(n) for n in ("x1_ready", "x1_sd", "h2_ready", "h2_ps", "h2_copied"))
        h2_stored = [sem("h2_stored0"), sem("h2_stored1")]
        log_ps, log_ready, e_ready, oh_ready, rank_ps, tab_ready, tab_ps = (sem(n) for n in ("log_ps", "log_ready", "e_ready", "oh_ready", "rank_ps", "tab_ready", "tab_ps"))
        routed = sem("routed")
        gu_full = [sem("gu_full0"), sem("gu_full1")]
        wd_full = [sem("wd_full0"), sem("wd_full1")]
        g_idx, s_idx = sem("g_idx"), sem("s_idx")
        gathered = [sem("gathered0"), sem("gathered1")]
        scattered = [sem("scattered0"), sem("scattered1")]
        t_ps, hg_ready, gu_done, sil_ready, he_ready, he_ps, het_ready, down_done = (sem(n) for n in ("t_ps", "hg_ready", "gu_done", "sil_ready", "he_ready", "he_ps", "het_ready", "down_done"))
        experts_done = sem("experts_done")
        y_act, y_dve = sem("y_act"), sem("y_dve")
        fin_in, pair_in = sem("fin_in"), [sem(f"pair_in{t}") for t in range(TT)]
        f_scaled = sem("f_scaled")
        f_sum, f_sd, f_out, f_stored = (sem(n) for n in ("f_sum", "f_sd", "f_out", "f_stored"))

        OHs = sb("OHs", [P, TT, NE], BF16)
        iotaI = sb("iotaI", [P, SLOTS], I32)
        iota = sb("iota", [P, SLOTS])
        tokidI = sb("tokidI", [P, TT], I32)
        tokid = sb("tokid", [P, TT])
        valid = sb("valid", [P, TT])
        steps = sb("steps", [P, STEPS])
        lg = table(TT, NLOG)
        one_g = table(TT, NG)
        one_e = table(2, TT, EPG)
        lsel = table(2, TT, EPG)
        prod = table(2 * TT, NE)
        scr = table(TT, EPG)
        mx = table(4, TT)
        diffs = table(TT, NG + 1)
        exps = table(TT, NG + 1)
        vals = table(3, 2, TT)
        OH = table(2, TT, NE)
        rank = table(2, TT)
        cmp = table(NE, STEPS)
        cum = table(2, 2 * NE)
        outside = table(2, TT)
        ovs = table(2, TT)
        eid = table(2, TT)
        q8 = table(2 * TT, STEPS)
        rev = table(1, EPG)
        q = table(2, TT)
        tile = table(2, TT)
        off = table(2, TT)
        TOH = table(2 * TT, TILES)
        FOH = table(2 * TT, SLOTS)
        R = table(2 * TT, 3 * TILES)
        un = table(TILES)
        ocmp = table(OVER, NE)
        oex = table(OVER)
        assert at_w[0] <= ARENA

        NCONST = 15 + STEPS
        block = ctx.enter_context(nc.Block())

        def cnt(i, c, per=1, more=0):
            return c * per + more if i is None else i * per + (c * per + more)

        def col(i, c):
            return slice(c, c + 1) if i is None else ds(i + c, 1)

        def slot(t):
            return (t + 1) % 2

        def tiles(eng, first, last, step, peeled=0):
            peeled += (last + 1 - first - peeled) % 2
            for t in range(first, first + peeled):
                step(None, t, slot(t))
            first += peeled
            if first <= last:
                with eng.Fori(0, (last + 1 - first) // 2) as half:
                    i = half * 2
                    for m in range(2):
                        step(i, first + m, slot(first + m))

        def some_overflow(eng):
            n = eng.value_load(over_expert[0:1, OVER:OVER + 1], min_val=0, max_val=OVER)
            return eng.If(n > ALWAYS - NE)

        def full(eng, n):
            eng.wait_ge(w_full[n % 2], 32 * (n // 2 - 1))

        U_A, U_V, U_U, U_YB, U_YA, U_O = 4, 12, 14, 18, 26, 34
        Q_A, Q_U, Q_YB = 4, 12, 16
        NGATE = 2 * KT
        LAG = 4
        NB = 12

        w_ada = a["w_ada"][0].rearrange("(k p) n -> p k n", p=P)
        w_adaf = a["w_ada_f"].rearrange("(k p) n -> p k n", p=P)
        w_in = a["w_in"][0].rearrange("(k p) n -> p k n", p=P)
        w_a = a["w_a"][0].rearrange("(k p) n -> p k n", p=P)
        w_b = a["w_b"][0].rearrange("(k p) n -> p k n", p=P)
        w_o = a["w_o"][0].rearrange("(k p) n -> p k n", p=P)
        w_gate = a["w_gate"][0].rearrange("e (p k) n -> e p (k n)", p=P)
        w_up = a["w_up"][0].rearrange("e (p k) n -> e p (k n)", p=P)
        w_down = a["w_down"][0].rearrange("e (k p) n -> e p k n", p=P)

        b_adaf = a["b_ada_f"].rearrange("(o n) -> o n", o=1)

        @block.sync
        def _(sp):
            for n in range(4):
                sp.dma_start(W1[n], w_ada[:, :, n * BLK:(n + 1) * BLK]).then_inc(ada1_in[n], 16)
                if n == 0:
                    for t in range(4):
                        sp.dma_start(x[:, t, :], a["x_prompt"][0, t * P:(t + 1) * P, :]).then_inc(x_in, 16)
                    sp.dma_start(x[0:NSAMPLE, 4, :], a["x_sample"][0]).then_inc(x_in, 16)
                    sp.dma_start(mod1[0:2, :], a["b_ada"][:, 0:4 * BLK].to_broadcast([2, 4 * BLK])).then_inc(ada1_bias_in, 16)

            def pair_loads(base, left, left0, right, right0):
                with sp.Fori(0, 8 // 2) as half:
                    i = half * 2
                    for b in range(2):
                        c_left, c_right = sp.snap(i * P + (left0 + b * P)), sp.snap(i * P + (right0 + b * P))
                        sp.wait_ge(w_used, i + (base + b - 1))
                        sp.sem_inc(loads_begun)
                        sp.dma_start(WP[b][:, 0], left[:, :, ds(c_left, P)]).then_inc(w_full[b], 16)
                        sp.dma_start(WP[b][:, 1], right[:, :, ds(c_right, P)]).then_inc(w_full[b], 16)

            pair_loads(U_A, w_in, 0, w_in, D)
            def halves(base, src, col0, early, k0):
                for b in range(2 if k0 < KT else 0):
                    sp.dma_start(W[b][:, k0:KT, :], src[:, k0:KT, col0 + b * BLK:col0 + (b + 1) * BLK]).then_inc(early, 16)
                for b in range(2):
                    sp.wait_ge(w_used, base + b - 1)
                    for m in range(2):
                        sp.dma_start(W[b][:, m * k0 // 2:(m + 1) * k0 // 2, :], src[:, m * k0 // 2:(m + 1) * k0 // 2, col0 + b * BLK:col0 + (b + 1) * BLK]).then_inc(w_full[b], 16)

            halves(U_V, w_in, 3 * D, None, KT)
            for n in range(4):
                if n:
                    sp.wait_ge(w_used, U_U + n - 1)
                else:
                    full(sp, U_V)
                for m in range(2):
                    dst = WU0[:, m] if n == 0 else WP[n % 2][:, m]
                    sp.dma_start(dst, w_in[:, :, 2 * D + (2 * n + m) * P:2 * D + (2 * n + m + 1) * P]).then_inc(w_full[n % 2], 16)

            pair_loads(U_YB, w_in, 5 * D, w_b, 0)
            pair_loads(U_YA, w_in, 4 * D, w_a, 0)
            halves(U_O, w_o, 0, o_early, 6)

            def mod_vec(n, rows, s):
                return mod[s:s + 1, n * D:(n + 1) * D].to_broadcast([rows, D])

            for p in range(2):
                sp.wait_ge(mod_stored[p], 16 * 3)
            sp.wait_ge(w_used, U_YB + 8)
            for s, rows in ((0, P), (1, NSAMPLE)):
                sp.dma_start(g1b[s][0:rows, :], mod_vec(2, rows, s)).then_inc(mb_in, 16)
                sp.dma_start(a2b[s][0:rows, :], mod_vec(4, rows, s)).then_inc(mb_in, 16)
            sp.wait_ge(w_used, U_YA + 8)
            sp.dma_start(gn2b, a["g_norm2"].to_broadcast([P, D])).then_inc(mb2_in, 16)
            for s, rows in ((0, P), (1, NSAMPLE)):
                sp.dma_start(sh2b[s][0:rows, :], mod_vec(3, rows, s)).then_inc(mb2_in, 16)
            sp.wait_ge(a_ready, 2 * KT)
            sp.wait_ge(hist_ps, 2)

            def load_gu(i, t, b, e=None):
                e = col(i, t - 1) if e is None else e
                if t >= 3:
                    sp.wait_ge(gu_done, cnt(i, t, 1, -2))
                    sp.sem_inc(loads_begun)
                sp.dma_start(WG[b].rearrange("p k n -> p (k n)"), w_gate[e].rearrange("o p n -> (o p) n")).then_inc(gu_full[b], 16)
                sp.dma_start(WU[b].rearrange("p k n -> p (k n)"), w_up[e].rearrange("o p n -> (o p) n")).then_inc(gu_full[b], 16)

            def load_d(i, t, b, e=None):
                e = col(i, t - 1) if e is None else e
                if t >= 3:
                    sp.wait_ge(down_done, cnt(i, t, 1, -2))
                    sp.sem_inc(loads_begun)
                sp.dma_start(WD[b], w_down[e].rearrange("o p k n -> (o p) k n")).then_inc(wd_full[b], 16)

            def owner(i, t):
                e = sp.value_load(over_expert[0:1, col(i, t - 1 - NE)], min_val=0, max_val=NE - 1)
                return ds(e, 1)

            load_gu(None, 1, 0)
            load_gu(None, 2, 1)
            load_d(None, 1, 0)
            for t in (3, 4):
                load_gu(None, t, slot(t))
                load_d(None, t - 1, slot(t - 1))

            def own(i, t, b):
                load_gu(i, t, b)
                load_d(i, t - 1, 1 - b)

            def over(i, t, b):
                load_gu(i, t, b, owner(i, t))
                load_d(i, t - 1, 1 - b, owner(i, t - 1))

            tiles(sp, 5, NE, own)
            sp.wait_ge(routed, 1)
            load_gu(None, NE + 1, 0, owner(None, NE + 1))
            load_d(None, NE, 1)
            load_d(None, ALWAYS, slot(ALWAYS), owner(None, ALWAYS))
            for p in range(2):
                sp.wait_ge(mod_stored[p], 16 * 6)
            sp.dma_start(gfb, a["g_final"].rearrange("(o n) -> o n", o=1).to_broadcast([P, D])).then_inc(fin_in, 16)
            for s, rows in ((0, P), (1, NSAMPLE)):
                for n, dst in ((5, g2b), (6, shfb), (7, afb)):
                    sp.dma_start(dst[s][0:rows, :], mod_vec(n, rows, s)).then_inc(fin_in, 16)
            with some_overflow(sp):
                load_gu(None, ALWAYS + 1, slot(ALWAYS + 1), owner(None, ALWAYS + 1))
                tiles(sp, ALWAYS + 2, TILES, over)
                load_d(None, TILES, slot(TILES), owner(None, TILES))
            sp.wait_ge(experts_done, 1)
            for t in range(TT):
                for k in range(2):
                    sp.dma_start(pair_rows[k][0:WIDTH[t], t, :], pairs[k * T + t * P:k * T + t * P + WIDTH[t], :]).then_inc(pair_in[t], 16)
            for t in range(TT):
                sp.wait_ge(f_out, t + 1)
                sp.dma_start(y_out[t * P:t * P + WIDTH[t], :], pair_rows[0][0:WIDTH[t], t, :]).then_inc(f_stored, 16)
            sp.wait_ge(f_stored, 16 * TT)
            sp.wait_ge(hist_stored, 32)
            sp.wait_ge(v_stored, 16)

        @block.tensor
        def _(pe):
            def product(bank, tile_w, act):
                for k in range(KT):
                    for h in range(2):
                        last = pe.matmul(PS[:, bank + h, 0:H], tile_w[:, k, :], act[:, k, h * H:(h + 1) * H],
                                         start=(k == 0), stop=(k == KT - 1))
                return last

            def ada(b):
                for k in range(KT):
                    last = pe.matmul(PS[0:2, 4 * b, :], cT[:, :, k], W[b][:, k, :], start=(k == 0), stop=(k == KT - 1))
                return last

            pe.wait_ge(consts, NCONST)
            pe.wait_ge(c_silu, 1)
            pe.transpose(PS[:, 0, 0:16], c16[:, :], ident[0:16, 0:16]).then_inc(start_ps, 1)
            def ada1(n):
                pe.wait_ge(start_dr, 1)
                pe.wait_ge(ada1_in[n], 16)
                for k in range(KT):
                    last = pe.matmul(PS[0:2, ADA1_BANK[n], :], cT[:, :, k], W1[n][:, k, :], start=(k == 0), stop=(k == KT - 1))
                last.then_inc(w_used, 1)

            ada1(0)
            def turn_x(t):
                w = WIDTH[t]
                bank = 6 if t % 2 == 0 else 2
                if t >= 2:
                    pe.wait_ge(xt_copied, t - 1)
                pe.wait_ge(xn_ready, t + 1)
                for j in range(KT):
                    last = pe.transpose(PS[:, bank + j // 4, (j % 4) * P:(j % 4) * P + w],
                                        xn[0:w, t % 2, j * P:(j + 1) * P], ident[0:w, 0:w])
                last.then_inc(xt_ps, 1)

            turn_x(0)
            turn_x(1)
            ada1(1)
            turn_x(2)
            turn_x(3)
            ada1(2)
            turn_x(4)
            ada1(3)
            pe.wait_ge(vec_in, 16 * 7)
            pe.wait_ge(ada1_ready, 1)
            pe.transpose(PS[:, 0, 0:128], VR[:, 0, :], ident[:, :])
            pe.transpose(PS[:, 0, 128:256], VR[:, 1, :], ident[:, :])
            pe.transpose(PS[:, 0, 256:328], VR[0:72, 2, :], ident[0:72, 0:72]).then_inc(start_ps, 1)
            pe.wait_ge(cache_in, 16)
            pe.wait_ge(xt_copied, 4)
            for j in range(KT):
                last = pe.transpose(PS[:, 2, j * HIST:(j + 1) * HIST], cacheR[0:HIST, j * P:(j + 1) * P], ident[0:HIST, 0:HIST])
            last.then_inc(start_ps, 1)

            pe.wait_ge(ws_masked, KT)
            pe.wait_ge(xt_copied, TT)
            for h in range(KT):
                last = pe.transpose(PS[:, 6 + h // 4, (h % 4) * P:(h % 4 + 1) * P], wsR[:, h, :], ident[:, :])
            last.then_inc(ws_ps, 1)
            pe.wait_ge(ada1_ready, 4)
            for n in range(2 * KT):
                last = pe.transpose(PS[:, 3, 2 * n:2 * n + 2], mod1[0:2, n * P:(n + 1) * P], ident[0:2, 0:2])
            last.then_inc(mod1_ps, 1)
            pe.wait_ge(ws_copied, 1)

            def product_split(bank, w_high, w_low, act_high, act_low, ready=None):
                for k in range(KT):
                    if ready:
                        pe.wait_ge(ready[k % 2], k // 2 + 1)
                    for n, (w, part) in enumerate(((w_high, act_high), (w_high, act_low), (w_low, act_high))):
                        for h in range(2):
                            last = pe.matmul(PS[:, bank + h, 0:H], w[:, k, :], part[:, k, h * H:(h + 1) * H],
                                             start=(k == 0 and n == 0), stop=(k == KT - 1 and n == 2))
                return last

            with pe.Fori(0, KT // 2) as half:
                i = half * 2
                for b in range(2):
                    pe.wait_ge(act_drained, i + (Q_A + b - 1))
                    for m in range(2):
                        pe.wait_ge(gw_split, i * 2 + (2 * b + m + 1))
                        last = product_split(4 * b + 2 * m, wH2[b][:, m], wL2[b][:, m], gH, gL, g_split)
                    last.then_inc(w_used, 1)
            def histories(first):
                for j in range(KT):
                    last = pe.transpose(PS[0:HIST, 6 + j // 4, (j % 4) * P:(j % 4 + 1) * P], aF[:, j, first:first + HIST], ident[:, :])
                last.then_inc(hist_ps, 1)

            pe.wait_ge(act_drained, Q_A + 8)
            pe.wait_ge(aF_written, 4 + 2 * KT)
            histories(NPROMPT)
            full(pe, U_V)
            for t in range(TT):
                for hf in range(2):
                    g = 2 * t + hf
                    if g == 1:
                        full(pe, U_V + 1)
                    if g >= 6:
                        pe.wait_ge(v_copied, g - 5)
                    for k in range(KT):
                        last = pe.matmul(PS[0:WIDTH[t], g % 6, :], hT[:, k, t * P:t * P + WIDTH[t]], W[hf][:, k, :],
                                         start=(k == 0), stop=(k == KT - 1))
                    if g < 2 * TT - 1:
                        last.then_inc(v_ps, 1)
            last.then_inc(w_used, 2)
            pe.wait_ge(v_copied, 2 * TT)
            pe.wait_ge(hist_copied, 1)
            for n in range(4):
                b = n % 2
                full(pe, U_U + n)
                pe.wait_ge(act_drained, Q_U + n - 1)
                for m in range(2):
                    last = product(4 * b + 2 * m, WU0[:, m] if n == 0 else WP[b][:, m], hT)
                last.then_inc(w_used, 1)
            pe.wait_ge(act_drained, Q_U + 4)
            histories(FULL - HIST)
            pe.wait_ge(v_norm, TT)
            for h in range(KT):
                b = h % 2
                if h >= 2:
                    pe.wait_ge(dve_drained, h - 1)
                for t in range(4):
                    pe.matmul(PS[:, 2 * b, t * P:(t + 1) * P], v[:, t, h * P:(h + 1) * P], wsT[:, h, :], start=True, stop=True)
                pe.matmul(PS[:, 2 * b + 1, 0:NSAMPLE], v[0:NSAMPLE, 4, h * P:(h + 1) * P],
                          wsT[0:NSAMPLE, h, 0:NSAMPLE], start=True, stop=True).then_inc(mix_ps, 1)

            def over_features(bank, src):
                for j in range(KT):
                    for h in range(2):
                        last = pe.matmul(PS[:, bank + h, 0:CH], meanm[:, :], src[:, j, h * CH:(h + 1) * CH],
                                         start=(j == 0), stop=(j == KT - 1))
                last.then_inc(stat_ps, 1)

            pe.wait_ge(conv_step, TAPS * KT)
            pe.wait_ge(hist_copied, 2)
            over_features(6, cv)
            def gated_use(i, u, b, right_act):
                pe.wait_ge(w_full[b], cnt(i, u, 16, 16 * (U_YB - b) - 32))
                pe.wait_ge(act_drained, cnt(i, u, 1, Q_YB - 1))
                pe.wait_ge(w_split, cnt(i, u, 1, 1))
                if u >= 2:
                    pe.wait_ge(dve_drained, cnt(i, u, 1, KT - 1))
                if u >= LAG + 2:
                    pe.wait_ge(mod_added, cnt(i, u, 1, -LAG - 1))
                product_split(4 * b, wH[b], wL[b], hH, hL)
                return product(4 * b + 2, WP[b][:, 1], right_act)

            def sum_mod(i, u, b):
                m = u - LAG
                pe.wait_ge(mod_step, cnt(i, m, 16, 16))
                for q in range(4):
                    for s in range(2):
                        last = pe.matmul(PS[0:2, 4 * b + q, 512 - P:512], pick[:, s, :], mod_sum[:, b, s, q * P:(q + 1) * P],
                                         start=(s == 0), stop=(s == 1))
                last.then_inc(w_used, 1)

            pe.wait_ge(gated, KT)
            pe.wait_ge(h_split, KT)
            gated_use(None, 0, 0, uT).then_inc(w_used, 1)
            pe.wait_ge(squared, KT)
            over_features(4, sq)
            pe.wait_ge(centred, KT)
            pe.wait_ge(c_std, 1)
            gated_use(None, 1, 1, uT).then_inc(w_used, 1)
            for u in range(2, LAG + 2):
                last = gated_use(None, u, u % 2, uT)
                if u < LAG:
                    last.then_inc(w_used, 1)
                else:
                    sum_mod(None, u, u % 2)
            for first, count, right_act in ((LAG + 2, 2, uT), (KT, 8, aT)):
                if first == KT:
                    pe.wait_ge(a_ready, 2 * KT)
                with pe.Fori(0, count // 2) as half:
                    i = half * 2
                    for b in range(2):
                        gated_use(i, first + b, b, right_act)
                        sum_mod(i, first + b, b)
            pe.wait_ge(o_early, 32)
            full(pe, U_O)
            pe.wait_ge(merged, 2 * KT)
            pe.wait_ge(act_drained, Q_YB + NGATE)
            pe.wait_ge(mod_added, NB)

            def project(t):
                if t == 3:
                    pe.wait_ge(h2_copied, 1)
                if t == 4:
                    pe.wait_ge(o_drained, 2)
                for hf in range(2):
                    if (t, hf) == (0, 1):
                        full(pe, U_O + 1)
                    for k in range(KT):
                        last = pe.matmul(PS[0:WIDTH[t], (2 * t + hf) % 8, :], mT[:, k, t * P:t * P + WIDTH[t]], W[hf][:, k, :],
                                         start=(k == 0), stop=(k == KT - 1))
                    if t < 4 or hf == 0:
                        last.then_inc(o_ps, 1)
                    else:
                        last.then_inc(w_used, 2)

            def turn_h2(t):
                bank = H2_BANK[t]
                pe.wait_ge(h2_ready, t + 1)
                if t == 4:
                    pe.wait_ge(h2_copied, 2)
                for j in range(KT):
                    last = pe.transpose(PS[:, bank + j // 4, (j % 4) * P:(j % 4) * P + WIDTH[t]],
                                        h2[0:WIDTH[t], t % 2, j * P:(j + 1) * P], ident[0:WIDTH[t], 0:WIDTH[t]])
                last.then_inc(h2_ps, 1)

            project(0)
            for t in range(1, TT):
                project(t)
                turn_h2(t - 1)
            def logits(t):
                pe.wait_ge(h2_copied, max(t + 1, 3))
                for k in range(KT):
                    last = pe.matmul(PS[0:WIDTH[t], 4, t * NLOG:(t + 1) * NLOG], h2T[:, k, t * P:t * P + WIDTH[t]], wr[:, k, :],
                                     start=(k == 0), stop=(k == KT - 1))
                return last

            pe.wait_ge(rt_in, 64)
            for t in range(3):
                logits(t)
            turn_h2(TT - 1)
            logits(3)
            logits(4).then_inc(log_ps, 1)
            pe.wait_ge(oh_ready, 1)
            for t in range(TT):
                for s in range(t + 1):
                    pe.matmul(PS[:, 1, t * NE:(t + 1) * NE], beforeB[:, :] if s == t else onesB[:, :], OHs[:, s, :],
                              start=(s == 0), stop=(s == t))
            for s in range(TT):
                last = pe.matmul(PS[:, 1, TT * NE:(TT + 1) * NE], onesB[:, :], OHs[:, s, :], start=(s == 0), stop=(s == TT - 1))
            last.then_inc(rank_ps, 1)
            pe.wait_ge(tab_ready, 1)
            for n in range(2 * TT):
                last = pe.matmul(PS[0:SLOTS, 2, 0:3 * TILES], FOH[:, n, :], R[:, n, :], start=(n == 0), stop=(n == 2 * TT - 1))
            last.then_inc(tab_ps, 1)

            def turn_rows(i, t, b):
                pe.wait_ge(gathered[b], cnt(i, t, 8, 8 * (1 - b)))
                pe.sem_inc(turns_begun)
                if t >= 2:
                    pe.wait_ge(hg_ready, cnt(i, t, 2, -2))
                    pe.sem_inc(turns_begun)
                for k in range(KT):
                    last = pe.transpose(PS[:, k // 4, (k % 4) * SLOTS:(k % 4 + 1) * SLOTS], G[:, b, k::KT], ident[:, :])
                last.then_inc(t_ps, 1)

            def gate_up(i, t, b):
                pe.wait_ge(gu_full[b], cnt(i, t, 16, 16 * (1 - b)))
                pe.wait_ge(hg_ready, cnt(i, t, 2))
                for n, w in enumerate((WG[b], WU[b])):
                    for k in range(KT):
                        last = pe.matmul(PS[:, 2, n * DE:(n + 1) * DE], hG[:, b, k * SLOTS:(k + 1) * SLOTS], w[:, k, :],
                                         start=(k == 0), stop=(k == KT - 1))
                last.then_inc(gu_done, 1)

            def turn_hidden(i, t):
                pe.wait_ge(he_ready, cnt(i, t))
                pe.sem_inc(turns_begun)
                for k in range(2):
                    last = pe.transpose(PS[:, 3, k * SLOTS:(k + 1) * SLOTS], he[:, k * P:(k + 1) * P], ident[:, :])
                last.then_inc(he_ps, 1)

            def down(i, t, b):
                pe.wait_ge(wd_full[b], cnt(i, t, 8, 8 * (1 - b)))
                pe.wait_ge(het_ready, cnt(i, t))
                for hf in range(2):
                    for k in range(2):
                        last = pe.matmul(PS[:, 4 + 2 * b + hf, :], heT[:, k, :], WD[b][:, k, hf * 512:(hf + 1) * 512],
                                         start=(k == 0), stop=(k == 1))
                last.then_inc(down_done, 1)

            def expert_tile(i, t, b):
                gate_up(i, t, b)
                turn_rows(i, t + 1, 1 - b)
                down(i, t - 1, 1 - b)
                turn_hidden(i, t)

            def expert_tiles(first, last):
                turn_rows(None, first, slot(first))
                gate_up(None, first, slot(first))
                turn_rows(None, first + 1, slot(first + 1))
                turn_hidden(None, first)
                tiles(pe, first + 1, last - 1, expert_tile)
                gate_up(None, last, slot(last))
                down(None, last - 1, slot(last - 1))
                turn_hidden(None, last)
                down(None, last, slot(last))

            pe.wait_ge(routed, 1)
            expert_tiles(1, ALWAYS)
            with some_overflow(pe):
                expert_tiles(ALWAYS + 1, TILES)
        @block.scalar
        def _(act):
            act.dma_start(c16[0:8, :], a["c_prompt"].rearrange("o (k p) -> (o k) p", p=P)).then_inc(c_in, 16)
            act.dma_start(c16[8:16, :], a["c_sample"].rearrange("o (k p) -> (o k) p", p=P)).then_inc(c_in, 16)
            act.wait_ge(c_in, 32)
            act.activation(c16[:, :], c16[:, :], ACT.Silu).then_inc(c_silu, 1)
            taps = a["conv_w"][0].rearrange("t (j p) -> (t j) p", p=P)
            act.dma_start(VR[:, 0, :], taps[0:P, :]).then_inc(vec_in, 16)
            act.dma_start(VR[0:TAPS * KT - P, 1, :], taps[P:TAPS * KT, :]).then_inc(vec_in, 16)

            def rows(name):
                return a[name].rearrange("o (j p) -> (o j) p", p=P)

            act.dma_start(VR[TAPS * KT - P:P, 1, :], rows("conv_b")).then_inc(vec_in, 16)
            act.dma_start(VR[0:48, 2, :], rows("b_in")).then_inc(vec_in, 16)
            act.dma_start(VR[48:56, 2, :], rows("ln_g")).then_inc(vec_in, 16)
            act.dma_start(VR[56:64, 2, :], rows("ln_b")).then_inc(vec_in, 16)
            act.dma_start(VR[64:72, 2, :], rows("g_norm1")).then_inc(vec_in, 16)
            act.dma_start(cacheR[0:HIST, :], a["cache_conv"][0, 0]).then_inc(cache_in, 16)
            act.dma_start(wsR, a["w_s"][0].rearrange("h t s -> t h s")).then_inc(ws_in, 16)

            act.wait_ge(x_in, 16 * TT)
            act.wait_ge(consts, NCONST)
            for t in range(TT):
                if t:
                    act.wait_ge(x_sq, t)
                act.activation(mg[0:WIDTH[t], :], x[0:WIDTH[t], t, :], ACT.Square, accum_out=ss[0:WIDTH[t], t:t + 1]).then_inc(x_sq, 1)
            act.wait_ge(x_sq, TT)
            act.activation(sd[:, 0:TT], ss[:, 0:TT], ACT.Sqrt, bias=eps[:, :], scale=1.0 / D).then_inc(x_sd, 1)
            act.dma_start(vecs[:, 0:D], a["b_s"].rearrange("o h t -> o (h t)").to_broadcast([P, D])).then_inc(bc_in, 16)
            act.dma_start(bvb, a["b_in"][:, 3 * D:4 * D].to_broadcast([P, D])).then_inc(bc_in, 16)
            act.dma_start(vgb, a["v_ln_g"].to_broadcast([P, D])).then_inc(bc_in, 16)
            act.dma_start(vbb, a["v_ln_b"].to_broadcast([P, D])).then_inc(bc_in, 16)
            act.dma_start(wr[:, :, 0:NG], a["w_rg"][0].rearrange("(k p) n -> p k n", p=P)).then_inc(rt_in, 16)
            act.dma_start(wr[:, :, NG:NLOG], a["w_re"][0].rearrange("(k p) n -> p k n", p=P)).then_inc(rt_in, 16)
            act.dma_start(brb[:, 0:NG], a["b_rg"].to_broadcast([P, NG])).then_inc(rt_in, 16)
            act.dma_start(brb[:, NG:NLOG], a["b_re"].to_broadcast([P, NE])).then_inc(rt_in, 16)
            def high2(i, n, b):
                act.wait_ge(w_full[b], cnt(i, n, 16, 32 - 16 * b))
                for m in range(2):
                    act.activation(wH2[b][:, m], WP[b][:, m], ACT.Copy).then_inc(gw_high, 1)

            high2(None, 0, 0)
            act.wait_ge(ws_ps, 1)
            act.activation(wsT[:, :, :].rearrange("p h t -> p (h t)"), PS[:, 6:8, :].rearrange("p b c -> p (b c)"), ACT.Copy).then_inc(ws_copied, 1)
            act.sem_inc(act_drained, Q_A)
            act.wait_ge(s1_ready, 1)
            for j in range(1, KT, 2):
                for s, (c0, c1) in enumerate(((0, NPROMPT), (NPROMPT, T))):
                    act.activation(hT[:, j, c0:c1], hT[:, j, c0:c1], ACT.Identity, scale=S1[:, s, j:j + 1],
                                   bias=VT[:, COL_MOD + 2 * j + s:COL_MOD + 2 * j + s + 1]).then_inc(h_odd, 1)
                act.wait_ge(h_odd, j + 1)
                act.activation(gH[:, j, :], hT[:, j, :], ACT.Copy).then_inc(g_high, 1)

            def two(ap):
                return ap.rearrange("p (h t) -> p h t", h=2)

            def glu(i, n, b):
                act.wait_ge(w_used, cnt(i, n, 1, U_A + 1))
                act.wait_ge(aF_written, cnt(i, n, 2, 2))
                act.activation(two(tmp[:, b, 0:T]), PS[:, 4 * b:4 * b + 2, 0:H], ACT.Identity, bias=VT[:, col(i, COL_BIN + n)])
                act.activation(two(tmp[:, 2 + b, 0:T]), PS[:, 4 * b + 2:4 * b + 4, 0:H], ACT.Sigmoid,
                               bias=VT[:, col(i, COL_BIN + KT + n)]).then_inc(act_drained, 1)

            with act.Fori(0, 6 // 2) as half:
                i = half * 2
                for b in range(2):
                    high2(i, b + 1, 1 - b)
                    glu(i, b, b)
            high2(None, KT - 1, 1)
            glu(None, KT - 2, 0)
            glu(None, KT - 1, 1)

            def store_history(n, dst):
                act.wait_ge(hist_ps, n + 1)
                act.activation(histR[0:HIST, n, :], PS[0:HIST, 6:8, :].rearrange("p b c -> p (b c)"), ACT.Copy).then_inc(hist_copied, 1)
                act.wait_ge(hist_copied, n + 1)
                act.dma_start(dst, histR[0:HIST, n, :]).then_inc(hist_stored, 16)

            store_history(0, hist_p_out)
            def v_part(g):
                t, hf = g // 2, g % 2
                return v[0:WIDTH[t], t, hf * 512:(hf + 1) * 512]

            def gelu_v(g):
                act.wait_ge(v_biased, g + 1)
                act.activation(v_part(g), v_part(g), ACT.Gelu_apprx_tanh).then_inc(v_gelu, 1)

            for g in range(2 * TT):
                if g < 2 * TT - 1:
                    act.wait_ge(v_ps, g + 1)
                else:
                    act.wait_ge(w_used, U_V + 2)
                act.activation(v_part(g), PS[0:WIDTH[g // 2], g % 6, :], ACT.Copy).then_inc(v_copied, 1)
                if g:
                    gelu_v(g - 1)
            gelu_v(2 * TT - 1)
            for n in range(4):
                b = n % 2
                if n == 2:
                    act.wait_ge(v_var, 1)
                    act.activation(vsd[:, 0:4], mv[:, 0:4, 1], ACT.Sqrt, bias=eps[:, :])
                    act.activation(vsd[0:NSAMPLE, 4:5], mv[0:NSAMPLE, 4, 1:2], ACT.Sqrt, bias=eps[0:NSAMPLE, :]).then_inc(v_sd, 1)
                act.wait_ge(w_used, U_U + n + 1)
                for m in range(2):
                    j = 2 * n + m
                    last = act.activation(two(uT[:, j, :]), PS[:, 4 * b + 2 * m:4 * b + 2 * m + 2, 0:H], ACT.Gelu_apprx_tanh,
                                          bias=VT[:, COL_BIN + 2 * KT + j:COL_BIN + 2 * KT + j + 1])
                last.then_inc(act_drained, 1)
            store_history(1, hist_s_out)
            act.wait_ge(hist_ps, 2)
            act.wait_ge(conv_step, TAPS * KT)
            for k in range(KT):
                act.activation(hH[:, k, :], hT[:, k, :], ACT.Copy).then_inc(h_high, 1)

            def high(i, u, b):
                act.wait_ge(w_full[b], cnt(i, u, 16, 16 * (U_YB - b) - 32))
                act.activation(wH[b], WP[b][:, 0], ACT.Copy).then_inc(w_high, 1)

            high(None, 0, 0)
            high(None, 1, 1)
            def gate(i, u, b):
                gate_col = COL_BIN + (5 * KT if u < KT else 3 * KT)
                act.wait_ge(w_used, cnt(i, u, 1, U_YB + 1))
                act.activation(two(tmp[:, b, 0:T]), PS[:, 4 * b:4 * b + 2, 0:H], ACT.Sigmoid,
                               bias=VT[:, col(i, gate_col + u)]).then_inc(act_drained, 1)

            gate(None, 0, 0)
            act.wait_ge(stat_ps, 2)
            act.activation(two(rstdc[:, :]), PS[:, 4:6, 0:CH], ACT.Sqrt, bias=eps[:, :]).then_inc(c_std, 1)
            act.wait_ge(hist_stored, 32)
            high(None, 2, 0)
            for j in range(KT):
                act.wait_ge(c_normed, j + 1)
                for at, n, first in ((0, NPROMPT, 0), (NPROMPT, NSAMPLE, SAMPLE0)):
                    act.activation(aT[:, j, at:at + n], cv[:, j, first:first + n], ACT.Silu,
                                   bias=VT[:, COL_LB + j:COL_LB + j + 1], scale=VT[:, COL_LG + j:COL_LG + j + 1]).then_inc(a_ready, 1)
            gate(None, 1, 1)
            for first, count in ((2, 6), (KT, 6)):
                with act.Fori(0, count // 2) as half:
                    i = half * 2
                    for b in range(2):
                        high(i, first + b + 1, 1 - b)
                        gate(i, first + b, b)
            high(None, NGATE - 1, 1)
            for b in range(2):
                gate(None, NGATE - 2 + b, b)

            def copy_h2(t):
                w = WIDTH[t]
                act.wait_ge(h2_ps, t + 1)
                act.activation(h2T[:, :, t * P:t * P + w],
                               PS[:, H2_BANK[t]:H2_BANK[t] + 2, :].rearrange("p b (j c) -> p (b j) c", c=P)[:, :, 0:w],
                               ACT.Copy).then_inc(h2_copied, 1)

            def deviation(t, done, summed, signal, scratch):
                w = WIDTH[t]
                act.wait_ge(summed, t + 1)
                act.activation(scratch[0:w, :], x[0:w, t, :], ACT.Square, accum_out=ss[0:w, t:t + 1]).then_inc(act_step, 1)
                act.wait_ge(act_step, done + t + 1)
                act.activation(sd[0:w, t:t + 1], ss[0:w, t:t + 1], ACT.Sqrt, bias=eps[0:w, :], scale=1.0 / D).then_inc(signal, 1)

            for t in range(TT):
                deviation(t, 0, x1_ready, x1_sd, sqj)
                if t:
                    copy_h2(t - 1)
                act.wait_ge(h2_ready, t + 1)
                act.dma_start(h2d[t * P:t * P + WIDTH[t], :], h2[0:WIDTH[t], t % 2, :]).then_inc(h2_stored[t % 2], 16)
            copy_h2(TT - 1)
            act.wait_ge(log_ready, 1)
            act.activation(exps, diffs, ACT.Exp).then_inc(e_ready, 1)
            def take_rows(i, t, b):
                act.wait_ge(t_ps, cnt(i, t))
                act.activation(hG[:, b, 0:512], PS[:, 0, :], ACT.Copy).then_inc(hg_ready, 1)

            def swish_gate(i, t):
                act.wait_ge(gu_done, cnt(i, t))
                act.activation(sil, PS[:, 2, 0:DE], ACT.Silu).then_inc(sil_ready, 1)

            def weigh(i, t, b):
                act.wait_ge(down_done, cnt(i, t))
                if t >= 3:
                    act.wait_ge(scattered[b], cnt(i, t, 8, -8 * (1 + b)))
                act.activation(Y[:, b, 0:512], PS[:, 4 + 2 * b, :], ACT.Copy, scale=wslot[:, col(i, t - 1)]).then_inc(y_act, 1)

            def expert_tile(i, t, b):
                swish_gate(i, t)
                take_rows(i, t + 1, 1 - b)
                weigh(i, t - 1, 1 - b)

            def expert_tiles(first, last, peeled):
                take_rows(None, first, slot(first))
                swish_gate(None, first)
                take_rows(None, first + 1, slot(first + 1))
                tiles(act, first + 1, last - 1, expert_tile, peeled)
                swish_gate(None, last)
                weigh(None, last - 1, slot(last - 1))
                weigh(None, last, slot(last))

            act.wait_ge(routed, 1)
            expert_tiles(1, ALWAYS, 2)
            with some_overflow(act):
                expert_tiles(ALWAYS + 1, TILES, 0)
            for t in range(TT):
                deviation(t, TT, f_sum, f_sd, sqj)

        @block.vector
        def _(dve):
            steps_done = [0]

            def then(ins):
                steps_done[0] += 1
                ins.then_inc(dve_step, 1)
                dve.wait_ge(dve_step, steps_done[0])

            def soon(ins):
                steps_done[0] += 1
                ins.then_inc(dve_step, 1)

            def rows_of(banks, w):
                return banks.rearrange("p b (j c) -> p (b j) c", c=P)[:, :, 0:w]

            def two(ap):
                return ap.rearrange("p (h t) -> p h t", h=2)

            dve.wait_ge(consts, NCONST)
            then(dve.tensor_copy(iota[:, :], iotaI[:, :]))
            then(dve.tensor_copy(tokid[:, :], tokidI[:, :]))
            then(dve.tensor_copy(beforeB[:, :], before))
            dve.wait_ge(start_ps, 1)
            dve.tensor_copy(cT.rearrange("p s k -> p (s k)"), PS[:, 0, 0:16]).then_inc(start_dr, 1)
            dve.wait_ge(x_sd, 1)
            then(dve.reciprocal(rs[:, 0:TT], sd[:, 0:TT]))

            def normalise_x(t):
                w = WIDTH[t]
                if t >= 2:
                    dve.wait_ge(xt_ps, t - 1)
                dve.tensor_scalar(xn[0:w, t % 2, :], x[0:w, t, :], rs[0:w, t:t + 1], None, ALU.mult).then_inc(xn_ready, 1)

            def copy_x(t):
                w = WIDTH[t]
                bank = 6 if t % 2 == 0 else 2
                dve.wait_ge(xt_ps, t + 1)
                dve.tensor_copy(hT[:, :, t * P:t * P + w], rows_of(PS[:, bank:bank + 2, :], w)).then_inc(xt_copied, 1)

            def add_ada1(n):
                cols = slice(n * BLK, (n + 1) * BLK)
                dve.wait_ge(w_used, n + 1)
                dve.tensor_tensor(mod1[0:2, cols], PS[0:2, ADA1_BANK[n], :], mod1[0:2, cols], ALU.add).then_inc(ada1_ready, 1)

            normalise_x(0)
            normalise_x(1)
            dve.wait_ge(ada1_bias_in, 16)
            add_ada1(0)
            copy_x(0)
            normalise_x(2)
            copy_x(1)
            normalise_x(3)
            add_ada1(1)
            copy_x(2)
            normalise_x(4)
            copy_x(3)
            add_ada1(2)
            copy_x(4)
            add_ada1(3)
            dve.wait_ge(start_ps, 2)
            dve.tensor_copy(VT[:, 0:328], PS[:, 0, 0:328]).then_inc(start_dr, 1)
            dve.wait_ge(start_ps, 3)
            dve.tensor_copy(aF[:, :, HIST + NPROMPT:2 * HIST + NPROMPT],
                            PS[:, 2, 0:KT * HIST].rearrange("p (j c) -> p j c", c=HIST)).then_inc(start_dr, 1)
            dve.wait_ge(mod1_ps, 1)
            then(dve.tensor_copy(VT[:, COL_MOD:COL_MOD + 32], PS[:, 3, 0:32]))
            for s in range(2):
                ins = dve.scalar_tensor_tensor(out=S1[:, s, :], in0=VT[:, COL_MOD + 2 * KT + s:COL_MOD + 4 * KT:2], scalar=1.0,
                                               in1=VT[:, COL_G1:COL_G1 + KT], op0=ALU.add, op1=ALU.mult)
                if s == 0:
                    then(ins)
            ins.then_inc(s1_ready, 1)
            dve.wait_ge(s1_ready, 1)
            dve.wait_ge(xt_copied, TT)
            for j in range(0, KT, 2):
                for s, (c0, c1) in enumerate(((0, NPROMPT), (NPROMPT, T))):
                    dve.tensor_scalar(hT[:, j, c0:c1], hT[:, j, c0:c1], S1[:, s, j:j + 1],
                                      VT[:, COL_MOD + 2 * j + s:COL_MOD + 2 * j + s + 1], ALU.mult, ALU.add).then_inc(h_even, 1)
                dve.wait_ge(h_even, j + 2)
                then(dve.tensor_copy(gH[:, j, :], hT[:, j, :]))
                dve.tensor_tensor(gL[:, j, :], hT[:, j, :], gH[:, j, :], ALU.subtract).then_inc(g_split[0], 1)

            def tile_of(buf, j, c0, n):
                return buf[:, ds(j, 1), c0:c0 + n].rearrange("p o t -> p (o t)")

            with dve.Fori(0, KT // 2) as half:
                i = half * 2
                dve.wait_ge(aF_written, i * 2 + 8)
                for k in range(TAPS):
                    for b in range(2):
                        total, src = tile_of(cv, i + b, 0, CONV), tile_of(aF, i + b, k, CONV)
                        tap = VT[:, ds(i + (k * KT + b), 1)]
                        if k == 0:
                            dve.tensor_scalar(total, src, tap, VT[:, ds(i + (COL_CB + b), 1)], ALU.mult, ALU.add).then_inc(conv_step, 1)
                        else:
                            dve.wait_ge(conv_step, i * TAPS + (2 * (k - 1) + b + 1))
                            dve.scalar_tensor_tensor(out=total, in0=src, scalar=tap, in1=total, op0=ALU.mult, op1=ALU.add).then_inc(conv_step, 1)

            dve.wait_ge(bc_in, 64)
            for t in range(TT):
                w = WIDTH[t]
                dve.wait_ge(v_gelu, 2 * t + 2)
                for hf in range(2):
                    then(dve.bn_stats(bn[0:w, hf, :], v[0:w, t, hf * 512:(hf + 1) * 512]))
                last = dve.bn_aggr(mv[0:w, t, :], bn[0:w, :, :].rearrange("p a b -> p (a b)"))
                if t < TT - 1:
                    then(last)
            last.then_inc(v_var, 1)
            dve.wait_ge(v_sd, 1)
            then(dve.reciprocal(vsd[:, 0:TT], vsd[:, 0:TT]))
            for t in (3, 4, 0, 1, 2):
                w = WIDTH[t]
                vt = v[0:w, t, :]
                ins = dve.tensor_scalar(vt, vt, mv[0:w, t, 0:1], vsd[0:w, t:t + 1], ALU.subtract, ALU.mult)
                if t >= 3:
                    ins.then_inc(v_scaled, 1)
                    continue
                then(ins)
                then(dve.tensor_tensor(vt, vt, vgb[0:w, :], ALU.mult))
                dve.tensor_tensor(vt, vt, vbb[0:w, :], ALU.add).then_inc(v_norm, 1)
            dve.wait_ge(act_drained, Q_U + 4)
            for h in range(KT):
                b = h % 2
                dve.wait_ge(mix_ps, h + 1)
                if h >= 2:
                    dve.wait_ge(gated, h - 1)
                dve.tensor_tensor(tmp[:, b, 0:NPROMPT].rearrange("p (c t) -> p c t", t=P),
                                  PS[:, 2 * b, :].rearrange("p (c t) -> p c t", t=P),
                                  bsb[:, h:h + 1, :].to_broadcast([P, 4, P]), ALU.add).then_inc(mix_added, 1)
                dve.tensor_tensor(tmp[:, b, NPROMPT:T], PS[:, 2 * b + 1, 0:NSAMPLE], bsb[:, h, 0:NSAMPLE], ALU.add).then_inc(dve_drained, 1)
                dve.wait_ge(mix_added, h + 1)
                dve.wait_ge(dve_drained, h + 1)
                dve.tensor_tensor(uT[:, h, :], uT[:, h, :], tmp[:, b, 0:T], ALU.mult).then_inc(gated, 1)
            dve.wait_ge(stat_ps, 1)
            for j in range(KT):
                dve.tensor_tensor(two(cv[:, j, :]), two(cv[:, j, :]), PS[:, 6:8, 0:CH], ALU.subtract).then_inc(centred, 1)
            dve.wait_ge(centred, KT)
            dve.wait_ge(c_std, 1)
            then(dve.reciprocal(rstdc[:, :], rstdc[:, :]))
            dve.wait_ge(squared, KT)
            for j in range(KT):
                dve.tensor_tensor(cv[:, j, :], cv[:, j, :], rstdc[:, :], ALU.mult).then_inc(c_normed, 1)

            def merge(i, u, b):
                m_j = mT[:, col(i, u % KT), :].rearrange("p o (h t) -> p (o h) t", h=2)
                dve.wait_ge(act_drained, cnt(i, u, 1, Q_YB + 1))
                y, gate = PS[:, 4 * b + 2:4 * b + 4, 0:H], two(tmp[:, b, 0:T])
                if u < KT:
                    dve.tensor_tensor(m_j, y, gate, ALU.mult).then_inc(dve_drained, 1)
                else:
                    dve.tensor_tensor(two(tmp[:, 2 + b, 0:T]), y, gate, ALU.mult).then_inc(dve_drained, 1)
                    dve.wait_ge(dve_drained, cnt(i, u, 1, KT + 1))
                    dve.tensor_tensor(m_j, m_j, two(tmp[:, 2 + b, 0:T]), ALU.add).then_inc(merged, 2)

            def mod_block(i, u, b):
                m = u - LAG
                for k in range(KT):
                    if k % 2 == 0:
                        dve.wait_ge(mod_in[k // 2], cnt(i, m, 16, 16))
                    for s in range(2):
                        w, c, total = WC[k // 2][:, k % 2, :], cT[:, s, k:k + 1], mod_sum[:, b, s, :]
                        if k == 0:
                            dve.tensor_scalar(total, w, c, None, ALU.mult).then_inc(mod_step, 1)
                        else:
                            dve.wait_ge(mod_step, cnt(i, m, 16, 2 * (k - 1) + s + 1))
                            dve.scalar_tensor_tensor(out=total, in0=w, scalar=c, in1=total, op0=ALU.mult, op1=ALU.add).then_inc(mod_step, 1)

            def add_bias(i, u, b):
                m = u - LAG
                dve.wait_ge(bias_in[b], cnt(i, m, 8, 16 - 8 * b))
                if m >= 2:
                    dve.wait_ge(mod_stored[b], cnt(i, m, 8, -8 * b))
                dve.tensor_tensor(mrow[:, b, :].rearrange("p (q n) -> p q n", n=P), PS[0:2, 4 * b:4 * b + 4, 512 - P:512],
                                  brow[:, b, :].rearrange("p (q n) -> p q n", n=P), ALU.add).then_inc(mod_added, 1)

            dve.wait_ge(stat_ps, 2)
            merge(None, 0, 0)
            merge(None, 1, 1)
            for u in range(2, LAG + 2):
                if u >= LAG:
                    mod_block(None, u, u % 2)
                merge(None, u, u % 2)
                if u >= LAG:
                    add_bias(None, u, u % 2)
            for first, count in ((LAG + 2, 2), (KT, 8)):
                with dve.Fori(0, count // 2) as half:
                    i = half * 2
                    for b in range(2):
                        mod_block(i, first + b, b)
                        merge(i, first + b, b)
                        add_bias(i, first + b, b)
            dve.wait_ge(mb_in, 64)
            dve.wait_ge(mb2_in, 48)
            for s, rows in ((0, P), (1, NSAMPLE)):
                then(dve.scalar_tensor_tensor(out=a2b[s][0:rows, :], in0=a2b[s][0:rows, :], scalar=1.0, in1=gn2b[0:rows, :],
                                              op0=ALU.add, op1=ALU.mult))
            for t in range(TT):
                w, s = WIDTH[t], t // 4
                for hf in range(2):
                    if t < 4 or hf == 0:
                        dve.wait_ge(o_ps, 2 * t + hf + 1)
                    else:
                        dve.wait_ge(w_used, U_O + 2)
                    cols = slice(hf * 512, (hf + 1) * 512)
                    dve.tensor_tensor(mg[0:w, cols], PS[0:w, (2 * t + hf) % 8, :], g1b[s][0:w, cols], ALU.mult).then_inc(o_drained, 1)
                dve.wait_ge(o_drained, 2 * t + 2)
                dve.tensor_tensor(x[0:w, t, :], x[0:w, t, :], mg[0:w, :], ALU.add).then_inc(x1_ready, 1)
                dve.wait_ge(x1_ready, t + 1)
                dve.wait_ge(x1_sd, t + 1)
                then(dve.reciprocal(rs[0:w, t:t + 1], sd[0:w, t:t + 1]))
                if t >= 2:
                    dve.wait_ge(h2_ps, t - 1)
                    dve.wait_ge(h2_stored[t % 2], 16 * (t // 2))
                then(dve.scalar_tensor_tensor(out=h2[0:w, t % 2, :], in0=x[0:w, t, :], scalar=rs[0:w, t:t + 1], in1=a2b[s][0:w, :],
                                              op0=ALU.mult, op1=ALU.mult))
                dve.tensor_tensor(h2[0:w, t % 2, :], h2[0:w, t % 2, :], sh2b[s][0:w, :], ALU.add).then_inc(h2_ready, 1)

            def wide(ap, *shape):
                return ap.to_broadcast(list(shape))

            def first_one(out, logits, n, best):
                then(dve.tensor_reduce(best, logits, AX, ALU.max))
                then(dve.tensor_tensor(scr[:, :, 0:n], logits, wide(best.unsqueeze(2), P, TT, n), ALU.is_equal))
                then(dve.tensor_tensor(scr[:, :, 0:n], scr[:, :, 0:n], wide(rev[:, 0:1, EPG - n:EPG], P, TT, n), ALU.mult))
                then(dve.tensor_reduce(mx[:, 3, :], scr[:, :, 0:n], AX, ALU.max))
                then(dve.tensor_tensor(out, scr[:, :, 0:n], wide(mx[:, 3, :].unsqueeze(2), P, TT, n), ALU.is_equal))

            soon(dve.tensor_scalar(rev[:, 0, :], iota[:, 0:EPG], -1.0, float(EPG), ALU.mult, ALU.add))
            for k in range(2):
                soon(dve.tensor_copy(vals[:, 0, k, :], tokid[:, :]))
                soon(dve.tensor_scalar(vals[:, 1, k, :], tokid[:, :], 1.0, float(k * T + 1), ALU.mult, ALU.add))
                soon(dve.tensor_scalar(outside[:, k, :], valid[:, :], -float(TILES), float(TILES), ALU.mult, ALU.add))
            soon(dve.memset(cum, 0.0))
            then(dve.memset(lg, 0.0))
            dve.wait_ge(log_ps, 1)
            soon(dve.tensor_tensor(lg[:, 0:4, :], PS[:, 4, 0:4 * NLOG].rearrange("p (t n) -> p t n", n=NLOG),
                                   wide(brb[:, :].unsqueeze(1), P, 4, NLOG), ALU.add))
            then(dve.tensor_tensor(lg[0:NSAMPLE, 4, :], PS[0:NSAMPLE, 4, 4 * NLOG:5 * NLOG], brb[0:NSAMPLE, :], ALU.add))
            groups = lg[:, :, 0:NG]
            first_one(one_g, groups, NG, mx[:, 0, :])
            soon(dve.tensor_tensor(diffs[:, :, 0:NG], groups, wide(mx[:, 0, :].unsqueeze(2), P, TT, NG), ALU.subtract))
            picked = prod.rearrange("p (g t) e -> p g t e", g=2)
            for g in range(NG):
                one = wide(one_g[:, :, g:g + 1], P, TT, EPG)
                (then if g == NG - 1 else soon)(
                    dve.tensor_tensor(picked[:, 0, :, g * EPG:(g + 1) * EPG], lg[:, :, NG + g * EPG:NG + (g + 1) * EPG], one, ALU.mult))
            then(dve.tensor_tensor(picked[:, 1, :, 0:2 * EPG], picked[:, 0, :, 0:2 * EPG], picked[:, 0, :, 2 * EPG:NE], ALU.add))
            then(dve.tensor_tensor(lsel[:, 0], picked[:, 1, :, 0:EPG], picked[:, 1, :, EPG:2 * EPG], ALU.add))
            first_one(one_e[:, 0], lsel[:, 0], EPG, mx[:, 1, :])
            then(dve.scalar_tensor_tensor(out=lsel[:, 1], in0=one_e[:, 0], scalar=-3.0e38, in1=lsel[:, 0], op0=ALU.mult, op1=ALU.add))
            first_one(one_e[:, 1], lsel[:, 1], EPG, mx[:, 2, :])
            dve.tensor_tensor(diffs[:, :, NG], mx[:, 2, :], mx[:, 1, :], ALU.subtract).then_inc(log_ready, 1)
            then(dve.tensor_tensor(one_g, one_g, wide(valid[:, :].unsqueeze(2), P, TT, NG), ALU.mult))
            for g in range(NG):
                for k in range(2):
                    ins = dve.tensor_tensor(OH[:, k, :, g * EPG:(g + 1) * EPG], one_e[:, k], wide(one_g[:, :, g:g + 1], P, TT, EPG), ALU.mult)
                    (then if (g, k) == (NG - 1, 1) else soon)(ins)
            dve.tensor_tensor(OHs[:, :, :], OH[:, 0], OH[:, 1], ALU.add).then_inc(oh_ready, 1)
            pair_oh = OH.rearrange("p k t e -> p (k t) e")
            flat = {n: ap.rearrange("p a b -> p (a b)") for n, ap in
                    (("rank", rank), ("ovs", ovs), ("eid", eid), ("q", q), ("tile", tile), ("off", off), ("outside", outside))}

            def dot(out, with_e):
                then(dve.tensor_tensor(prod, pair_oh, wide(with_e.unsqueeze(1), P, 2 * TT, NE), ALU.mult))
                then(dve.tensor_reduce(out, prod, AX, ALU.add))

            dot(flat["eid"], iota[:, 0:NE])
            dve.wait_ge(e_ready, 1)
            then(dve.tensor_reduce(mx[:, 0, :], exps[:, :, 0:NG], AX, ALU.add))
            then(dve.scalar_tensor_tensor(out=mx[:, 0, :], in0=exps[:, :, NG], scalar=1.0, in1=mx[:, 0, :], op0=ALU.add, op1=ALU.mult))
            then(dve.reciprocal(vals[:, 2, 0, :], mx[:, 0, :]))
            soon(dve.tensor_tensor(vals[:, 2, 1, :], vals[:, 2, 0, :], exps[:, :, NG], ALU.mult))
            dve.wait_ge(rank_ps, 1)
            earlier = PS[:, 1, 0:TT * NE].rearrange("p (t e) -> p t e", e=NE)
            for k in range(2):
                soon(dve.tensor_tensor(prod[:, k * TT:(k + 1) * TT, :], OH[:, k], earlier, ALU.mult))
            then(dve.tensor_tensor(cmp, wide(PS[:, 1, TT * NE:(TT + 1) * NE].unsqueeze(2), P, NE, STEPS),
                                   wide(steps[:, :].unsqueeze(1), P, NE, STEPS), ALU.is_gt))
            soon(dve.tensor_reduce(cum[:, 0, NE:2 * NE], cmp, AX, ALU.add))
            then(dve.tensor_reduce(flat["rank"], prod, AX, ALU.add))
            at, step = 0, 1
            while step < NE:
                then(dve.tensor_tensor(cum[:, 1 - at, NE:2 * NE], cum[:, at, NE:2 * NE], cum[:, at, NE - step:2 * NE - step], ALU.add))
                at, step = 1 - at, 2 * step
            upto, before_it = cum[:, at, NE:2 * NE], cum[:, at, NE - 1:2 * NE - 1]
            dot(flat["ovs"], before_it)
            then(dve.tensor_tensor(q8, wide(flat["rank"].unsqueeze(2), P, 2 * TT, STEPS), wide(steps[:, :].unsqueeze(1), P, 2 * TT, STEPS), ALU.is_ge))
            then(dve.tensor_reduce(flat["q"], q8, AX, ALU.add))
            soon(dve.scalar_tensor_tensor(out=flat["off"], in0=flat["q"], scalar=-float(SLOTS), in1=flat["rank"], op0=ALU.mult, op1=ALU.add))
            then(dve.tensor_tensor(flat["ovs"], flat["ovs"], flat["q"], ALU.add))
            soon(dve.scalar_tensor_tensor(out=flat["ovs"], in0=flat["ovs"], scalar=float(NE - 1), in1=flat["eid"], op0=ALU.add, op1=ALU.subtract))
            then(dve.tensor_scalar(flat["q"], flat["q"], 1.0, None, ALU.min))
            soon(dve.tensor_tensor(flat["eid"], flat["eid"], flat["outside"], ALU.add))
            then(dve.tensor_tensor(flat["ovs"], flat["ovs"], flat["q"], ALU.mult))
            then(dve.tensor_tensor(flat["tile"], flat["eid"], flat["ovs"], ALU.add))
            soon(dve.tensor_tensor(FOH, wide(flat["off"].unsqueeze(2), P, 2 * TT, SLOTS), wide(iota[:, 0:SLOTS].unsqueeze(1), P, 2 * TT, SLOTS), ALU.is_equal))
            then(dve.tensor_tensor(TOH, wide(flat["tile"].unsqueeze(2), P, 2 * TT, TILES), wide(iota[:, 0:TILES].unsqueeze(1), P, 2 * TT, TILES), ALU.is_equal))
            for n in range(3):
                what = vals[:, n].rearrange("p k t -> p (k t)")
                last = dve.tensor_tensor(R[:, :, n * TILES:(n + 1) * TILES], TOH, wide(what.unsqueeze(2), P, 2 * TT, TILES), ALU.mult)
                if n < 2:
                    soon(last)
            last.then_inc(tab_ready, 1)
            then(dve.tensor_tensor(ocmp, wide(upto.unsqueeze(1), P, OVER, NE), wide(iota[:, 0:OVER].unsqueeze(2), P, OVER, NE), ALU.is_le))
            then(dve.tensor_reduce(oex, ocmp, AX, ALU.add))
            soon(dve.tensor_scalar(over_expert[0:1, 0:OVER], oex[0:1, :], float(NE - 1), None, ALU.min))
            then(dve.tensor_copy(over_expert[0:1, OVER:OVER + 1], upto[0:1, NE - 1:NE]))
            dve.wait_ge(tab_ps, 1)
            soon(dve.tensor_copy(tokI[:, :], PS[0:SLOTS, 2, 0:TILES]))
            then(dve.tensor_scalar(un[0:SLOTS, :], PS[0:SLOTS, 2, TILES:2 * TILES], 0.0, 4096.0, ALU.is_equal, ALU.mult))
            soon(dve.tensor_copy(wslot[:, :], PS[0:SLOTS, 2, 2 * TILES:3 * TILES]))
            dve.scalar_tensor_tensor(out=pairI[:, :], in0=PS[0:SLOTS, 2, TILES:2 * TILES], scalar=-1.0, in1=un[0:SLOTS, :],
                                     op0=ALU.add, op1=ALU.add).then_inc(routed, 1)
            dve.wait_ge(routed, 1)
            dve.wait_ge(dve_step, steps_done[0])

            def take_rows(i, t, b):
                dve.wait_ge(t_ps, cnt(i, t))
                dve.tensor_copy(hG[:, b, 512:1024], PS[:, 1, :]).then_inc(hg_ready, 1)

            def gate_hidden(i, t):
                dve.wait_ge(sil_ready, cnt(i, t))
                dve.tensor_tensor(he, PS[:, 2, DE:2 * DE], sil, ALU.mult).then_inc(he_ready, 1)

            def take_hidden(i, t):
                dve.wait_ge(he_ps, cnt(i, t))
                dve.tensor_copy(heT.rearrange("p k s -> p (k s)"), PS[:, 3, 0:2 * SLOTS]).then_inc(het_ready, 1)

            def weigh(i, t, b):
                dve.wait_ge(down_done, cnt(i, t))
                if t >= 3:
                    dve.wait_ge(scattered[b], cnt(i, t, 8, -8 * (1 + b)))
                dve.tensor_scalar(Y[:, b, 512:1024], PS[:, 5 + 2 * b, :], wslot[:, col(i, t - 1)], None, ALU.mult).then_inc(y_dve, 1)

            def expert_tile(i, t, b):
                gate_hidden(i, t)
                take_rows(i, t + 1, 1 - b)
                weigh(i, t - 1, 1 - b)
                take_hidden(i, t)

            def expert_tiles(first, last, peeled):
                take_rows(None, first, slot(first))
                gate_hidden(None, first)
                take_rows(None, first + 1, slot(first + 1))
                take_hidden(None, first)
                tiles(dve, first + 1, last - 1, expert_tile, peeled)
                gate_hidden(None, last)
                weigh(None, last - 1, slot(last - 1))
                take_hidden(None, last)
                weigh(None, last, slot(last))

            expert_tiles(1, ALWAYS, 2)
            with some_overflow(dve):
                expert_tiles(ALWAYS + 1, TILES, 0)

            dve.wait_ge(fin_in, 16 * 7)
            for s, rows in ((0, P), (1, NSAMPLE)):
                then(dve.scalar_tensor_tensor(out=afb[s][0:rows, :], in0=afb[s][0:rows, :], scalar=1.0, in1=gfb[0:rows, :],
                                              op0=ALU.add, op1=ALU.mult))

            def finish(t):
                w, s = WIDTH[t], t // 4
                o = pair_rows[0][0:w, t, :]
                dve.wait_ge(f_sd, t + 1)
                then(dve.reciprocal(rs[0:w, t:t + 1], sd[0:w, t:t + 1]))
                dve.scalar_tensor_tensor(out=o, in0=x[0:w, t, :], scalar=rs[0:w, t:t + 1], in1=afb[s][0:w, :],
                                         op0=ALU.mult, op1=ALU.mult).then_inc(f_scaled, 1)

            for t in range(TT):
                w, s = WIDTH[t], t // 4
                o = pair_rows[0][0:w, t, :]
                dve.wait_ge(pair_in[t], 32)
                then(dve.tensor_tensor(o, o, pair_rows[1][0:w, t, :], ALU.add))
                then(dve.tensor_tensor(o, o, g2b[s][0:w, :], ALU.mult))
                dve.tensor_tensor(x[0:w, t, :], x[0:w, t, :], o, ALU.add).then_inc(f_sum, 1)
                if t:
                    finish(t - 1)
            finish(TT - 1)

        @block.gpsimd
        def _(pool):
            pool.memset(pick[:, :, :], 0.0).then_inc(consts, 1)
            pool.memset(ident[:, :], 0.0).then_inc(consts, 1)
            pool.memset(before, 1.0).then_inc(consts, 1)
            pool.memset(valid[:, :], 1.0).then_inc(consts, 1)
            pool.wait_ge(consts, 4)
            pool.memset(pick.rearrange("p s r -> p (s r)")[:, 0::3], 1.0).then_inc(consts, 1)
            pool.affine_select(out=ident[:, :], in_=ident[:, :], compare_op=ALU.not_equal, fill=1.0, base=0,
                               pattern=[[-1, P]], channel_multiplier=1).then_inc(consts, 1)
            pool.affine_select(out=before, in_=before, compare_op=ALU.is_gt, fill=0.0, base=0,
                               pattern=[[1, P]], channel_multiplier=-1).then_inc(consts, 1)
            pool.affine_select(out=valid[:, :], in_=valid[:, :], compare_op=ALU.is_gt, fill=0.0, base=T,
                               pattern=[[-P, TT]], channel_multiplier=-1).then_inc(consts, 1)
            pool.iota(iotaI[:, :], pattern=[[1, SLOTS]], base=0, channel_multiplier=0).then_inc(consts, 1)
            pool.iota(tokidI[:, :], pattern=[[P, TT]], base=0, channel_multiplier=1).then_inc(consts, 1)
            pool.memset(meanm[:, :], 1.0 / D).then_inc(consts, 1)
            pool.memset(onesB[:, :], 1.0).then_inc(consts, 1)
            pool.memset(eps[:, :], EPS).then_inc(consts, 1)
            pool.memset(ss[:, :], 1.0).then_inc(consts, 1)
            pool.memset(vsd[:, :], 1.0).then_inc(consts, 1)
            for m in range(STEPS):
                pool.memset(steps[:, m:m + 1], float(SLOTS * (m + 1))).then_inc(consts, 1)
            pool.memset(aF[:, :, 0:HIST], 0.0).then_inc(aF_written, 4)
            pool.wait_ge(ws_in, 16)
            for h in range(KT):
                pool.affine_select(out=wsR[:, h, :], in_=wsR[:, h, :], compare_op=ALU.is_ge, fill=0.0, base=0,
                                   pattern=[[-1, P]], channel_multiplier=1).then_inc(ws_masked, 1)

            def low2(i, n, b, parts=(0, 1)):
                for m in parts:
                    pool.wait_ge(gw_high, cnt(i, n, 2, m + 1))
                    pool.tensor_tensor(wL2[b][:, m], WP[b][:, m], wH2[b][:, m], ALU.subtract).then_inc(gw_split, 1)

            def glu(i, n, b):
                pool.wait_ge(act_drained, cnt(i, n, 1, Q_A + 1))
                for at, w, first in ((HIST, NPROMPT, 0), (2 * HIST + NPROMPT, NSAMPLE, NPROMPT)):
                    pool.tensor_tensor(aF[:, col(i, n), at:at + w].rearrange("p o t -> p (o t)"), tmp[:, b, first:first + w],
                                       tmp[:, 2 + b, first:first + w], ALU.mult).then_inc(aF_written, 1)

            low2(None, 0, 0, (0,))
            for j in range(1, KT, 2):
                if j == 5:
                    low2(None, 0, 0, (1,))
                pool.wait_ge(g_high, j // 2 + 1)
                pool.tensor_tensor(gL[:, j, :], hT[:, j, :], gH[:, j, :], ALU.subtract).then_inc(g_split[1], 1)
            with pool.Fori(0, 6 // 2) as half:
                i = half * 2
                for b in range(2):
                    low2(i, b + 1, 1 - b)
                    glu(i, b, b)
            low2(None, KT - 1, 1)
            glu(None, KT - 2, 0)
            glu(None, KT - 1, 1)
            pool.wait_ge(bc_in, 64)
            for t in range(TT):
                for hf in range(2):
                    vh, cols = v[0:WIDTH[t], t, hf * 512:(hf + 1) * 512], slice(hf * 512, (hf + 1) * 512)
                    pool.wait_ge(v_copied, 2 * t + hf + 1)
                    pool.tensor_tensor(vh, vh, bvb[0:WIDTH[t], cols], ALU.add).then_inc(v_biased, 1)
            for t in (3, 4):
                vt = v[0:WIDTH[t], t, :]
                pool.wait_ge(v_scaled, t - 2)
                pool.tensor_tensor(vt, vt, vgb[0:WIDTH[t], :], ALU.mult).then_inc(v_gained, 1)
                pool.wait_ge(v_gained, t - 2)
                pool.tensor_tensor(vt, vt, vbb[0:WIDTH[t], :], ALU.add).then_inc(v_norm, 1)
            pool.wait_ge(v_norm, TT)
            pool.dma_start(v_out, v[0:NSAMPLE, 4, :]).then_inc(v_stored, 16)
            pool.wait_ge(w_used, U_U + 4)
            for k in range(KT):
                pool.wait_ge(h_high, k + 1)
                pool.tensor_tensor(hL[:, k, :], hT[:, k, :], hH[:, k, :], ALU.subtract).then_inc(h_split, 1)

            def low(i, u, b):
                pool.wait_ge(w_high, cnt(i, u, 1, 1))
                pool.tensor_tensor(wL[b], WP[b][:, 0], wH[b], ALU.subtract).then_inc(w_split, 1)

            low(None, 0, 0)
            low(None, 1, 1)
            pool.wait_ge(v_stored, 16)
            for j in range(KT):
                pool.wait_ge(centred, j + 1)
                pool.tensor_tensor(sq[:, j, :], cv[:, j, :], cv[:, j, :], ALU.mult).then_inc(squared, 1)

            def load_mod(i, m, b, src, bias, c0):
                for c in range(4):
                    if m >= 1:
                        pool.wait_ge(mod_step, cnt(i, m, 16, 4 * (c + 1) - 16))
                        pool.sem_inc(mod_loads_begun)
                    pool.dma_start(WC[c], src[:, 2 * c:2 * c + 2, c0]).then_inc(mod_in[c], 16)
                pool.dma_start(brow[:, b, :], bias[:, c0].to_broadcast([2, BLK])).then_inc(bias_in[b], 16)

            def store_mod(i, m, b, cols):
                pool.wait_ge(mod_added, cnt(i, m, 1, 1))
                pool.sem_inc(mod_loads_begun)
                pool.dma_start(mod[:, cols], mrow[:, b, :]).then_inc(mod_stored[b], 16)

            low(None, 2, 0)
            low(None, 3, 1)
            pool.wait_ge(a_ready, 2 * KT)
            for m in range(2):
                low(None, m + LAG, m)
                load_mod(None, m, m, w_ada, a["b_ada"], slice((4 + m) * BLK, (5 + m) * BLK))
            for first, count, src, bias, col0 in ((2, 6, w_ada, a["b_ada"], 6), (8, 4, w_adaf, b_adaf, 0)):
                with pool.Fori(0, count // 2) as half:
                    i = half * 2
                    for b in range(2):
                        store_mod(i, first - 2 + b, b, ds(i * BLK + (first + 2 + b) * BLK, BLK))
                        low(i, first + LAG + b, b)
                        load_mod(i, first + b, b, src, bias, ds(i * BLK + (col0 + b) * BLK, BLK))
            for b in range(2):
                store_mod(None, NB - 2 + b, b, slice((NB + 2 + b) * BLK, (NB + 3 + b) * BLK))

            pool.wait_ge(routed, 1)
            pool.wait_ge(h2_stored[0], 48)
            pool.wait_ge(h2_stored[1], 32)

            last_token, last_pair = pool.to_reg(T - 1), pool.to_reg(2 * T - 1)

            def gather(i, t, b):
                if t >= 3:
                    pool.wait_ge(t_ps, cnt(i, t, 1, -2))
                pool.tensor_copy(gidx[b][:, :], tokI[:, col(i, t - 1)]).then_inc(g_idx, 1)
                pool.wait_ge(g_idx, cnt(i, t))
                pool.sem_inc(gathers_begun)
                pool.indirect_dma_start(out=G[:, b, :], out_offset=None, in_=h2d,
                                        in_offset=bass.IndirectOffsetOnAxis(ap=gidx[b][:, 0:1], axis=0),
                                        bounds_check=last_token, oob_is_err=True).then_inc(gathered[b], 16)

            def scatter(i, t, b):
                if t >= 3:
                    pool.wait_ge(scattered[b], cnt(i, t, 8, -8 * (1 + b)))
                pool.tensor_copy(sidx[b][:, :], pairI[:, col(i, t - 1)]).then_inc(s_idx, 1)
                pool.wait_ge(s_idx, cnt(i, t))
                pool.wait_ge(y_act, cnt(i, t))
                pool.wait_ge(y_dve, cnt(i, t))
                pool.sem_inc(scatters_begun)
                pool.indirect_dma_start(out=pairs, out_offset=bass.IndirectOffsetOnAxis(ap=sidx[b][:, 0:1], axis=0),
                                        in_=Y[:, b, :], in_offset=None,
                                        bounds_check=last_pair, oob_is_err=False).then_inc(scattered[b], 16)

            def rows_in_and_out(i, t, b):
                gather(i, t + 3, 1 - b)
                scatter(i, t, b)

            def expert_tiles(first, last):
                for t in range(first, first + 3):
                    gather(None, t, slot(t))
                tiles(pool, first, last - 3, rows_in_and_out, 3)
                for t in range(last - 2, last + 1):
                    scatter(None, t, slot(t))
                for b in range(2):
                    pool.wait_ge(scattered[b], 16 * ((last + 1 - b) // 2))

            expert_tiles(1, ALWAYS)
            with some_overflow(pool):
                expert_tiles(ALWAYS + 1, TILES)
            pool.sem_inc(experts_done)
            for t in range(TT):
                w, s = WIDTH[t], t // 4
                o = pair_rows[0][0:w, t, :]
                pool.wait_ge(f_scaled, t + 1)
                pool.tensor_tensor(o, o, shfb[s][0:w, :], ALU.add).then_inc(f_out, 1)


_INS = ["x_prompt", "x_sample", "cache_conv", "c_prompt", "c_sample", "w_ada", "b_ada", "g_norm1", "g_norm2",
        "w_in", "b_in", "conv_w", "conv_b", "ln_g", "ln_b", "w_a", "v_ln_g", "v_ln_b", "w_s", "b_s", "w_b", "w_o",
        "w_rg", "b_rg", "w_re", "b_re", "w_gate", "w_up", "w_down", "g_final", "w_ada_f", "b_ada_f"]


def kernel(**inputs):
    import concourse.bacc as bacc
    from concourse.bass_utils import run_bass_kernel_spmd

    nc = bacc.Bacc("TRN2", target_bir_lowering=False, num_devices=1)
    arrays = {name: np.ascontiguousarray(inputs[name]) for name in _INS}
    aps = {name: nc.dram_tensor(name, arr.shape, mybir.dt.from_np(arr.dtype), kind="ExternalInput").ap()
           for name, arr in arrays.items()}
    outs = [nc.dram_tensor(name, shape, F32, kind="ExternalOutput").ap() for name, shape in
            (("y", (T, D)), ("hist_prompt", (HIST, D)), ("hist_sample", (HIST, D)), ("v_rows", (NSAMPLE, D)))]
    build(nc, aps, *outs)
    r = run_bass_kernel_spmd(nc, [arrays], core_ids=[0]).results[0]
    y = r["y"]
    return (y[:NPROMPT].reshape(1, NPROMPT, D), y[NPROMPT:].reshape(1, NSAMPLE, D),
            r["hist_prompt"].reshape(1, 1, HIST, D), r["hist_sample"].reshape(1, 1, HIST, D),
            r["v_rows"].reshape(1, 1, NSAMPLE, D))
```
